# Optimizing a Trainium2 kernel written in Bass

```python
import jax
import jax.numpy as jnp
from jax import lax
import numpy as np

D_MODEL = 1024
BATCH = 1
SEQ = 128
DEPTH = 2
DEC_BATCH = 1
DEC_SEQ = 256
PAST_LEN = 128

GRID_W = 64
N_MIXERS = 2
N_HGRN_LAYERS = (DEPTH + N_MIXERS - 1) // N_MIXERS
N_FOURIER_LAYERS = DEPTH // N_MIXERS
HGRN_HEADS = 8
HGRN_DK = 128
HGRN_DV = D_MODEL // HGRN_HEADS
HGRN_HK = HGRN_HEADS * HGRN_DK
HGRN_HV = HGRN_HEADS * HGRN_DV
HGRN_IN = 3 * HGRN_HK + 2 * HGRN_HV
CHUNK = 16
FOURIER_GROUPS = 4
FOURIER_CG = D_MODEL // FOURIER_GROUPS
MOE_GROUPS = 4
MOE_EXPERTS_PER_GROUP = 4
MOE_EXPERTS = MOE_GROUPS * MOE_EXPERTS_PER_GROUP
MOE_TOP_K = 2
MOE_D_FF = D_MODEL // 2
NORM_EPS = 1e-6
POS_BASE = 10000.0

kernel_name = 'hybrid_hgrn2_fnet_hmoe_diffusion_step'

def _rmsnorm(x, g):
    xf = x.astype(jnp.float32)
    y = xf * lax.rsqrt(jnp.mean(xf * xf, axis=-1, keepdims=True) + NORM_EPS)
    return (y * g.astype(jnp.float32)).astype(x.dtype)

def _modulate(h, shift, scale):
    return h * (1 + scale[:, None, :]) + shift[:, None, :]

def _grid_pos_embed(n_tokens, dtype):
    rows = n_tokens // GRID_W
    t = jnp.arange(rows * GRID_W)
    r = (t // GRID_W).astype(jnp.float32)
    col = (t % GRID_W).astype(jnp.float32)
    quarter = D_MODEL // 4
    omega = 1.0 / (POS_BASE ** (jnp.arange(quarter, dtype=jnp.float32) / quarter))
    ar = r[:, None] * omega[None, :]
    ac = col[:, None] * omega[None, :]
    return jnp.concatenate([jnp.sin(ar), jnp.cos(ar), jnp.sin(ac), jnp.cos(ac)], axis=-1).astype(dtype)

def _hgrn_lower_bounds(lb_logits):
    p = jax.nn.softmax(lb_logits.astype(jnp.float32), axis=0)
    cs = jnp.cumsum(p, axis=0)
    return cs - cs[0:1]

def _chunk_scan(q, log_f, k, v, s0):
    B, H, L, DK = q.shape
    DV = v.shape[-1]
    N = L // CHUNK
    q, log_f, k = (t.reshape(B, H, N, CHUNK, DK) for t in (q, log_f, k))
    v = v.reshape(B, H, N, CHUNK, DV)
    b = jnp.cumsum(log_f, axis=3)
    b_last = b[:, :, :, -1:, :]
    tri = jnp.tril(jnp.ones((CHUNK, CHUNK), dtype=bool))[:, :, None]
    diff = b[:, :, :, :, None, :] - b[:, :, :, None, :, :]
    decay = jnp.where(tri, jnp.exp(jnp.where(tri, diff, 0.0)), 0.0)
    scores = jnp.einsum('bhntk,bhntsk,bhnsk->bhnts', q, decay, k)
    o_intra = jnp.einsum('bhnts,bhnsv->bhntv', scores, v)
    u = jnp.einsum('bhnsk,bhnsv->bhnkv', k * jnp.exp(b_last - b), v)
    g = jnp.exp(b_last[:, :, :, 0, :])

    def step(s, gu):
        gn, un = gu
        return gn[..., None] * s + un, s

    s_final, s_start = lax.scan(step, s0, (jnp.moveaxis(g, 2, 0), jnp.moveaxis(u, 2, 0)))
    s_start = jnp.moveaxis(s_start, 0, 2)
    o_inter = jnp.einsum('bhntk,bhnkv->bhntv', q * jnp.exp(b), s_start)
    return (o_intra + o_inter).reshape(B, H, L, DV), s_final

def _hgrn_mixer(h, w_in, lb, norm_g, w_out, s0_f, s0_b):
    B, L, _ = h.shape
    proj = jnp.einsum('bld,de->ble', h, w_in).astype(jnp.float32)
    q, zf, zb, v, g = jnp.split(proj, [HGRN_HK, 2 * HGRN_HK, 3 * HGRN_HK, 3 * HGRN_HK + HGRN_HV], axis=-1)

    def heads(t, d):
        return t.reshape(B, L, HGRN_HEADS, d).transpose(0, 2, 1, 3)

    def gates(z, lb_dir):
        log_f = jnp.logaddexp(jnp.log(lb_dir), jnp.log1p(-lb_dir) + jax.nn.log_sigmoid(z))
        log_f = heads(log_f, HGRN_DK)
        return log_f, -jnp.expm1(log_f)

    q = heads(q, HGRN_DK)
    v = heads(v, HGRN_DV)
    lf_f, k_f = gates(zf, lb[0])
    lf_b, k_b = gates(zb, lb[1])
    o_f, s_f = _chunk_scan(q, lf_f, k_f, v, s0_f)
    flip = lambda t: jnp.flip(t, axis=2)
    o_b, s_b = _chunk_scan(flip(q), flip(lf_b), flip(k_b), flip(v), s0_b)
    o = (o_f + flip(o_b)).transpose(0, 2, 1, 3)
    o = o * lax.rsqrt(jnp.mean(o * o, axis=-1, keepdims=True) + NORM_EPS)
    o = o * norm_g.astype(jnp.float32).reshape(HGRN_HEADS, HGRN_DV)
    o = o.reshape(B, L, HGRN_HV) * jax.nn.silu(g)
    out = jnp.einsum('ble,ed->bld', o.astype(h.dtype), w_out)
    return out, s_f, s_b

def _fourier_mixer(h, w_out):
    B, L, _ = h.shape
    hg = h.astype(jnp.float32).reshape(B, L, FOURIER_GROUPS, FOURIER_CG)
    z = jnp.fft.fftn(hg, axes=(1, 3), norm='ortho').real.reshape(B, L, D_MODEL)
    return jnp.einsum('bld,de->ble', z.astype(h.dtype), w_out)

def _hier_moe(h, w_rg, b_rg, w_re, b_re, w_gate, w_up, w_down):
    B, L, _ = h.shape
    t = h.reshape(B * L, D_MODEL)
    T = t.shape[0]
    pg = jax.nn.softmax((t @ w_rg + b_rg).astype(jnp.float32), axis=-1)
    gi = jnp.argmax(pg, axis=-1)
    pgv = jnp.max(pg, axis=-1, keepdims=True)
    el = (t @ w_re + b_re).astype(jnp.float32).reshape(T, MOE_GROUPS, MOE_EXPERTS_PER_GROUP)
    sel = jnp.take_along_axis(el, gi[:, None, None], axis=1)[:, 0]
    pe = jax.nn.softmax(sel, axis=-1)
    tv, ti = lax.top_k(pe, MOE_TOP_K)
    tv = tv / jnp.sum(tv, axis=-1, keepdims=True)
    eidx = gi[:, None] * MOE_EXPERTS_PER_GROUP + ti
    gates = jnp.sum(jax.nn.one_hot(eidx, MOE_EXPERTS, dtype=jnp.float32) * (pgv * tv)[..., None], axis=1)
    hid = jax.nn.silu(jnp.einsum('td,edf->tef', t, w_gate)) * jnp.einsum('td,edf->tef', t, w_up)
    y = jnp.einsum('tef,te,efd->td', hid, gates.astype(hid.dtype), w_down)
    return y.reshape(B, L, D_MODEL)

def _run_trunk(x, cond, init_states, w, lb):
    B = x.shape[0]
    states = []
    for i in range(DEPTH):
        j = i // N_MIXERS
        mod = jnp.einsum('bd,de->be', jax.nn.silu(cond), w['w_mod'][i]) + w['b_mod'][i]
        sh1, sc1, g1, sh2, sc2, g2 = jnp.split(mod, 6, axis=-1)
        h = _modulate(_rmsnorm(x, w['norm1_g'][i]), sh1, sc1)
        if i % N_MIXERS == 0:
            if init_states is None:
                s0_f = jnp.zeros((B, HGRN_HEADS, HGRN_DK, HGRN_DV), jnp.float32)
                s0_b = s0_f
            else:
                s0_f = init_states[:, j, 0].astype(jnp.float32)
                s0_b = init_states[:, j, 1].astype(jnp.float32)
            out, s_f, s_b = _hgrn_mixer(h, w['hgrn_w_in'][j], lb[j], w['hgrn_norm_g'][j], w['hgrn_w_out'][j], s0_f, s0_b)
            states.append(jnp.stack([s_f, s_b], axis=1))
        else:
            out = _fourier_mixer(h, w['fourier_w_out'][j])
        x = x + g1[:, None, :] * out
        h = _modulate(_rmsnorm(x, w['norm2_g'][i]), sh2, sc2)
        x = x + g2[:, None, :] * _hier_moe(h, w['router_group_w'][i], w['router_group_b'][i],
                                            w['router_expert_w'][i], w['router_expert_b'][i],
                                            w['moe_w_gate'][i], w['moe_w_up'][i], w['moe_w_down'][i])
    return _rmsnorm(x, w['final_norm_g']), states

def setup_inputs(seed: int = 0) -> dict:
    key = jax.random.key(seed)
    ks = jax.random.split(key, 22)
    f32 = jnp.float32

    def nrm(k, shape, s):
        return jax.random.normal(k, shape, f32) * s

    return {
        'x_prompt': nrm(ks[0], (BATCH, SEQ, D_MODEL), 1.0),
        'x_sample': nrm(ks[1], (DEC_BATCH, DEC_SEQ, D_MODEL), 1.0),
        'state_hgrn': nrm(ks[2], (DEC_BATCH, N_HGRN_LAYERS, 2, HGRN_HEADS, HGRN_DK, HGRN_DV), 0.5),
        'c': nrm(ks[3], (DEC_BATCH, D_MODEL), 1.0),
        'c_ctx': nrm(ks[4], (D_MODEL,), 1.0),
        'w_mod': nrm(ks[5], (DEPTH, D_MODEL, 6 * D_MODEL), 0.5 * D_MODEL ** -0.5),
        'b_mod': nrm(ks[6], (DEPTH, 6 * D_MODEL), 0.02),
        'norm1_g': 1.0 + nrm(ks[7], (DEPTH, D_MODEL), 0.02),
        'norm2_g': 1.0 + nrm(ks[8], (DEPTH, D_MODEL), 0.02),
        'hgrn_w_in': nrm(ks[9], (N_HGRN_LAYERS, D_MODEL, HGRN_IN), D_MODEL ** -0.5),
        'hgrn_lb_logits': nrm(ks[10], (N_HGRN_LAYERS, 2, HGRN_HK), 0.5),
        'hgrn_norm_g': 1.0 + nrm(ks[11], (N_HGRN_LAYERS, HGRN_HV), 0.02),
        'hgrn_w_out': nrm(ks[12], (N_HGRN_LAYERS, HGRN_HV, D_MODEL), HGRN_HV ** -0.5),
        'fourier_w_out': nrm(ks[13], (N_FOURIER_LAYERS, D_MODEL, D_MODEL), D_MODEL ** -0.5),
        'router_group_w': nrm(ks[14], (DEPTH, D_MODEL, MOE_GROUPS), D_MODEL ** -0.5),
        'router_group_b': nrm(ks[15], (DEPTH, MOE_GROUPS), 0.01),
        'router_expert_w': nrm(ks[16], (DEPTH, D_MODEL, MOE_EXPERTS), D_MODEL ** -0.5),
        'router_expert_b': nrm(ks[17], (DEPTH, MOE_EXPERTS), 0.01),
        'moe_w_gate': nrm(ks[18], (DEPTH, MOE_EXPERTS, D_MODEL, MOE_D_FF), D_MODEL ** -0.5),
        'moe_w_up': nrm(ks[19], (DEPTH, MOE_EXPERTS, D_MODEL, MOE_D_FF), D_MODEL ** -0.5),
        'moe_w_down': nrm(ks[20], (DEPTH, MOE_EXPERTS, MOE_D_FF, D_MODEL), MOE_D_FF ** -0.5),
        'final_norm_g': 1.0 + nrm(ks[21], (D_MODEL,), 0.02),
    }

def reference(x_prompt, x_sample, state_hgrn, c, c_ctx, w_mod, b_mod, norm1_g, norm2_g,
              hgrn_w_in, hgrn_lb_logits, hgrn_norm_g, hgrn_w_out, fourier_w_out,
              router_group_w, router_group_b, router_expert_w, router_expert_b,
              moe_w_gate, moe_w_up, moe_w_down, final_norm_g):
    w = {
        'w_mod': w_mod, 'b_mod': b_mod, 'norm1_g': norm1_g, 'norm2_g': norm2_g,
        'hgrn_w_in': hgrn_w_in, 'hgrn_norm_g': hgrn_norm_g, 'hgrn_w_out': hgrn_w_out,
        'fourier_w_out': fourier_w_out,
        'router_group_w': router_group_w, 'router_group_b': router_group_b,
        'router_expert_w': router_expert_w, 'router_expert_b': router_expert_b,
        'moe_w_gate': moe_w_gate, 'moe_w_up': moe_w_up, 'moe_w_down': moe_w_down,
        'final_norm_g': final_norm_g,
    }
    lb = _hgrn_lower_bounds(hgrn_lb_logits)
    y_prompt, ctx_states = _run_trunk(x_prompt, c_ctx[None, :], None, w, lb)
    new_state_hgrn = jnp.stack(ctx_states, axis=1).astype(x_prompt.dtype)
    x_lat = x_sample + _grid_pos_embed(x_sample.shape[1], x_sample.dtype)[None]
    y_sample, _ = _run_trunk(x_lat, c, state_hgrn, w, lb)
    return (y_prompt, y_sample, new_state_hgrn)


_drawn_inputs = setup_inputs


def setup_inputs(seed=0):
    import zlib

    import numpy as np

    out = dict(_drawn_inputs(seed))
    spreads = {}
    factors = {'state_hgrn': 8.0,
     'norm2_g': 6.275,
     'hgrn_norm_g': 6.995,
     'router_group_b': 8.0,
     'router_expert_b': 8.0,
     'final_norm_g': 2.742}
    for name, (base, spread) in spreads.items():
        noise = np.random.default_rng([zlib.crc32(name.encode()), seed]).standard_normal(out[name].shape)
        drawn = base * np.exp(spread * noise) if base else spread * noise
        out[name] = jnp.asarray(drawn.astype(out[name].dtype))
    for name, factor in factors.items():
        out[name] = (out[name] * factor).astype(out[name].dtype)
    return out
```

```python
from contextlib import ExitStack

import numpy as np
import concourse.bass as bass
from concourse import mybir

F32 = mybir.dt.float32
I32 = mybir.dt.int32
U32 = mybir.dt.uint32
ACT = mybir.ActivationFunctionType
ALU = mybir.AluOpType
AX = mybir.AxisListType

P = 128
D = 1024
KD = D // P
TT = 3
T = TT * P
NH = 8
HH = NH // 2
C512 = 512
NE = 16
NG = 4
NL = 20
F = 512
KF = F // P
WIN = 3
EPS = 1e-6
BIG = 4096.0
NEG = 1e30
RING = 6
UNIT = 4096
SIZES = [1, 2, 4, 8, 16, 32, 64]
SMALL = 32
GROUP_OF = [0, 1, 1]


def const_columns():
    at, n = {}, 0
    for name, w in [("ident", 128), ("upper", 128), ("ones", 128), ("iota", 128), ("sel", 256), ("sel2", 2),
                    ("rev_group", 4), ("rev_expert", 16), ("window", 3), ("value", 12),
                    ("minus_half", 4)]:
        at[name] = (n, n + w)
        n += w
    return at, n


CONST_AT, CONST_W = const_columns()
NMASK = 11


def program(nc, io, scratch):
    with ExitStack() as ctx:
        def sb(name, shape, dt=F32):
            return ctx.enter_context(nc.sbuf_tensor(name, shape, dt))

        def sem(name):
            return ctx.enter_context(nc.semaphore(name))

        ring = sb("ring", [P, RING, UNIT])
        x = sb("x", [P, TT, D])
        hT = sb("hT", [P, KD, T])
        gate_bc = sb("gate_bc", [P, 2, 2, D])
        WORK = 15800
        work = sb("work", [P, WORK])
        const = sb("const", [P, CONST_W])
        masks = sb("masks", [P, NMASK, SMALL], I32)
        cond = sb("cond", [P, 2, KD])
        scond = sb("scond", [P, 2, KD])
        gnorm = sb("gnorm", [P, 4, KD])
        colmod = sb("colmod", [P, 2, 4, KD, 2])
        colA = sb("colA", [P, KD, 2])
        stat = sb("stat", [P, 8])
        wroute = sb("wroute", [P, 2, KD, NL])
        broute = sb("broute", [P, 2, NL])
        ps = ctx.enter_context(nc.psum_tensor("ps", [P, 8, 512], F32))

        def c_(name):
            a, b = CONST_AT[name]
            return const[:, a:b]

        ident = c_("ident")

        class Area:
            def __init__(self, t, start=0):
                self.t, self.n = t, start

            def take(self, n):
                a = self.t[:, self.n:self.n + n]
                self.n += n
                return a

        flat_ring = ring[:].rearrange("p s n -> p (s n)")
        rows = work[:, WORK - 2 * D:WORK].rearrange("p (b n) -> p b n", b=2)
        xn = work[:, 0:TT * D].rearrange("p (t n) -> p t n", t=TT)
        hg = Area(work)
        oT = hg.take(KD * T).rearrange("p (k t) -> p k t", k=KD)
        qT = hg.take(HH * T)
        vrow = hg.take(TT * C512).rearrange("p (t n) -> p t n", t=TT)
        gsil = hg.take(TT * C512).rearrange("p (t n) -> p t n", t=TT)
        on = hg.take(TT * C512).rearrange("p (t n) -> p t n", t=TT)
        score = hg.take(TT * HH * P).rearrange("p (t h s) -> p t h s", t=TT, h=HH)
        compact = hg.take(TT * HH * SMALL).rearrange("p (a s) -> p a s", s=SMALL)
        kT = hg.take(2 * HH * P).rearrange("p (b h s) -> p b h s", b=2, h=HH)
        s0 = hg.take(2 * HH * P).rearrange("p (d h v) -> p d h v", d=2, h=HH)
        s1 = hg.take(2 * HH * P).rearrange("p (d h v) -> p d h v", d=2, h=HH)
        s_out = hg.take(2 * HH * P).rearrange("p (d h v) -> p d h v", d=2, h=HH)
        hnorm = hg.take(C512)
        ssq = hg.take(TT * HH).rearrange("p (t h) -> p t h", t=TT)
        rsq = hg.take(TT * HH).rearrange("p (t h) -> p t h", t=TT)
        tail = Area(flat_ring, 3 * UNIT)
        qd = [tail.take(HH * T) for _ in range(2)]
        kd = [tail.take(HH * T) for _ in range(2)]
        G = []
        for d in range(2):
            G.append({h: tail.take(HH * T // h) for h in SIZES + [128]})
        assert hg.n <= WORK and tail.n <= RING * UNIT
        fo = Area(work, TT * D)
        U = fo.take(TT * 4 * C512).rearrange("p (t g n) -> p t g n", t=TT, g=4)
        dft_c = fo.take(2 * C512).rearrange("p (k n) -> p k n", k=2)
        dft_ctx = fo.take(2 * P).rearrange("p (c n) -> p c n", c=2)
        dft_lat = fo.take(4 * 2 * P).rearrange("p (t c n) -> p t c n", t=2, c=2)
        zT = work[:, 0:TT * D].rearrange("p (k t) -> p k t", k=KD)
        assert fo.n <= WORK - 2 * D
        me = Area(work)
        hrow = me.take(TT * D).rearrange("p (t n) -> p t n", t=TT)
        yall = work[:, 0:2 * TT * D].rearrange("p (t c n) -> p t c n", t=TT, c=2)
        me.n = 2 * TT * D
        xg = me.take(D)
        xt = me.take(D).rearrange("p (k s) -> p k s", k=KD)
        sg = me.take(F)
        hid = me.take(F)
        hidT = me.take(F).rearrange("p (k s) -> p k s", k=KF)
        ysb = me.take(D)
        pos_oh = me.take(2 * TT * P).rearrange("p (c t s) -> p c t s", c=2, t=TT)
        vals = me.take(2 * TT * 2 * NE * WIN).rearrange("p (c t v e w) -> p c t v e w", c=2, t=TT, v=2, e=NE)
        lg = me.take(TT * NL).rearrange("p (t n) -> p t n", t=TT)
        r4 = me.take(TT * NG).rearrange("p (t n) -> p t n", t=TT)
        ohg = me.take(TT * NG).rearrange("p (t n) -> p t n", t=TT)
        el = me.take(TT * NE).rearrange("p (t n) -> p t n", t=TT)
        e16 = me.take(TT * NE).rearrange("p (t n) -> p t n", t=TT)
        oh = me.take(2 * TT * NE).rearrange("p (c t n) -> p c t n", c=2, t=TT)
        both = me.take(TT * NE).rearrange("p (t n) -> p t n", t=TT)
        pos = me.take(TT * NE).rearrange("p (t n) -> p t n", t=TT)
        small = me.take(16 * TT).rearrange("p (n t) -> p n t", t=TT)
        wnd = me.take(TT * WIN).rearrange("p (t w) -> p t w", t=TT)
        wv = me.take(TT * WIN).rearrange("p (t w) -> p t w", t=TT)
        assert me.n <= WORK - 2 * D, me.n
        slots_idx = sb("slots_idx", [P, 2, NE * WIN], U32)
        gi = sb("gi", [P, 1], U32)
        si = sb("si", [P, 1], U32)
        npass = sb("npass", [P, NE], I32)
        npass_f = sb("npass_f", [P, NE])
        wgt = sb("wgt", [P, 2, TT])

        landed = [sem(f"landed{s}") for s in range(RING)]
        s_const, s_x, s_cond, s_small = sem("const_in"), sem("x_in"), sem("cond_in"), sem("small_in")
        s_pos = sem("pos_in")
        scond_ready = sem("scond_ready")
        x_ready = sem("x_ready")
        mod_mm = [sem(f"mod_mm{l}") for l in range(2)]
        mod_evac = [sem(f"mod_evac{l}") for l in range(2)]
        mod_bias = [[sem(f"mod_bias{l}_{b}") for b in range(2)] for l in range(2)]
        mod_spread = [sem(f"mod_spread{l}") for l in range(2)]
        mod_col = [sem(f"mod_col{l}") for l in range(2)]
        NORM = {"a0": 0, "m0": 1, "a1": 2, "m1": 3, "fin": 4}
        n_sq = sem("square")
        n_rs = sem("rms")
        n_ms = sem("mean_square")
        o_ms, o_rs = sem("o_mean_square"), sem("o_rms")
        n_xn = sem("xn")
        n_tp = sem("xn_turned")
        n_hA = sem("hT_act")
        n_hV = sem("hT_dve")
        n_col = sem("col")
        proj_mm, proj_evac = sem("proj_mm"), sem("proj_evac")
        hg_in = sem("hgrn_in")
        hg_unit = sem("hgrn_unit_used")
        lvl_upd = [sem("level_updated_f"), sem("level_updated_b")]
        lvl_mm = [sem("level_scored_f"), sem("level_scored_b")]
        sd_copied = sem("compact_copied")
        score_ready, kT_mm, kT_ready, u_mm, s_ready = (sem("score_ready"), sem("kT_turned"), sem("kT_ready"),
                                                       sem("u_mm"), sem("state_ready"))
        off_copied = sem("score_off_copied")
        o_mm, o_sq, o_ready, o_tp, oT_ready = (sem("o_mm"), sem("o_square"), sem("o_ready"), sem("o_turned"),
                                               sem("oT_ready"))
        st_written = sem("state_written")
        gsil_ready = sem("gsil_ready")
        out_mm = [sem(f"out_mm{l}") for l in range(2)]
        out_x = [sem(f"out_x{l}") for l in range(2)]
        four_in, u_done4, u_evac4, z_done, z_evac = (sem("dft_in"), sem("dftc_mm"), sem("dftc_evac"),
                                                     sem("dftt_mm"), sem("dftt_evac"))
        M = []
        for l in range(2):
            M.append({n: sem(f"moe{l}_{n}") for n in [
                "logits", "chosen", "pos_mm", "onehots", "idx_mm", "idx_ready", "back_mm", "back_act", "back_dve",
                "hrow_out", "zeroed", "si_set", "gi_set", "gathered", "turned", "xt_a", "xt_b", "gate_mm", "up_mm",
                "silu", "hid", "hid_turned", "hidT", "y_mm_a", "y_mm_b", "y_a", "y_b", "scattered", "used", "yback", "all_out", "x_done",
                "exp_in", "exp_out"]})
        chain = sem("dve_chain")
        y_out = sem("y_out")
        fin_in = sem("final_gain_in")
        fin_done = sem("final_done")

        w_mod = io["w_mod"].rearrange("l (p k) n -> l p k n", k=KD)
        w_in = io["hgrn_w_in"].rearrange("l (p k) n -> l p k n", k=KD)
        w_o = [io["hgrn_w_out"].rearrange("l (k p) n -> l p k n", p=P),
               io["fourier_w_out"].rearrange("l (k p) n -> l p k n", p=P)]
        w_g = io["moe_w_gate"].rearrange("l e (p k) n -> l e p (k n)", k=KD)
        w_u = io["moe_w_up"].rearrange("l e (p k) n -> l e p (k n)", k=KD)
        w_d = io["moe_w_down"].rearrange("l e (p k) n -> l e p (k n)", k=KF)

        uses = [0] * RING
        plan = {}

        def place(phase, n, slots):
            for u in range(n):
                s = slots[u % len(slots)]
                uses[s] += 1
                plan[(phase, u)] = (s, 16 * uses[s])

        MOE_SLOTS = [[0, 1, 2, 3, 4, 5], [2, 3, 4, 5, 0, 1]]
        moe_before = []
        place("mod0", 12, [0, 1, 2, 3, 4, 5])
        place("hgrn", 12, [0, 1, 2])
        moe_before.append(list(uses))
        place("moe0", 3 * NE, MOE_SLOTS[0])
        place("mod1", 12, [0, 1, 2, 3, 4, 5])
        place("four", 2, [0, 1])
        moe_before.append(list(uses))
        place("moe1", 3 * NE, MOE_SLOTS[1])

        def slot3(s):
            return ring[:, s, :].rearrange("p (k n) -> p k n", k=KD)

        def slot_d(s):
            return ring[:, s, :].rearrange("p (k n) -> p k n", k=KF)

        def in_cols(u):
            half, kind = divmod(u, 5)
            return kind * D + half * C512

        block = ctx.enter_context(nc.Block())

        @block.sync
        def _(sp):
            def mod_units(l, first_wait):
                for u in range(12):
                    s, _ = plan[(f"mod{l}", u)]
                    first_wait(u)
                    sp.dma_start(slot3(s), w_mod[l, :, :, u * C512:(u + 1) * C512]).then_inc(landed[s], 16)

            def moe_units(l, first_wait):
                slots = MOE_SLOTS[l]
                for u in range(6):
                    first_wait(u)
                    w = [w_g, w_u, w_d][u % 3]
                    sp.dma_start(ring[:, slots[u], :], w[l, u // 3]).then_inc(landed[slots[u]], 16)
                with sp.Fori(1, NE // 2) as i:
                    for par in range(2):
                        sp.wait_ge(M[l]["used"], 2 * i + (par - 1))
                        for j, w in enumerate([w_g, w_u, w_d]):
                            s = slots[3 * par + j]
                            sp.dma_start(ring[:, s, :], w[l, 2 * i + par]).then_inc(landed[s], 16)

            sp.dma_start(cond[:, 0, :], io["c_ctx"].rearrange("(p k) -> p k", k=KD)).then_inc(s_cond, 16)
            sp.dma_start(cond[:, 1, :], io["c"].rearrange("b (p k) -> (b p) k", k=KD)).then_inc(s_cond, 16)
            sp.dma_start(const[:], io["const"]).then_inc(s_const, 16)

            def mod0_wait(u):
                if u >= RING:
                    sp.wait_ge(mod_mm[0], u - RING + 1)
                if u == 4:
                    sp.dma_start(x[:, 0, :], io["x_prompt"].rearrange("b t n -> (b t) n")).then_inc(s_x, 16)
                    sp.dma_start(x[:, 1:3, :], io["x_sample"].rearrange("b (t p) n -> (b p) t n", p=P)
                                 ).then_inc(s_x, 16)
                    sp.dma_start(yall[:, 0], io["pos"]).then_inc(s_pos, 16)

            mod_units(0, mod0_wait)

            for u in range(12):
                s, _ = plan[("hgrn", u)]
                if u < 3:
                    sp.wait_ge(mod_mm[0], 6 + u + 1)
                else:
                    sp.wait_ge(hg_unit, u - 2)
                src = (w_in[0, :, :, in_cols(u):in_cols(u) + C512] if u < 10
                       else w_o[0][0, :, :, (u - 10) * C512:(u - 9) * C512])
                sp.dma_start(slot3(s), src).then_inc(landed[s], 16)

            def moe0_wait(u):
                if u < 3:
                    sp.wait_ge(hg_unit, 10 + u if u < 2 else 12)
                elif u == 3:
                    sp.wait_ge(o_mm, 6)
            moe_units(0, moe0_wait)

            def mod1_wait(u):
                if u < RING:
                    if u % 3 == 0:
                        sp.wait_ge(M[0]["used"], NE - 1 + u // 3)
                else:
                    sp.wait_ge(mod_mm[1], u - RING + 1)
            mod_units(1, mod1_wait)

            for u in range(2):
                s, _ = plan[("four", u)]
                sp.wait_ge(mod_mm[1], 6 + u + 1)
                sp.dma_start(slot3(s), w_o[1][0, :, :, u * C512:(u + 1) * C512]).then_inc(landed[s], 16)

            def moe1_wait(u):
                if u < 4:
                    sp.wait_ge(mod_mm[1], 8 + u + 1)
                else:
                    sp.wait_ge(out_mm[1], 3 * (u - 4) + 3)
            moe_units(1, moe1_wait)

            sp.wait_ge(y_out, 16 * TT)
            sp.wait_ge(st_written, 16 * 4)

        @block.tensor
        def _(pe):
            mm = pe.matmul

            def modulation(l):
                if l == 0:
                    pe.wait_ge(scond_ready, 1)
                    pe.wait_ge(s_const, 16)

                def spread(q):
                    pe.wait_ge(mod_evac[l], 2 * q + 2)
                    pe.wait_ge(mod_bias[l][q % 2], 16 * (q // 2 + 1))
                    if q >= 1:
                        pe.wait_ge(mod_col[l], q)
                    row = rows[0:3, q % 2, :]
                    if q in (2, 5):
                        for g in range(2):
                            for j in range(2):
                                last = mm(ps[:, 4 + 2 * g + j, :], c_("sel")[0:3, g * P:(g + 1) * P],
                                          row[:, j * C512:(j + 1) * C512], start=True, stop=True)
                    else:
                        v = (row.rearrange("a (k p) -> a k p", p=P) if l == 1 and q < 2
                             else row.rearrange("a (p k) -> a k p", k=KD))
                        for k in range(KD):
                            last = mm(ps[:, 2, 2 * k:2 * k + 2], v[:, k, :], c_("sel2")[0:3, :],
                                      start=True, stop=True)
                    last.then_inc(mod_spread[l], 1)

                for u in range(12):
                    s, val = plan[(f"mod{l}", u)]
                    pe.wait_ge(landed[s], val)
                    if u >= 2:
                        pe.wait_ge(mod_evac[l], u - 1)
                    for k in range(KD):
                        last = mm(ps[0:2, u % 2, :], scond[:, :, k], slot3(s)[:, k, :],
                                  start=(k == 0), stop=(k == KD - 1))
                    last.then_inc(mod_mm[l], 1)
                    if u >= 2 and u % 2 == 0:
                        spread(u // 2 - 1)
                spread(5)

            def turn_norm(name, strided):
                for k in range(KD):
                    if k == 0:
                        pe.wait_ge(n_xn, 3 * NORM[name] + TT)
                    if k >= 4:
                        pe.wait_ge(n_hA if k % 2 == 0 else n_hV, 4 * NORM[name] + (k - 4) // 2 + 1)
                    for t in range(TT):
                        src = xn[:, t, k:D:KD] if strided else xn[:, t, k * P:(k + 1) * P]
                        last = pe.transpose(ps[:, k % 4, t * P:(t + 1) * P], src, ident)
                    last.then_inc(n_tp, 1)

            def wait_hT(name):
                pe.wait_ge(n_hA, 4 * NORM[name] + KD // 2)
                pe.wait_ge(n_hV, 4 * NORM[name] + KD // 2)

            def project_half(half):
                n = 18 * half
                for kind in range(5):
                    s, val = plan[("hgrn", 5 * half + kind)]
                    pe.wait_ge(landed[s], val)
                    W = slot3(s)
                    for c in range(4 if kind < 3 else TT):
                        if n % 18 >= 4:
                            pe.wait_ge(proj_evac, n - 3)
                        bank = ps[:, n % 18 % 4, :]
                        for k in range(KD):
                            if kind < 3:
                                last = mm(bank[:, 0:T], W[:, k, c * P:(c + 1) * P], hT[:, k, :],
                                          start=(k == 0), stop=(k == KD - 1))
                            else:
                                last = mm(bank, hT[:, k, c * P:(c + 1) * P], W[:, k, :],
                                          start=(k == 0), stop=(k == KD - 1))
                        last.then_inc(proj_mm, 1)
                        n += 1

            def scan_half(half):
                lv = half * len(SIZES)
                n = half * 11

                def compact_scores(d, i, lhs, rhs, more=None):
                    nonlocal n
                    if n >= half * 11 + 2:
                        pe.wait_ge(sd_copied, n - 1)
                    bank = ps[:, 4 + n % 2, :]
                    for t in range(TT):
                        for h in range(HH):
                            o = (t * HH + h) * SMALL
                            for g in range(4):
                                a = h * T + t * P + g * SMALL
                                pairs = [(lhs, rhs)] + ([more] if more else [])
                                for j, (L, R) in enumerate(pairs):
                                    last = mm(bank[g * SMALL:(g + 1) * SMALL, o:o + SMALL], L[:, a:a + SMALL],
                                              R[:, a:a + SMALL], start=(j == 0), stop=(j == len(pairs) - 1))
                    n += 1
                    return last

                pe.wait_ge(proj_evac, 18 * half + 12)
                compact_scores(0, 0, kd[0], qT, (kd[1], qT)).then_inc(lvl_mm[0], 1)
                for i, h in enumerate(SIZES):
                    for d in range(2):
                        pe.wait_ge(lvl_upd[d], lv + half + i + 1)
                        if h < SMALL:
                            last = compact_scores(d, i, kd[d], qd[d])
                        else:
                            if h == SMALL and d == 0:
                                pe.wait_ge(proj_evac, 18 * half + 18)
                            for t in range(TT):
                                for hh in range(HH):
                                    for b in range(0, P, 2 * h):
                                        lo, hi = b, b + h
                                        sk, tq = (lo, hi) if d == 0 else (hi, lo)
                                        a = hh * T + t * P
                                        last = mm(ps[sk:sk + h, t, hh * P + tq:hh * P + tq + h],
                                                  kd[d][:, a + sk:a + sk + h], qd[d][:, a + tq:a + tq + h],
                                                  start=True, stop=True)
                        last.then_inc(lvl_mm[d], 1)
                pe.wait_ge(lvl_upd[0], lv + half + 8)
                pe.wait_ge(lvl_upd[1], lv + half + 8)
                UNITS = [(0, 0), (0, 1), (1, 0), (2, 1)]

                def turn_keys(j):
                    t, d = UNITS[j]
                    if 4 * half + j >= 2:
                        pe.wait_ge(kT_ready, 4 * half + j - 1)
                        pe.wait_ge(u_mm, 4 * half + j - 1)
                    for h in range(HH):
                        a = h * T + t * P
                        last = pe.transpose(ps[:, [3, 7][j % 2], h * P:(h + 1) * P], kd[d][:, a:a + P], ident)
                    last.then_inc(kT_mm, 1)

                def increment(j):
                    t, d = UNITS[j]
                    pe.wait_ge(kT_ready, 4 * half + j + 1)
                    if j == 0:
                        pe.wait_ge(sd_copied, 11 * half + 11)
                    if j >= 2:
                        pe.wait_ge(s_ready, 4 * half + j - 1)
                    for h in range(HH):
                        last = mm(ps[:, 4 + j % 2, h * P:(h + 1) * P], kT[:, j % 2, h, :],
                                  vrow[:, t, h * P:(h + 1) * P], start=True, stop=True)
                    last.then_inc(u_mm, 1)

                turn_keys(0)
                turn_keys(1)
                for j in range(4):
                    increment(j)
                    if j + 2 < 4:
                        turn_keys(j + 2)

                OB = [6, 7, 3]
                pe.wait_ge(score_ready, 4 * (half + 1))
                pe.wait_ge(s_ready, 4 * half + 4)
                pe.wait_ge(kT_ready, 4 * half + 4)
                for t in range(TT):
                    for h in range(HH):
                        a = h * T + t * P
                        out = ps[:, OB[t], h * P:(h + 1) * P]
                        last = mm(out, score[:, t, h, :], vrow[:, t, h * P:(h + 1) * P], start=True, stop=(t == 0))
                        if t:
                            st_f = s0[:, 0, h, :] if t == 1 else s1[:, 0, h, :]
                            st_b = s1[:, 1, h, :] if t == 1 else s0[:, 1, h, :]
                            mm(out, qd[0][:, a:a + P], st_f, start=False, stop=False)
                            last = mm(out, qd[1][:, a:a + P], st_b, start=False, stop=True)
                    last.then_inc(o_mm, 1)
                for t in range(TT):
                    pe.wait_ge(o_ready, 3 * half + t + 1)
                    for h in range(HH):
                        last = pe.transpose(ps[:, 4 + t % 2 if t < 2 else 6, h * P:(h + 1) * P],
                                            on[:, t, h * P:(h + 1) * P], ident)
                    last.then_inc(o_tp, 1)

            def out_project(l, src, phase, u0):
                for j in range(2):
                    s, val = plan[(phase, u0 + j)]
                    pe.wait_ge(landed[s], val)
                    for t in range(TT):
                        n = 3 * j + t
                        if n >= 4:
                            pe.wait_ge(out_x[l], n - 3)
                        for k in range(KD):
                            last = mm(ps[:, n % 4, :], src[:, k, t * P:(t + 1) * P], slot3(s)[:, k, :],
                                      start=(k == 0), stop=(k == KD - 1))
                        last.then_inc(out_mm[l], 1)

            def fourier():
                pe.wait_ge(four_in, 48)
                for t in range(TT):
                    for g in range(4):
                        n = 4 * t + g
                        if n >= 4:
                            pe.wait_ge(u_evac4, n - 3)
                        for k in range(2):
                            last = mm(ps[:, 4 + n % 4, :], hT[:, 2 * g + k, t * P:(t + 1) * P], dft_c[:, k, :],
                                      start=(k == 0), stop=(k == 1))
                        last.then_inc(u_done4, 1)
                pe.wait_ge(u_evac4, 12)
                for k in range(KD):
                    if k >= 4:
                        pe.wait_ge(z_evac, k - 3)
                    g, o = k // 2, (k % 2) * P
                    bank = ps[:, k % 4, :]
                    for c in range(2):
                        mm(bank[:, 0:P], U[:, 0, g, c * 256 + o:c * 256 + o + P], dft_ctx[:, c, :],
                           start=(c == 0), stop=(c == 1))
                    for t in range(2):
                        for c in range(2):
                            last = mm(bank[:, P:T], U[:, 1 + t, g, c * 256 + o:c * 256 + o + P], dft_lat[:, t, c, :],
                                      start=(t + c == 0), stop=(t + c == 2))
                    last.then_inc(z_done, 1)

            def route(l):
                m = M[l]
                for t in range(TT):
                    for k in range(KD):
                        last = mm(ps[:, 4, t * 32:t * 32 + NL], hT[:, k, t * P:(t + 1) * P], wroute[:, l, k, :],
                                  start=(k == 0), stop=(k == KD - 1))
                last.then_inc(m["logits"], 1)
                for t in range(TT):
                    for j in range(2):
                        n = 2 * t + j
                        if n >= 4:
                            pe.wait_ge(m["back_act"] if j == 0 else m["back_dve"], t - 1)
                        for k in range(4):
                            last = pe.transpose(ps[:, n % 4, k * P:(k + 1) * P],
                                                hT[:, 4 * j + k, t * P:(t + 1) * P], ident)
                        last.then_inc(m["back_mm"], 1)
                pe.wait_ge(m["chosen"], 1)
                for t in range(TT):
                    mm(ps[:, 5, t * NE:(t + 1) * NE], c_("upper"), both[:, t, :], start=True, stop=(t == 0))
                    for b in range(t):
                        mm(ps[:, 5, t * NE:(t + 1) * NE], c_("ones"), both[:, b, :], start=False, stop=(b == t - 1))
                for t in range(TT):
                    last = mm(ps[:, 5, TT * NE:(TT + 1) * NE], c_("ones"), both[:, t, :],
                              start=(t == 0), stop=(t == TT - 1))
                last.then_inc(m["pos_mm"], 1)
                pe.wait_ge(m["onehots"], 1)
                for c in range(2):
                    for t in range(TT):
                        last = mm(ps[:, 6, 0:2 * NE * WIN], pos_oh[:, c, t, :],
                                  vals[:, c, t].rearrange("p v e w -> p (v e w)"),
                                  start=(c + t == 0), stop=(c == 1 and t == TT - 1))
                last.then_inc(m["idx_mm"], 1)

            def turn_tokens(m):
                for k in range(KD):
                    last = pe.transpose(ps[:, k // 4, (k % 4) * P:(k % 4 + 1) * P], xg[:, k * P:(k + 1) * P], ident)
                last.then_inc(m["turned"], 1)

            def experts(l):
                m = M[l]
                pe.wait_ge(m["idx_ready"], 1)
                n = pe.alloc_register(f"pe_pass{l}")
                pe.reg_mov(n, 0)
                pe.wait_ge(m["gathered"], 16)
                turn_tokens(m)
                with pe.Fori(0, NE // 2) as i:
                    for par in range(2):
                        S = [MOE_SLOTS[l][3 * par + j] for j in range(3)]
                        windows = pe.value_load(npass[0:1, bass.ds(2 * i + par, 1)], min_val=1, max_val=WIN)
                        with pe.Fori(0, windows):
                            pe.reg_add(n, n, 1)
                            k_ = pe.snap(n, min_val=1, max_val=WIN * NE)
                            for s in S:
                                pe.wait_ge(landed[s], 16 * i + 16 * (moe_before[l][s] + 1))
                            pe.wait_ge(m["xt_a"], k_)
                            pe.wait_ge(m["xt_b"], k_)
                            for j, name in ((0, "gate_mm"), (1, "up_mm")):
                                for k in range(KD):
                                    last = mm(ps[:, 2 + j, :], xt[:, k, :], slot3(S[j])[:, k, :],
                                              start=(k == 0), stop=(k == KD - 1))
                                last.then_inc(m[name], 1)
                            pe.wait_ge(m["gathered"], 16 * k_ + 16)
                            turn_tokens(m)
                            pe.wait_ge(m["hid"], k_)
                            for k in range(KF):
                                last = pe.transpose(ps[:, 4, k * P:(k + 1) * P], hid[:, k:F:KF], ident)
                            last.then_inc(m["hid_turned"], 1)
                            pe.wait_ge(m["hidT"], k_)
                            pe.wait_ge(m["y_a"], k_)
                            pe.wait_ge(m["y_b"], k_)
                            for j in range(2):
                                for k in range(KF):
                                    last = mm(ps[:, 5 + j, :], hidT[:, k, :],
                                              slot_d(S[2])[:, k, j * C512:(j + 1) * C512],
                                              start=(k == 0), stop=(k == KF - 1))
                                last.then_inc(m["y_mm_a" if j == 0 else "y_mm_b"], 1)

                pe.reg_add(n, n, 1)
                k_ = pe.snap(n, min_val=NE + 1, max_val=WIN * NE + 1)
                for name in ("xt_a", "xt_b", "y_a", "y_b"):
                    pe.wait_ge(m[name], k_)

            modulation(0)
            turn_norm("a0", True)
            wait_hT("a0")
            for half in range(2):
                project_half(half)
                scan_half(half)
            pe.wait_ge(oT_ready, 6)
            out_project(0, oT, "hgrn", 10)
            turn_norm("m0", True)
            wait_hT("m0")
            route(0)
            experts(0)
            modulation(1)
            turn_norm("a1", False)
            wait_hT("a1")
            fourier()
            pe.wait_ge(z_evac, KD)
            out_project(1, zT, "four", 0)
            turn_norm("m1", True)
            wait_hT("m1")
            route(1)
            experts(1)

        @block.scalar
        def _(act):
            A = nc.scalar.activation

            def modulation(l):
                for u in range(12):
                    q, j = divmod(u, 2)
                    if j == 0:
                        if q >= 2:
                            act.wait_ge(mod_spread[l], q - 1)
                        if l == 1 and q == 0:
                            act.wait_ge(M[0]["used"], NE)
                        act.dma_start(rows[2:3, q % 2, :], io["b_mod"][l:l + 1, q * D:(q + 1) * D]
                                      ).then_inc(mod_bias[l][q % 2], 16)
                    act.wait_ge(mod_mm[l], u + 1)
                    A(rows[0:2, q % 2, j * C512:(j + 1) * C512], ps[0:2, u % 2, :], ACT.Copy
                      ).then_inc(mod_evac[l], 1)
                    if u >= 2 and u % 2 == 0:
                        spread_out(l, u // 2 - 1)
                spread_out(l, 5)

            def spread_out(l, q):
                act.wait_ge(mod_spread[l], q + 1)
                if q in (2, 5):
                    w = q // 3
                    if l == 1:
                        act.wait_ge(out_x[0], 6) if w == 0 else act.wait_ge(M[0]["x_done"], TT)
                    for g in range(2):
                        last = A(gate_bc[:, w, g, :].rearrange("p (j n) -> p j n", j=2), ps[:, 4 + 2 * g:6 + 2 * g, :],
                                 ACT.Copy)
                else:
                    c = {0: 0, 1: 1, 3: 2, 4: 3}[q]
                    last = A(colmod[:, l, c].rearrange("p k g -> p (k g)"), ps[:, 2, 0:2 * KD], ACT.Copy)
                last.then_inc(mod_col[l], 1)

            def squares(name):
                for t in range(TT):
                    if name == "a0":
                        act.wait_ge(x_ready, 1)
                    elif name in ("m0", "m1"):
                        act.wait_ge(out_mm[int(name[1])], 6)
                        act.wait_ge(out_x[int(name[1])], 4 + t)
                    else:
                        act.wait_ge(M[0 if name == "a1" else 1]["x_done"], t + 1)
                    A(xn[:, t, :], x[:, t, :], ACT.Square, accum_out=stat[:, t:t + 1]).then_inc(n_sq, 1)

            def modulate(name, l, which):
                act.wait_ge(n_col, 1 * NORM[name] + 1)
                for k in range(0, KD, 2):
                    act.wait_ge(n_tp, 8 * NORM[name] + k + 1)
                    A(hT[:, k, 0:P], ps[:, k % 4, 0:P], ACT.Identity, bias=colmod[:, l, 2 * which, k, 0:1],
                      scale=colA[:, k, 0:1])
                    A(hT[:, k, P:T], ps[:, k % 4, P:T], ACT.Identity, bias=colmod[:, l, 2 * which, k, 1:2],
                      scale=colA[:, k, 1:2]).then_inc(n_hA, 1)

            def project_half(half):
                n = 18 * half
                if half == 1:
                    act.wait_ge(s_ready, 4)
                    act.wait_ge(o_mm, 3)
                for kind in range(5):
                    for c in range(4 if kind < 3 else TT):
                        act.wait_ge(proj_mm, n + 1)
                        bank = ps[:, n % 18 % 4, :]
                        sl = slice(c * T, (c + 1) * T)
                        if kind == 0:
                            ins = A(qT[:, sl], bank[:, 0:T], ACT.Copy)
                        elif kind < 3:
                            A(G[kind - 1][1][:, sl], bank[:, 0:T], ACT.Sigmoid)
                            ins = A(kd[kind - 1][:, sl], bank[:, 0:T], ACT.Sigmoid, scale=-1.0)
                        elif kind == 3:
                            ins = A(vrow[:, c, :], bank, ACT.Copy)
                        else:
                            if half == 1 and c == 0:
                                act.wait_ge(o_ready, 3)
                            ins = A(gsil[:, c, :], bank, ACT.Silu)
                        ins.then_inc(proj_evac, 1)
                        n += 1
                    act.sem_inc(hg_unit, 1)

            def scan_half(half):
                act.wait_ge(lvl_mm[0], 8 * half + 8)
                act.wait_ge(lvl_mm[1], 7 * half + 7)
                A(score[:].rearrange("p t h s -> p t (h s)"), ps[:, 0:3, :], ACT.Copy).then_inc(off_copied, 1)
                act.wait_ge(off_copied, half + 1)
                act.wait_ge(sd_copied, 11 * half + 11)
                for g in range(4):
                    r = slice(g * SMALL, (g + 1) * SMALL)
                    A(score[r].rearrange("p t h s -> p (t h) s")[:, :, r], compact[r], ACT.Copy
                      ).then_inc(score_ready, 1)
                for j in range(4):
                    act.wait_ge(kT_mm, 4 * half + j + 1)
                    A(kT[:, j % 2].rearrange("p h s -> p (h s)"), ps[:, [3, 7][j % 2], :], ACT.Copy
                      ).then_inc(kT_ready, 1)
                OB = [6, 7, 3]
                for t in range(TT):
                    act.wait_ge(o_mm, 3 * half + t + 1)
                    for h in range(HH):
                        last = A(on[:, t, h * P:(h + 1) * P], ps[:, OB[t], h * P:(h + 1) * P],
                                 ACT.Square, accum_out=ssq[:, t, h:h + 1])
                    last.then_inc(o_sq, 1)
                for t in range(TT):
                    act.wait_ge(o_tp, 3 * half + t + 1)
                    A(oT[:, HH * half:HH * (half + 1), t * P:(t + 1) * P],
                      ps[:, 4 + t % 2 if t < 2 else 6, :].rearrange("p (h s) -> p h s", h=HH), ACT.Copy
                      ).then_inc(oT_ready, 1)

            def route(l):
                m = M[l]
                act.wait_ge(m["exp_in"], 1)
                A(r4[:], r4[:], ACT.Exp).then_inc(m["exp_out"], 1)
                for t in range(TT):
                    act.wait_ge(m["back_mm"], 2 * t + 1)
                    A(hrow[:, t, 0:C512], ps[:, (2 * t) % 4, :], ACT.Copy).then_inc(m["back_act"], 1)
                    act.wait_ge(m["back_act"], t + 1)
                    act.wait_ge(m["back_dve"], t + 1)
                    act.dma_start(scratch["hrow"][l].rearrange("(t p) n -> p t n", p=P)[:, t, :], hrow[:, t, :]
                                  ).then_inc(m["hrow_out"], 16)
                act.wait_ge(m["exp_in"], 2)
                A(small[:, 6, :], small[:, 5, :], ACT.Exp).then_inc(m["exp_out"], 1)

            def experts(l):
                m = M[l]
                act.wait_ge(m["idx_ready"], 1)
                n = act.alloc_register(f"act_pass{l}")
                act.reg_mov(n, 0)
                act.wait_ge(m["turned"], 1)
                A(xt[:, 0:4, :].rearrange("p k s -> p (k s)"), ps[:, 0, :], ACT.Copy).then_inc(m["xt_a"], 1)
                with act.Fori(0, NE) as e:
                    windows = act.value_load(npass[0:1, bass.ds(e, 1)], min_val=1, max_val=WIN)
                    with act.Fori(0, windows):
                        act.reg_add(n, n, 1)
                        k_ = act.snap(n, min_val=1, max_val=WIN * NE)
                        act.wait_ge(m["gate_mm"], k_)
                        A(sg, ps[:, 2, :], ACT.Silu).then_inc(m["silu"], 1)
                        act.wait_ge(m["turned"], k_ + 1)
                        A(xt[:, 0:4, :].rearrange("p k s -> p (k s)"), ps[:, 0, :], ACT.Copy).then_inc(m["xt_a"], 1)
                        act.wait_ge(m["hid_turned"], k_)
                        A(hidT[:].rearrange("p k s -> p (k s)"), ps[:, 4, :], ACT.Copy).then_inc(m["hidT"], 1)
                        act.wait_ge(m["y_mm_a"], k_)
                        act.wait_ge(m["scattered"], 16 * k_)
                        A(ysb[:, 0:C512], ps[:, 5, :], ACT.Copy).then_inc(m["y_a"], 1)

            with nc.allow_non_contiguous_dma(reason="per-channel gains, small"):
                for j, (src, l) in enumerate([("norm1_g", 0), ("norm2_g", 0), ("norm1_g", 1), ("norm2_g", 1)]):
                    v = io[src][l]
                    v = v.rearrange("(k p) -> p k", p=P) if j == 2 else v.rearrange("(p k) -> p k", k=KD)
                    act.dma_start(gnorm[:, j, :], v).then_inc(s_small, 16)
                for l in range(2):
                    act.dma_start(wroute[:, l, :, 0:NG], io["router_group_w"][l].rearrange("(p k) n -> p k n", k=KD)
                                  ).then_inc(s_small, 16)
                    act.dma_start(wroute[:, l, :, NG:NL], io["router_expert_w"][l].rearrange("(p k) n -> p k n", k=KD)
                                  ).then_inc(s_small, 16)
                    act.dma_start(broute[:, l, 0:NG], io["router_group_b"][l:l + 1, :].to_broadcast((P, NG))
                                  ).then_inc(s_small, 16)
                    act.dma_start(broute[:, l, NG:NL], io["router_expert_b"][l:l + 1, :].to_broadcast((P, NE))
                                  ).then_inc(s_small, 16)
                act.dma_start(masks[:], io["masks"]).then_inc(s_small, 16)
            act.wait_ge(s_cond, 32)
            A(scond[:], cond[:], ACT.Silu).then_inc(scond_ready, 1)
            modulation(0)
            squares("a0")
            modulate("a0", 0, 0)
            act.wait_ge(n_tp, 8 * NORM["a0"] + KD)
            for half in range(2):
                if half == 1:
                    act.wait_ge(o_mm, 3)
                    act.wait_ge(gsil_ready, 3)
                for d in range(2):
                    act.dma_start(s0[:, d], io["state_hgrn"][0, 0, d, HH * half:HH * (half + 1)]
                                  .rearrange("h k v -> k h v")).then_inc(hg_in, 16)
                act.dma_start(hnorm, io["hgrn_norm_g"][:, C512 * half:C512 * (half + 1)].to_broadcast((P, C512))
                              ).then_inc(hg_in, 16)
                project_half(half)
                scan_half(half)
            act.wait_ge(out_mm[0], 3)
            act.sem_inc(hg_unit, 1)
            act.wait_ge(out_mm[0], 6)
            act.sem_inc(hg_unit, 1)
            squares("m0")
            modulate("m0", 0, 1)
            route(0)
            experts(0)
            modulation(1)
            squares("a1")
            act.dma_start(dft_c[:], io["dft_c"]).then_inc(four_in, 16)
            act.dma_start(dft_ctx[:], io["dft_ctx"]).then_inc(four_in, 16)
            act.dma_start(dft_lat[:], io["dft_lat"]).then_inc(four_in, 16)
            modulate("a1", 1, 0)
            for n in range(12):
                act.wait_ge(u_done4, n + 1)
                A(U[:, n // 4, n % 4, :], ps[:, 4 + n % 4, :], ACT.Copy).then_inc(u_evac4, 1)
            for k in range(KD):
                act.wait_ge(z_done, k + 1)
                A(zT[:, k, :], ps[:, k % 4, 0:T], ACT.Copy).then_inc(z_evac, 1)
            squares("m1")
            modulate("m1", 1, 1)
            route(1)
            experts(1)
            squares("fin")

        @block.vector
        def _(dve):
            V = nc.vector
            count = [0]

            def step(ins):
                count[0] += 1
                ins.then_inc(chain, 1)
                dve.wait_ge(chain, count[0])

            def normalise(name, tail_sem=None):
                for t in range(TT):
                    if t == 0:
                        dve.wait_ge(n_rs, 1 * NORM[name] + 1)
                    V.tensor_scalar(xn[:, t, :], x[:, t, :], stat[:, 3 + t:4 + t], None, ALU.mult).then_inc(n_xn, 1)

            def modulate(name, l, which):
                for g in range(2):
                    ins = V.scalar_tensor_tensor(out=colA[:, :, g], in0=colmod[:, l, 2 * which + 1, :, g], scalar=1.0,
                                                 in1=gnorm[:, 2 * l + which, :], op0=ALU.add, op1=ALU.mult)
                    if g == 0:
                        step(ins)
                ins.then_inc(n_col, 1)
                dve.wait_ge(n_col, 1 * NORM[name] + 1)
                for k in range(1, KD, 2):
                    dve.wait_ge(n_tp, 8 * NORM[name] + k + 1)
                    V.tensor_scalar(hT[:, k, 0:P], ps[:, k % 4, 0:P], colA[:, k, 0:1],
                                    colmod[:, l, 2 * which, k, 0:1], ALU.mult, ALU.add)
                    V.tensor_scalar(hT[:, k, P:T], ps[:, k % 4, P:T], colA[:, k, 1:2],
                                    colmod[:, l, 2 * which, k, 1:2], ALU.mult, ALU.add).then_inc(n_hV, 1)

            def scan_half(half):
                n = 11 * half
                lv = 8 * half

                def take_compact(m, wait):
                    nonlocal n
                    if n:
                        dve.wait_ge(sd_copied, n)
                    V.copy_predicated(compact[:], masks[:, m:m + 1, :].to_broadcast((P, TT * HH, SMALL)),
                                      ps[:, 4 + n % 2, 0:TT * HH * SMALL].rearrange("p (a s) -> p a s", s=SMALL)
                                      ).then_inc(sd_copied, 1)
                    n += 1

                if half == 1:
                    dve.wait_ge(score_ready, 4)
                dve.wait_ge(proj_evac, 18 * half + 12)
                for d in range(2):
                    V.tensor_tensor(qd[d], qT, G[d][1], ALU.mult).then_inc(lvl_upd[d], 1)
                dve.wait_ge(lvl_mm[0], 8 * half + 1)
                take_compact(10, None)
                for i, h in enumerate(SIZES):
                    for d in range(2):
                        dve.wait_ge(lvl_mm[d], (8 * half + 2 + i) if d == 0 else (7 * half + 1 + i))
                        dve.wait_ge(lvl_upd[d], lv + i + 1)
                        halves = [a.rearrange("p (b two h) -> p b two h", two=2, h=h) for a in (qd[d], kd[d])]
                        nb = HH * T // (2 * h)
                        g = G[d][h].rearrange("p (b two) -> p b two", two=2)
                        late, early = (1, 0) if d == 0 else (0, 1)
                        V.tensor_tensor(halves[0][:, :, late, :], halves[0][:, :, late, :],
                                        g[:, :, early:early + 1].to_broadcast((P, nb, h)), ALU.mult)
                        V.tensor_tensor(halves[1][:, :, early, :], halves[1][:, :, early, :],
                                        g[:, :, late:late + 1].to_broadcast((P, nb, h)), ALU.mult)
                        V.tensor_tensor(G[d][2 * h], g[:, :, 0], g[:, :, 1], ALU.mult).then_inc(lvl_upd[d], 1)
                        if h < SMALL:
                            take_compact(2 * i + d, None)
                dve.wait_ge(hg_in, 48 * (half + 1))
                dve.wait_ge(lvl_upd[0], lv + 8)
                dve.wait_ge(lvl_upd[1], lv + 8)
                for j in range(4):
                    dve.wait_ge(u_mm, 4 * half + j + 1)
                    bank = ps[:, 4 + j % 2, :]
                    if j < 2:
                        if half == 1:
                            dve.wait_ge(st_written, 32)
                        V.tensor_copy(s_out[:, j].rearrange("p h v -> p (h v)"), bank).then_inc(s_ready, 1)
                    else:
                        t, d = (1, 0) if j == 2 else (2, 1)
                        for h in range(HH):
                            c = h * TT + t
                            ins = V.scalar_tensor_tensor(out=s1[:, d, h, :], in0=s0[:, d, h, :],
                                                         scalar=G[d][128][:, c:c + 1],
                                                         in1=bank[:, h * P:(h + 1) * P], op0=ALU.mult, op1=ALU.add)
                        ins.then_inc(s_ready, 1)
                dve.wait_ge(proj_evac, 18 * half + 18)
                for t in range(TT):
                    ins = V.tensor_tensor(gsil[:, t, :], gsil[:, t, :], hnorm, ALU.mult)
                    ins.then_inc(gsil_ready, 1)
                dve.wait_ge(gsil_ready, 3 * half + 3)
                OB = [6, 7, 3]
                for t in range(TT):
                    dve.wait_ge(o_rs, 3 * half + t + 1)
                    for h in range(HH):
                        s = slice(h * P, (h + 1) * P)
                        ins = V.scalar_tensor_tensor(out=on[:, t, s], in0=ps[:, OB[t], s], scalar=rsq[:, t, h:h + 1],
                                                     in1=gsil[:, t, s], op0=ALU.mult, op1=ALU.mult)
                    ins.then_inc(o_ready, 1)

            def residual(l):
                for n in range(6):
                    j, t = divmod(n, 3)
                    dve.wait_ge(out_mm[l], n + 1)
                    s = slice(j * C512, (j + 1) * C512)
                    tmp = [sg, hid][n % 2]
                    if n >= 2:
                        dve.wait_ge(out_x[l], n - 1)
                    step(V.tensor_tensor(tmp, ps[:, n % 4, :], gate_bc[:, 0, GROUP_OF[t], s], ALU.mult))
                    V.tensor_tensor(x[:, t, s], x[:, t, s], tmp, ALU.add).then_inc(out_x[l], 1)
                dve.wait_ge(out_x[l], 6)

            def route(l):
                m = M[l]
                b3 = lambda a, w: a.rearrange("p (t o) -> p t o", o=1).to_broadcast((P, TT, w))
                sm = lambda i: small[:, i, :]
                rg = c_("rev_group").rearrange("p (o n) -> p o n", o=1).to_broadcast((P, TT, NG))
                re = c_("rev_expert").rearrange("p (o n) -> p o n", o=1).to_broadcast((P, TT, NE))
                dve.wait_ge(s_small, 16 * 13)
                dve.wait_ge(m["logits"], 1)
                step(V.tensor_tensor(lg[:], ps[:, 4, 0:TT * 32].rearrange("p (t n) -> p t n", n=32)[:, :, 0:NL],
                                     broute[:, l:l + 1, :].to_broadcast((P, TT, NL)), ALU.add))
                step(V.tensor_reduce(sm(0), lg[:, :, 0:NG], AX.X, ALU.max))
                V.tensor_tensor(r4[:], lg[:, :, 0:NG], b3(sm(0), NG), ALU.subtract).then_inc(m["exp_in"], 1)
                step(V.tensor_tensor(ohg[:], lg[:, :, 0:NG], b3(sm(0), NG), ALU.is_equal))
                step(V.tensor_tensor(ohg[:], ohg[:], rg, ALU.mult))
                step(V.tensor_reduce(sm(1), ohg[:], AX.X, ALU.max))
                step(V.tensor_tensor(ohg[:], rg, b3(sm(1), NG), ALU.is_equal))
                go = ohg[:].rearrange("p t (g o) -> p t g o", o=1)
                for t in range(TT):
                    ins = V.tensor_tensor(el[:, t].rearrange("p (g e) -> p g e", g=NG),
                                          lg[:, t, NG:NL].rearrange("p (g e) -> p g e", g=NG),
                                          go[:, t].to_broadcast((P, NG, 4)), ALU.mult)
                    ins2 = V.tensor_scalar(e16[:, t].rearrange("p (g e) -> p g e", g=NG),
                                           go[:, t].to_broadcast((P, NG, 4)), -1.0, NEG, ALU.add, ALU.mult)
                step(ins2)
                step(V.tensor_tensor(el[:], el[:], e16[:], ALU.add))
                for c in range(2):
                    step(V.tensor_reduce(sm(2 + c), el[:], AX.X, ALU.max))
                    step(V.tensor_tensor(oh[:, c], el[:], b3(sm(2 + c), NE), ALU.is_equal))
                    step(V.tensor_tensor(oh[:, c], oh[:, c], re, ALU.mult))
                    step(V.tensor_reduce(sm(4), oh[:, c], AX.X, ALU.max))
                    step(V.tensor_tensor(oh[:, c], re, b3(sm(4), NE), ALU.is_equal))
                    if c == 0:
                        step(V.tensor_scalar(e16[:], oh[:, 0], -4 * NEG, None, ALU.mult))
                        step(V.tensor_tensor(el[:], el[:], e16[:], ALU.add))
                V.tensor_tensor(both[:], oh[:, 0], oh[:, 1], ALU.add).then_inc(m["chosen"], 1)
                V.tensor_tensor(sm(5), sm(3), sm(2), ALU.subtract).then_inc(m["exp_in"], 1)
                for t in range(TT):
                    dve.wait_ge(m["back_mm"], 2 * t + 2)
                    V.tensor_copy(hrow[:, t, C512:D], ps[:, (2 * t + 1) % 4, :]).then_inc(m["back_dve"], 1)
                dve.wait_ge(m["exp_out"], 2)
                step(V.tensor_reduce(sm(7), r4[:], AX.X, ALU.add))
                step(V.tensor_scalar(sm(8), sm(6), 1.0, None, ALU.add))
                step(V.tensor_tensor(sm(7), sm(7), sm(8), ALU.mult))
                step(V.reciprocal(wgt[:, 0, :], sm(7)))
                step(V.tensor_tensor(wgt[:, 1, :], wgt[:, 0, :], sm(6), ALU.mult))
                dve.wait_ge(m["pos_mm"], 1)
                step(V.tensor_copy(pos[:].rearrange("p t n -> p (t n)"), ps[:, 5, 0:TT * NE]))
                step(V.tensor_scalar(npass_f[:], ps[:, 5, TT * NE:(TT + 1) * NE], float(2 * P), 1.0, ALU.is_gt, ALU.add))
                step(V.scalar_tensor_tensor(out=npass_f[:], in0=ps[:, 5, TT * NE:(TT + 1) * NE], scalar=float(P),
                                            in1=npass_f[:], op0=ALU.is_gt, op1=ALU.add))
                step(V.tensor_copy(npass[:], npass_f[:]))
                for c in range(2):
                    step(V.tensor_tensor(e16[:], pos[:], oh[:, c], ALU.mult))
                    step(V.tensor_reduce(sm(9), e16[:], AX.X, ALU.add))
                    step(V.tensor_scalar(sm(10), sm(9), float(P), None, ALU.is_ge))
                    step(V.scalar_tensor_tensor(out=sm(10), in0=sm(9), scalar=float(2 * P), in1=sm(10),
                                                op0=ALU.is_ge, op1=ALU.add))
                    step(V.scalar_tensor_tensor(out=sm(9), in0=sm(10), scalar=-float(P), in1=sm(9),
                                                op0=ALU.mult, op1=ALU.add))
                    step(V.tensor_tensor(wnd[:], c_("window").rearrange("p (o n) -> p o n", o=1)
                                         .to_broadcast((P, TT, WIN)), b3(sm(10), WIN), ALU.is_equal))
                    for t in range(TT):
                        V.tensor_scalar(pos_oh[:, c, t, :], c_("iota"), small[:, 9, t:t + 1], None, ALU.is_equal)
                    for v in range(2):
                        a = CONST_AT["value"][0] + 3 * (2 * c + v)
                        step(V.tensor_tensor(wv[:], wnd[:], b3(const[:, a:a + 3], WIN), ALU.mult))
                        for t in range(TT):
                            ins = V.tensor_tensor(vals[:, c, t, v], oh[:, c, t].rearrange("p (e o) -> p e o", o=1)
                                                  .to_broadcast((P, NE, WIN)),
                                                  wv[:, t:t + 1, :].to_broadcast((P, NE, WIN)), ALU.mult)
                        step(ins)
                V.memset(stat[:, 6:7], 0.0).then_inc(m["onehots"], 1)
                dve.wait_ge(m["idx_mm"], 1)
                V.tensor_scalar(slots_idx[:].rearrange("p v n -> p (v n)"), ps[:, 6, 0:2 * NE * WIN], -1.0, BIG,
                                ALU.mult, ALU.add).then_inc(m["idx_ready"], 1)

            def experts(l):
                m = M[l]
                dve.wait_ge(m["idx_ready"], 1)
                n = dve.alloc_register(f"dve_pass{l}")
                dve.reg_mov(n, 0)
                dve.wait_ge(m["turned"], 1)
                V.tensor_copy(xt[:, 4:8, :].rearrange("p k s -> p (k s)"), ps[:, 1, :]).then_inc(m["xt_b"], 1)
                with dve.Fori(0, NE) as e:
                    windows = dve.value_load(npass[0:1, bass.ds(e, 1)], min_val=1, max_val=WIN)
                    with dve.Fori(0, windows):
                        dve.reg_add(n, n, 1)
                        k_ = dve.snap(n, min_val=1, max_val=WIN * NE)
                        dve.wait_ge(m["up_mm"], k_)
                        dve.wait_ge(m["silu"], k_)
                        V.tensor_tensor(hid, sg, ps[:, 3, :], ALU.mult).then_inc(m["hid"], 1)
                        dve.wait_ge(m["turned"], k_ + 1)
                        V.tensor_copy(xt[:, 4:8, :].rearrange("p k s -> p (k s)"), ps[:, 1, :]).then_inc(m["xt_b"], 1)
                        dve.wait_ge(m["y_mm_b"], k_)
                        dve.wait_ge(m["scattered"], 16 * k_)
                        V.tensor_copy(ysb[:, C512:D], ps[:, 6, :]).then_inc(m["y_b"], 1)
                    dve.sem_inc(m["used"], 1)

            def combine(l):
                m = M[l]
                for t in range(TT):
                    dve.wait_ge(m["yback"], 16 * TT)
                    a, b = yall[:, t, 0, :], yall[:, t, 1, :]
                    step(V.tensor_scalar(a, a, wgt[:, 0, t:t + 1], None, ALU.mult))
                    step(V.scalar_tensor_tensor(out=a, in0=b, scalar=wgt[:, 1, t:t + 1], in1=a,
                                                op0=ALU.mult, op1=ALU.add))
                    step(V.tensor_tensor(a, a, gate_bc[:, 1, GROUP_OF[t], :], ALU.mult))
                    V.tensor_tensor(x[:, t, :], x[:, t, :], a, ALU.add).then_inc(m["x_done"], 1)

            dve.wait_ge(s_x, 32)
            dve.wait_ge(s_pos, 16)
            V.tensor_tensor(x[:, 1:3, :], x[:, 1:3, :], yall[:, 0], ALU.add).then_inc(x_ready, 1)
            dve.wait_ge(x_ready, 1)
            normalise("a0")
            dve.wait_ge(mod_col[0], 6)
            dve.wait_ge(s_small, 16 * 13)
            modulate("a0", 0, 0)
            for half in range(2):
                scan_half(half)
            residual(0)
            normalise("m0")
            modulate("m0", 0, 1)
            route(0)
            experts(0)
            combine(0)
            normalise("a1")
            dve.wait_ge(mod_col[1], 6)
            modulate("a1", 1, 0)
            residual(1)
            normalise("m1")
            modulate("m1", 1, 1)
            route(1)
            experts(1)
            combine(1)
            dve.wait_ge(M[1]["x_done"], TT)
            normalise("fin")
            dve.wait_ge(fin_in, 16)
            dve.wait_ge(n_xn, 3 * NORM["fin"] + TT)
            for t in range(TT):
                V.tensor_tensor(xn[:, t, :], xn[:, t, :], gate_bc[:, 0, 0, :], ALU.mult).then_inc(fin_done, 1)

        @block.gpsimd
        def _(pool):
            G_ = nc.gpsimd

            def experts(l):
                m = M[l]
                pool.wait_ge(out_x[l], 6)
                G_.memset(xg, 0.0).then_inc(m["zeroed"], 1)
                G_.memset(ysb, 0.0).then_inc(m["zeroed"], 1)
                pool.wait_ge(m["zeroed"], 2)
                G_.memset(si[:], int(BIG)).then_inc(m["si_set"], 1)
                pool.sem_inc(m["y_a"], 1)
                pool.sem_inc(m["y_b"], 1)
                pool.wait_ge(m["idx_ready"], 1)
                pool.wait_ge(m["hrow_out"], 16 * TT)
                n = pool.alloc_register(f"pool_pass{l}")
                pool.reg_mov(n, 0)

                def gather(k_):
                    pool.wait_ge(m["idx_ready"], 1)
                    pool.wait_ge(m["gi_set"], k_)
                    G_.indirect_dma_start(out=xg, out_offset=None, in_=scratch["hrow"][l],
                                          in_offset=bass.IndirectOffsetOnAxis(ap=gi[:, 0:1], axis=0),
                                          bounds_check=T - 1, oob_is_err=False).then_inc(m["gathered"], 16)

                def scatter(k_):
                    pool.wait_ge(m["idx_ready"], 1)
                    pool.wait_ge(m["y_a"], k_)
                    pool.wait_ge(m["y_b"], k_)
                    pool.wait_ge(m["si_set"], k_)
                    G_.indirect_dma_start(out=scratch["y"][l], out_offset=bass.IndirectOffsetOnAxis(ap=si[:, 0:1], axis=0),
                                          in_=ysb, in_offset=None, bounds_check=2 * T - 1, oob_is_err=False
                                          ).then_inc(m["scattered"], 16)

                with pool.Fori(0, NE) as e:
                    windows = pool.value_load(npass[0:1, bass.ds(e, 1)], min_val=1, max_val=WIN)
                    with pool.Fori(0, windows) as w:
                        pool.reg_add(n, n, 1)
                        k_ = pool.snap(n, min_val=1, max_val=WIN * NE)
                        G_.tensor_copy(gi[:], slots_idx[:, 0, bass.ds(e * WIN + w, 1)]).then_inc(m["gi_set"], 1)
                        gather(k_)
                        scatter(k_)
                        pool.wait_ge(m["scattered"], 16 * k_)
                        G_.tensor_copy(si[:], slots_idx[:, 1, bass.ds(e * WIN + w, 1)]).then_inc(m["si_set"], 1)
                        pool.wait_ge(m["turned"], k_)
                        pool.wait_ge(m["gathered"], 16 * k_)
                G_.tensor_copy(gi[:], slots_idx[:, 0, 0:1]).then_inc(m["gi_set"], 1)
                pool.reg_add(n, n, 1)
                k1 = pool.snap(n, min_val=NE + 1, max_val=WIN * NE + 1)
                gather(k1)
                scatter(k1)
                scattered = pool.snap(16 * k1, min_val=16, max_val=16 * (WIN * NE + 1))
                pool.wait_ge(m["used"], NE)
                pool.wait_ge(m["scattered"], scattered)
                pool.wait_ge(m["xt_a"], k1)
                pool.sem_inc(m["all_out"], 1)
                pool.wait_ge(m["all_out"], 1)
                for t in range(TT):
                    pool.dma_start(yall[:, t].rearrange("p c n -> p (c n)"),
                                   scratch["y"][l].rearrange("(t p c) n -> t p (c n)", p=P, c=2)[t]
                                   ).then_inc(m["yback"], 16)

            def rms(name):
                pool.wait_ge(n_sq, 3 * NORM[name] + TT)
                G_.tensor_scalar(stat[:, 0:3], stat[:, 0:3], 1.0 / D, EPS, ALU.mult, ALU.add).then_inc(n_ms, 1)
                pool.wait_ge(n_ms, 1 * NORM[name] + 1)
                G_.tensor_tensor(stat[:, 3:6], stat[:, 0:3], c_("minus_half")[:, 0:3], ALU.pow
                                 ).then_inc(n_rs, 1)

            pool.wait_ge(s_const, 16)
            rms("a0")
            for half in range(2):
                for t in range(TT):
                    n = 3 * half + t + 1
                    pool.wait_ge(o_sq, n)
                    G_.tensor_scalar(rsq[:, t, :], ssq[:, t, :], 1.0 / P, EPS, ALU.mult, ALU.add).then_inc(o_ms, 1)
                    pool.wait_ge(o_ms, n)
                    G_.tensor_tensor(rsq[:, t, :], rsq[:, t, :], c_("minus_half"), ALU.pow).then_inc(o_rs, 1)
                for d in range(2):
                    pool.wait_ge(s_ready, 4 * half + d + 1)
                    pool.dma_start(io["o_state"][0, 0, d, HH * half:HH * (half + 1)].rearrange("h k v -> k h v"),
                                   s_out[:, d]).then_inc(st_written, 16)
            rms("m0")
            experts(0)
            rms("a1")
            rms("m1")
            experts(1)
            rms("fin")
            pool.dma_start(gate_bc[:, 0, 0, :], io["final_norm_g"].rearrange("(o n) -> o n", o=1)
                           .to_broadcast((P, D))).then_inc(fin_in, 16)
            for t in range(TT):
                pool.wait_ge(fin_done, t + 1)
                dst = (io["o_prompt"].rearrange("b t n -> (b t) n") if t == 0
                       else io["o_sample"].rearrange("b (t p) n -> t (b p) n", p=P)[t - 1])
                pool.dma_start(dst, xn[:, t, :]).then_inc(y_out, 16)


def shape_constants():
    f = np.float32
    const = np.zeros((P, CONST_W), f)

    def put(name, a):
        i, j = CONST_AT[name]
        const[:a.shape[0], i:j] = a

    r = np.arange(P)
    put("ident", np.eye(P))
    put("upper", (r[:, None] < r[None, :]))
    put("ones", np.ones((P, P)))
    put("iota", np.tile(r, (P, 1)))
    sel = np.zeros((3, 2, P))
    sel[0, 0] = sel[1, 1] = 1
    sel[2] = 1
    put("sel", sel.reshape(3, -1))
    put("sel2", np.array([[1, 0], [0, 1], [1, 1]]))
    put("rev_group", np.tile(4 - np.arange(4), (P, 1)))
    put("rev_expert", np.tile(16 - np.arange(16), (P, 1)))
    put("window", np.tile(np.arange(3), (P, 1)))
    tok = r[:, None] + P * np.arange(TT)[None, :]
    put("value", np.concatenate([BIG - tok, BIG - 2 * tok, BIG - tok, BIG - 2 * tok - 1], 1))
    put("minus_half", np.full((P, 4), -0.5))
    s, t = np.arange(P)[:, None] % SMALL, np.arange(SMALL)[None, :]
    masks = np.zeros((P, NMASK, SMALL), np.int32)
    for i, h in enumerate([1, 2, 4, 8, 16]):
        same = s // (2 * h) == t // (2 * h)
        masks[:, 2 * i] = same & (s // h % 2 == 0) & (t // h % 2 == 1)
        masks[:, 2 * i + 1] = same & (s // h % 2 == 1) & (t // h % 2 == 0)
    masks[:, 10] = s == t
    n, width, quarter = 2 * P, 64, D // 4
    tt = np.arange(n)
    omega = (1.0 / (f(10000.0) ** (np.arange(quarter, dtype=f) / f(quarter)))).astype(f)
    ar = (tt // width).astype(f)[:, None] * omega[None]
    ac = (tt % width).astype(f)[:, None] * omega[None]
    pos = np.concatenate([np.sin(ar), np.cos(ar), np.sin(ac), np.cos(ac)], -1).astype(f)
    pos = np.ascontiguousarray(pos.reshape(2, P, D).transpose(1, 0, 2))

    def dft(m):
        a = 2 * np.pi * (np.outer(np.arange(m), np.arange(m)) % m) / m
        return np.cos(a) / np.sqrt(m), np.sin(a) / np.sqrt(m)

    cc, sc = dft(256)
    dft_c = np.concatenate([cc, sc], 1).reshape(2, P, 512).transpose(1, 0, 2)
    c1, s1 = dft(P)
    dft_ctx = np.stack([c1, -s1], 1)
    dft_lat = np.stack([cc, -sc], 1).reshape(2, P, 2, 256).transpose(1, 0, 2, 3)
    out = dict(const=const, masks=masks, pos=pos, dft_c=dft_c, dft_ctx=dft_ctx, dft_lat=dft_lat)
    return {k: np.ascontiguousarray(v, v.dtype if v.dtype == np.int32 else f) for k, v in out.items()}


_INS = ["x_prompt", "x_sample", "state_hgrn", "c", "c_ctx", "w_mod", "b_mod", "norm1_g", "norm2_g", "hgrn_w_in",
        "hgrn_norm_g", "hgrn_w_out", "fourier_w_out", "router_group_w", "router_group_b", "router_expert_w",
        "router_expert_b", "moe_w_gate", "moe_w_up", "moe_w_down", "final_norm_g"]


def kernel(**inputs):
    import numpy as _np
    import concourse.bacc as _bacc
    from concourse import mybir as _mybir
    from concourse.bass_utils import run_bass_kernel_spmd as _run

    nc = _bacc.Bacc("TRN2", target_bir_lowering=False, num_devices=1)
    arrays = {n: _np.ascontiguousarray(inputs[n]) for n in _INS}
    arrays.update(shape_constants())
    io = {n: nc.dram_tensor(f"in_{n}", a.shape, _mybir.dt.from_np(a.dtype), kind="ExternalInput").ap()
          for n, a in arrays.items()}
    f32 = _mybir.dt.float32
    for n, shape in [("o_prompt", (1, 128, 1024)), ("o_sample", (1, 256, 1024)), ("o_state", (1, 1, 2, 8, 128, 128))]:
        io[n] = nc.dram_tensor(n, shape, f32, kind="ExternalOutput").ap()
    scratch = {"hrow": [nc.dram_tensor(f"hrow{l}", (T, D), f32, kind="Internal").ap() for l in range(2)],
               "y": [nc.dram_tensor(f"yrows{l}", (2 * T, D), f32, kind="Internal").ap() for l in range(2)]}
    program(nc, io, scratch)
    r = _run(nc, [{f"in_{n}": a for n, a in arrays.items()}], core_ids=[0]).results[0]
    return r["o_prompt"], r["o_sample"], r["o_state"]
```

```python
from contextlib import ExitStack

import numpy as np
import concourse.bass as bass
from concourse import mybir

F32 = mybir.dt.float32
I32 = mybir.dt.int32
U32 = mybir.dt.uint32
ACT = mybir.ActivationFunctionType
ALU = mybir.AluOpType
AX = mybir.AxisListType

P = 128
D = 1024
KD = D // P
TT = 3
T = TT * P
NH = 8
HH = NH // 2
C512 = 512
NE = 16
NG = 4
NL = 20
F = 512
KF = F // P
WIN = 3
EPS = 1e-6
BIG = 4096.0
NEG = 1e30
RING = 6
UNIT = 4096
SIZES = [1, 2, 4, 8, 16, 32, 64]
SMALL = 32
GROUP_OF = [0, 1, 1]


def const_columns():
    at, n = {}, 0
    for name, w in [("ident", 128), ("upper", 128), ("ones", 128), ("iota", 128), ("rev_group", 4), ("rev_expert", 16), ("window", 3), ("value", 12),
                    ("minus_half", 4), ("pick", 4)]:
        at[name] = (n, n + w)
        n += w
    return at, n


CONST_AT, CONST_W = const_columns()
NMASK = 11


def program(nc, io, scratch):
    with ExitStack() as ctx:
        def sb(name, shape, dt=F32):
            return ctx.enter_context(nc.sbuf_tensor(name, shape, dt))

        def sem(name):
            return ctx.enter_context(nc.semaphore(name))

        ring = sb("ring", [P, RING, UNIT])
        x = sb("x", [P, TT, D])
        hT = sb("hT", [P, KD, T])
        gate_bc = sb("gate_bc", [P, 2, 2, D])
        WORK = 15800
        work = sb("work", [P, WORK])
        const = sb("const", [P, CONST_W])
        masks = sb("masks", [P, NMASK, SMALL], I32)
        cond = sb("cond", [P, 2, KD])
        scond = sb("scond", [P, 2, KD])
        gnorm = sb("gnorm", [P, 4, KD])
        colmod = sb("colmod", [P, 2, 4, 2, KD])
        colA = sb("colA", [P, KD, 2])
        stat = sb("stat", [P, 8])
        wroute = sb("wroute", [P, 2, KD, NL])
        broute = sb("broute", [P, 2, NL])
        ps = ctx.enter_context(nc.psum_tensor("ps", [P, 8, 512], F32))

        def c_(name):
            a, b = CONST_AT[name]
            return const[:, a:b]

        ident = c_("ident")

        class Area:
            def __init__(self, t, start=0):
                self.t, self.n = t, start

            def take(self, n):
                a = self.t[:, self.n:self.n + n]
                self.n += n
                return a

        flat_ring = ring[:].rearrange("p s n -> p (s n)")
        mod_row = [work[0:2, WORK - 2 * D:WORK - 2 * D + C512]] * 4
        mod_b = [work[0:2, WORK - D:WORK - D + C512]] * 4
        xn = work[:, 0:TT * D].rearrange("p (t n) -> p t n", t=TT)
        hg = Area(work)
        oT = hg.take(KD * T).rearrange("p (k t) -> p k t", k=KD)
        qT = hg.take(HH * T)
        vrow = hg.take(TT * C512).rearrange("p (t n) -> p t n", t=TT)
        gsil = hg.take(TT * C512).rearrange("p (t n) -> p t n", t=TT)
        on = hg.take(TT * C512).rearrange("p (t n) -> p t n", t=TT)
        score = hg.take(TT * HH * P).rearrange("p (t h s) -> p t h s", t=TT, h=HH)
        compact = hg.take(TT * HH * SMALL).rearrange("p (a s) -> p a s", s=SMALL)
        kT = hg.take(2 * HH * P).rearrange("p (b h s) -> p b h s", b=2, h=HH)
        s0 = hg.take(2 * HH * P).rearrange("p (d h v) -> p d h v", d=2, h=HH)
        s1 = hg.take(2 * HH * P).rearrange("p (d h v) -> p d h v", d=2, h=HH)
        s_out = hg.take(2 * HH * P).rearrange("p (d h v) -> p d h v", d=2, h=HH)
        hnorm = hg.take(C512)
        ssq = hg.take(TT * HH).rearrange("p (t h) -> p t h", t=TT)
        rsq = hg.take(TT * HH).rearrange("p (t h) -> p t h", t=TT)
        tail = Area(flat_ring, 3 * UNIT)
        qd = [tail.take(HH * T) for _ in range(2)]
        G = [{h: tail.take(HH * T // h) for h in SIZES[1:] + [128]} for _ in range(2)]
        assert tail.n >= 4 * UNIT
        kd = [tail.take(HH * T) for _ in range(2)]
        for d in range(2):
            G[d][1] = tail.take(HH * T)
        assert hg.n <= WORK and tail.n <= RING * UNIT
        o0 = 3 * D + HH * T + 2 * TT * C512
        part_hg = work[:, o0:o0 + 4 * C512].rearrange("p (b g n) -> p b g n", b=2, g=2)
        mod_row += [work[0:2, o0 + 4 * C512:o0 + 5 * C512]] * 16
        mod_b += [work[0:2, o0 + 5 * C512:o0 + 6 * C512]] * 16
        fo = Area(work, TT * D)
        U = fo.take(TT * 4 * C512).rearrange("p (t g n) -> p t g n", t=TT, g=4)
        dft_c = fo.take(2 * C512).rearrange("p (k n) -> p k n", k=2)
        dft_ctx = fo.take(2 * P).rearrange("p (c n) -> p c n", c=2)
        dft_lat = fo.take(4 * 2 * P).rearrange("p (t c n) -> p t c n", t=2, c=2)
        zT = work[:, 0:TT * D].rearrange("p (k t) -> p k t", k=KD)
        part_fo = fo.take(4 * C512).rearrange("p (b g n) -> p b g n", b=2, g=2)
        assert fo.n <= WORK - 2 * D
        mod_row += [work[0:2, WORK - 2 * D:WORK - 2 * D + C512]] * 4
        mod_b += [work[0:2, WORK - D:WORK - D + C512]] * 4
        me = Area(work)
        hrow = me.take(TT * D).rearrange("p (t n) -> p t n", t=TT)
        yall = work[:, 0:2 * TT * D].rearrange("p (t c n) -> p t c n", t=TT, c=2)
        me.n = 2 * TT * D
        xg = me.take(D)
        xt = me.take(D).rearrange("p (k s) -> p k s", k=KD)
        sg = me.take(F)
        hid = me.take(F)
        hidT = me.take(F).rearrange("p (k s) -> p k s", k=KF)
        ysb = me.take(D)
        pos_oh = me.take(2 * TT * P).rearrange("p (c t s) -> p c t s", c=2, t=TT)
        vals = me.take(2 * TT * 2 * NE * WIN).rearrange("p (c t v e w) -> p c t v e w", c=2, t=TT, v=2, e=NE)
        lg = me.take(TT * NL).rearrange("p (t n) -> p t n", t=TT)
        r4 = me.take(TT * NG).rearrange("p (t n) -> p t n", t=TT)
        ohg = me.take(TT * NG).rearrange("p (t n) -> p t n", t=TT)
        el = me.take(TT * NE).rearrange("p (t n) -> p t n", t=TT)
        e16 = me.take(TT * NE).rearrange("p (t n) -> p t n", t=TT)
        oh = me.take(2 * TT * NE).rearrange("p (c t n) -> p c t n", c=2, t=TT)
        both = me.take(TT * NE).rearrange("p (t n) -> p t n", t=TT)
        pos = me.take(TT * NE).rearrange("p (t n) -> p t n", t=TT)
        small = me.take(16 * TT).rearrange("p (n t) -> p n t", t=TT)
        wnd = me.take(TT * WIN).rearrange("p (t w) -> p t w", t=TT)
        wv = me.take(TT * WIN).rearrange("p (t w) -> p t w", t=TT)
        assert me.n <= WORK - 2 * D, me.n
        slots_idx = sb("slots_idx", [P, 2, NE * WIN + 1], U32)
        gi = sb("gi", [P, 1], U32)
        si = sb("si", [P, 1], U32)
        npass = sb("npass", [P, NE], I32)
        npass_f = sb("npass_f", [P, NE])
        wgt = sb("wgt", [P, 2, TT])

        landed = [sem(f"landed{s}") for s in range(RING)]
        s_const, s_x, s_cond, s_small = sem("const_in"), sem("x_in"), sem("cond_in"), sem("small_in")
        s_pos = sem("pos_in")
        scond_ready = sem("scond_ready")
        x_ready = sem("x_ready")
        mod_bias, mod_mm, mod_evac, mod_row_out = (sem("mod_bias_in"), sem("mod_mm"), sem("mod_evac"),
                                                   sem("mod_row_out"))
        gemv_step, gemv_done = sem("gemv_step"), sem("gemv_done")
        mod_in = [sem(f"mod_in{i}") for i in range(4)]
        NORM = {"a0": 0, "m0": 1, "a1": 2, "m1": 3, "fin": 4}
        n_sq = sem("square")
        n_rs = sem("rms")
        n_ms = sem("mean_square")
        o_ms, o_rs = sem("o_mean_square"), sem("o_rms")
        n_xn = sem("xn")
        n_tp = sem("xn_turned")
        n_hA = sem("hT_act")
        n_hV = sem("hT_dve")
        n_col = sem("col")
        proj_mm, proj_evac = sem("proj_mm"), sem("proj_evac")
        hg_in = sem("hgrn_in")
        hg_unit = sem("hgrn_unit_used")
        lvl_upd = [sem("level_updated_f"), sem("level_updated_b")]
        lvl_mm = [sem("level_scored_f"), sem("level_scored_b")]
        sd_copied = sem("compact_copied")
        score_ready, kT_mm, kT_ready, u_mm, s_ready = (sem("score_ready"), sem("kT_turned"), sem("kT_ready"),
                                                       sem("u_mm"), sem("state_ready"))
        off_copied = sem("score_off_copied")
        o_mm, o_sq, o_ready, o_tp, oT_ready = (sem("o_mm"), sem("o_square"), sem("o_ready"), sem("o_turned"),
                                               sem("oT_ready"))
        st_written = sem("state_written")
        gsil_ready = sem("gsil_ready")
        out_mm = [sem(f"out_mm{l}") for l in range(2)]
        out_x = [sem(f"out_x{l}") for l in range(2)]
        four_in, u_done4, u_evac4, z_done, z_evac = (sem("dft_in"), sem("dftc_mm"), sem("dftc_evac"),
                                                     sem("dftt_mm"), sem("dftt_evac"))
        M = []
        for l in range(2):
            M.append({n: sem(f"moe{l}_{n}") for n in [
                "logits", "chosen", "pos_mm", "onehots", "idx_mm", "idx_ready", "back_mm", "back_act", "back_dve",
                "hrow_out", "zeroed", "si_set", "gi_set", "gathered", "turned", "xt_a", "xt_b", "gate_mm", "up_mm",
                "silu", "hid", "hid_turned", "hidT", "y_mm_a", "y_mm_b", "y_a", "y_b", "scattered", "used", "yback", "all_out", "x_done",
                "exp_in", "exp_out"]})
        chain = sem("dve_chain")
        y_out = sem("y_out")
        fin_in = sem("final_gain_in")
        fin_done = sem("final_done")

        w_mod = io["w_mod"].rearrange("l (p k) n -> l p k n", k=KD)
        w_in = io["hgrn_w_in"].rearrange("l (p k) n -> l p k n", k=KD)
        w_o = [io["hgrn_w_out"].rearrange("l (k p) n -> l p k n", p=P),
               io["fourier_w_out"].rearrange("l (k p) n -> l p k n", p=P)]
        w_g = io["moe_w_gate"].rearrange("l e (p k) n -> l e p (k n)", k=KD)
        w_u = io["moe_w_up"].rearrange("l e (p k) n -> l e p (k n)", k=KD)
        w_d = io["moe_w_down"].rearrange("l e (p k) n -> l e p (k n)", k=KF)

        uses = [0] * RING
        plan = {}

        def place(phase, u, s):
            uses[s] += 1
            plan[(phase, u)] = (s, 16 * uses[s])

        def mod_unit(U):
            return (0, U) if U < 12 else (1, U - 12)

        def mod_slot(U):
            return [3, 4, 5, 2][U] if U < 4 else ([2, 3][U % 2] if 12 <= U < 20 else [3, 2][U % 2])

        STREAM = ([("mod", U) for U in range(4)] + [("hgrn", 0), ("hgrn", 1)]
                  + [("mod", 4), ("mod", 5), ("mod", 6), ("mod", 7), ("hgrn", 2), ("mod", 8), ("mod", 9), ("hgrn", 3),
                     ("mod", 10), ("mod", 11), ("hgrn", 4), ("hgrn", 5)]
                  + [("mod", 12), ("hgrn", 6), ("mod", 13), ("mod", 14), ("hgrn", 7), ("mod", 15), ("mod", 16),
                     ("hgrn", 8), ("mod", 17), ("mod", 18), ("hgrn", 9), ("mod", 19), ("hgrn", 10), ("hgrn", 11)])
        for phase, u in STREAM:
            place(phase, u, mod_slot(u) if phase == "mod" else u % 2)
        MOE_SLOTS = [[3, 4, 5, 2, 0, 1], [4, 5, 2, 3, 0, 1]]
        moe_before = [list(uses)]
        for u in range(3 * NE):
            place("moe0", u, MOE_SLOTS[0][u % 6])
        for phase, u, s in [("mod", 20, 3), ("four", 0, 0), ("four", 1, 1), ("mod", 21, 2), ("mod", 22, 3),
                            ("mod", 23, 2)]:
            place(phase, u, s)
        moe_before.append(list(uses))

        def slot3(s):
            return ring[:, s, :].rearrange("p (k n) -> p k n", k=KD)

        def slot_d(s):
            return ring[:, s, :].rearrange("p (k n) -> p k n", k=KF)

        def in_cols(u):
            half, kind = divmod(u, 5)
            return kind * D + half * C512

        block = ctx.enter_context(nc.Block())

        @block.sync
        def _(sp):
            def mod_load(U):
                l, u = mod_unit(U)
                s, _ = plan[("mod", U)]
                sp.dma_start(slot3(s), w_mod[l, :, :, u * C512:(u + 1) * C512]).then_inc(landed[s], 16)

            def moe_units(l, first_wait):
                slots = MOE_SLOTS[l]
                for u in range(6):
                    first_wait(u)
                    w = [w_g, w_u, w_d][u % 3]
                    sp.dma_start(ring[:, slots[u], :], w[l, u // 3]).then_inc(landed[slots[u]], 16)
                with sp.Fori(1, NE // 2) as i:
                    for par in range(2):
                        sp.wait_ge(M[l]["used"], 2 * i + (par - 1))
                        for j, w in enumerate([w_g, w_u, w_d]):
                            s = slots[3 * par + j]
                            sp.dma_start(ring[:, s, :], w[l, 2 * i + par]).then_inc(landed[s], 16)

            sp.dma_start(cond[:, 0, :], io["c_ctx"].rearrange("(p k) -> p k", k=KD)).then_inc(s_cond, 16)
            sp.dma_start(cond[:, 1, :], io["c"].rearrange("b (p k) -> (b p) k", k=KD)).then_inc(s_cond, 16)
            sp.dma_start(const[:], io["const"]).then_inc(s_const, 16)

            for phase, u in STREAM:
                if phase == "hgrn":
                    s, _ = plan[("hgrn", u)]
                    if u >= 2:
                        sp.wait_ge(hg_unit, u - 1)
                    src = (w_in[0, :, :, in_cols(u):in_cols(u) + C512] if u < 10
                           else w_o[0][0, :, :, (u - 10) * C512:(u - 9) * C512])
                    sp.dma_start(slot3(s), src).then_inc(landed[s], 16)
                    continue
                if u == 4:
                    sp.wait_ge(mod_mm, 1)
                elif u == 5:
                    sp.wait_ge(mod_mm, 4)
                elif u > 5:
                    if u == 13:
                        sp.wait_ge(o_mm, 3)
                    sp.wait_ge(gemv_done, u - 4 if u == 12 else u - 5)
                mod_load(u)
                if u == 1:
                    sp.dma_start(x[:, 0, :], io["x_prompt"].rearrange("b t n -> (b t) n")).then_inc(s_x, 16)
                    sp.dma_start(x[:, 1:3, :], io["x_sample"].rearrange("b (t p) n -> (b p) t n", p=P)
                                 ).then_inc(s_x, 16)
                    sp.dma_start(yall[:, 0], io["pos"]).then_inc(s_pos, 16)

            def moe0_wait(u):
                s = MOE_SLOTS[0][u]
                if s >= 3:
                    sp.wait_ge(o_mm, 6)
                if s in (2, 3):
                    sp.wait_ge(gemv_done, 16)
                if s < 2:
                    sp.wait_ge(hg_unit, 11 + s)
            moe_units(0, moe0_wait)

            sp.wait_ge(M[0]["used"], NE - 1)
            sp.wait_ge(gemv_done, 15)
            mod_load(20)
            sp.wait_ge(M[0]["used"], NE)
            sp.wait_ge(M[0]["yback"], 16 * TT)
            for u in range(2):
                s, _ = plan[("four", u)]
                sp.dma_start(slot3(s), w_o[1][0, :, :, u * C512:(u + 1) * C512]).then_inc(landed[s], 16)
            mod_load(21)
            for U in (22, 23):
                sp.wait_ge(gemv_done, U - 5)
                mod_load(U)

            def moe1_wait(u):
                s = MOE_SLOTS[1][u]
                if s in (2, 3):
                    sp.wait_ge(gemv_done, 20)
                if s < 2:
                    sp.wait_ge(out_mm[1], 3 * s + 3)
            moe_units(1, moe1_wait)

            sp.wait_ge(y_out, 16 * TT)
            sp.wait_ge(st_written, 16 * 4)

        @block.tensor
        def _(pe):
            mm = pe.matmul

            def modulation():
                pe.wait_ge(scond_ready, 1)
                for U in range(4):
                    s, val = plan[("mod", U)]
                    pe.wait_ge(landed[s], val)
                    if U >= 2:
                        pe.wait_ge(mod_evac, U - 1)
                    for k in range(KD):
                        last = mm(ps[0:2, U % 2, :], scond[:, :, k], slot3(s)[:, k, :],
                                  start=(k == 0), stop=(k == KD - 1))
                    last.then_inc(mod_mm, 1)
                pe.wait_ge(s_const, 16)
                pe.wait_ge(mod_evac, 4)

            def mod_sum(U, bank):
                pe.wait_ge(gemv_done, U - 3)
                if U >= 6:
                    pe.wait_ge(mod_evac, U - 1)
                part = part_hg if U < 20 else part_fo
                for g in range(2):
                    last = mm(ps[0:2, bank, :], c_("pick")[:, 2 * g:2 * g + 2], part[:, U % 2, g, :],
                              start=(g == 0), stop=(g == 1))
                last.then_inc(mod_mm, 1)

            def turn_norm(name, strided):
                for k in range(KD):
                    if k == 0:
                        pe.wait_ge(n_xn, 3 * NORM[name] + TT)
                    if k >= 4:
                        pe.wait_ge(n_hA if k % 2 == 0 else n_hV, 4 * NORM[name] + (k - 4) // 2 + 1)
                    for t in range(TT):
                        src = xn[:, t, k:D:KD] if strided else xn[:, t, k * P:(k + 1) * P]
                        last = pe.transpose(ps[:, k % 4, t * P:(t + 1) * P], src, ident)
                    last.then_inc(n_tp, 1)

            def wait_hT(name):
                pe.wait_ge(n_hA, 4 * NORM[name] + KD // 2)
                pe.wait_ge(n_hV, 4 * NORM[name] + KD // 2)

            def project_half(half):
                n = 18 * half
                for kind in range(5):
                    s, val = plan[("hgrn", 5 * half + kind)]
                    pe.wait_ge(landed[s], val)
                    W = slot3(s)
                    for c in range(4 if kind < 3 else TT):
                        if n % 18 >= 4:
                            pe.wait_ge(proj_evac, n - 3)
                        bank = ps[:, n % 18 % 4, :]
                        for k in range(KD):
                            if kind < 3:
                                last = mm(bank[:, 0:T], W[:, k, c * P:(c + 1) * P], hT[:, k, :],
                                          start=(k == 0), stop=(k == KD - 1))
                            else:
                                last = mm(bank, hT[:, k, c * P:(c + 1) * P], W[:, k, :],
                                          start=(k == 0), stop=(k == KD - 1))
                        last.then_inc(proj_mm, 1)
                        n += 1
                        c18 = n - 18 * half
                        if c18 >= 4 and c18 % 2 == 0:
                            U = 4 + 8 * half + (c18 - 4) // 2
                            if U == 12:
                                pe.wait_ge(oT_ready, 3)
                            mod_sum(U, 6 + U % 2)

            def scan_half(half):
                lv = half * len(SIZES)
                n = half * 11

                def compact_scores(d, i, lhs, rhs, more=None):
                    nonlocal n
                    if n >= half * 11 + 2:
                        pe.wait_ge(sd_copied, n - 1)
                    bank = ps[:, 4 + n % 2, :]
                    for t in range(TT):
                        for h in range(HH):
                            o = (t * HH + h) * SMALL
                            for g in range(4):
                                a = h * T + t * P + g * SMALL
                                pairs = [(lhs, rhs)] + ([more] if more else [])
                                for j, (L, R) in enumerate(pairs):
                                    last = mm(bank[g * SMALL:(g + 1) * SMALL, o:o + SMALL], L[:, a:a + SMALL],
                                              R[:, a:a + SMALL], start=(j == 0), stop=(j == len(pairs) - 1))
                    n += 1
                    return last

                pe.wait_ge(proj_evac, 18 * half + 12)
                compact_scores(0, 0, kd[0], qT, (kd[1], qT)).then_inc(lvl_mm[0], 1)
                for i, h in enumerate(SIZES):
                    for d in range(2):
                        pe.wait_ge(lvl_upd[d], lv + half + i + 1)
                        if h < SMALL:
                            last = compact_scores(d, i, kd[d], qd[d])
                        else:
                            if h == SMALL and d == 0:
                                pe.wait_ge(proj_evac, 18 * half + 18)
                            for t in range(TT):
                                for hh in range(HH):
                                    for b in range(0, P, 2 * h):
                                        lo, hi = b, b + h
                                        sk, tq = (lo, hi) if d == 0 else (hi, lo)
                                        a = hh * T + t * P
                                        last = mm(ps[sk:sk + h, t, hh * P + tq:hh * P + tq + h],
                                                  kd[d][:, a + sk:a + sk + h], qd[d][:, a + tq:a + tq + h],
                                                  start=True, stop=True)
                        last.then_inc(lvl_mm[d], 1)
                pe.wait_ge(lvl_upd[0], lv + half + 8)
                pe.wait_ge(lvl_upd[1], lv + half + 8)
                UNITS = [(0, 0), (0, 1), (1, 0), (2, 1)]

                def turn_keys(j):
                    t, d = UNITS[j]
                    if 4 * half + j >= 2:
                        pe.wait_ge(kT_ready, 4 * half + j - 1)
                        pe.wait_ge(u_mm, 4 * half + j - 1)
                    for h in range(HH):
                        a = h * T + t * P
                        last = pe.transpose(ps[:, [3, 7][j % 2], h * P:(h + 1) * P], kd[d][:, a:a + P], ident)
                    last.then_inc(kT_mm, 1)

                def increment(j):
                    t, d = UNITS[j]
                    pe.wait_ge(kT_ready, 4 * half + j + 1)
                    if j == 0:
                        pe.wait_ge(sd_copied, 11 * half + 11)
                    if j >= 2:
                        pe.wait_ge(s_ready, 4 * half + j - 1)
                    for h in range(HH):
                        last = mm(ps[:, 4 + j % 2, h * P:(h + 1) * P], kT[:, j % 2, h, :],
                                  vrow[:, t, h * P:(h + 1) * P], start=True, stop=True)
                    last.then_inc(u_mm, 1)

                turn_keys(0)
                turn_keys(1)
                for j in range(4):
                    increment(j)
                    if j + 2 < 4:
                        turn_keys(j + 2)

                OB = [6, 7, 3]
                pe.wait_ge(score_ready, 4 * (half + 1))
                pe.wait_ge(s_ready, 4 * half + 4)
                pe.wait_ge(kT_ready, 4 * half + 4)
                for t in range(TT):
                    for h in range(HH):
                        a = h * T + t * P
                        out = ps[:, OB[t], h * P:(h + 1) * P]
                        last = mm(out, score[:, t, h, :], vrow[:, t, h * P:(h + 1) * P], start=True, stop=(t == 0))
                        if t:
                            st_f = s0[:, 0, h, :] if t == 1 else s1[:, 0, h, :]
                            st_b = s1[:, 1, h, :] if t == 1 else s0[:, 1, h, :]
                            mm(out, qd[0][:, a:a + P], st_f, start=False, stop=False)
                            last = mm(out, qd[1][:, a:a + P], st_b, start=False, stop=True)
                    last.then_inc(o_mm, 1)
                for t in range(TT):
                    pe.wait_ge(o_ready, 3 * half + t + 1)
                    for h in range(HH):
                        last = pe.transpose(ps[:, 4 + t % 2 if t < 2 else 6, h * P:(h + 1) * P],
                                            on[:, t, h * P:(h + 1) * P], ident)
                    last.then_inc(o_tp, 1)

            def out_project(l, src, phase, u0):
                for j in range(2):
                    s, val = plan[(phase, u0 + j)]
                    pe.wait_ge(landed[s], val)
                    for t in range(TT):
                        n = 3 * j + t
                        if n >= 4:
                            pe.wait_ge(out_x[l], n - 3)
                        for k in range(KD):
                            last = mm(ps[:, n % 4, :], src[:, k, t * P:(t + 1) * P], slot3(s)[:, k, :],
                                      start=(k == 0), stop=(k == KD - 1))
                        last.then_inc(out_mm[l], 1)

            def fourier():
                pe.wait_ge(four_in, 48)
                for t in range(TT):
                    for g in range(4):
                        n = 4 * t + g
                        if n >= 4:
                            pe.wait_ge(u_evac4, n - 3)
                        for k in range(2):
                            last = mm(ps[:, 4 + n % 4, :], hT[:, 2 * g + k, t * P:(t + 1) * P], dft_c[:, k, :],
                                      start=(k == 0), stop=(k == 1))
                        last.then_inc(u_done4, 1)
                pe.wait_ge(u_evac4, 12)
                mod_sum(20, 4)
                mod_sum(21, 5)
                for k in range(KD):
                    if k == 4:
                        mod_sum(22, 6)
                    if k >= 4:
                        pe.wait_ge(z_evac, k - 3)
                    g, o = k // 2, (k % 2) * P
                    bank = ps[:, k % 4, :]
                    for c in range(2):
                        mm(bank[:, 0:P], U[:, 0, g, c * 256 + o:c * 256 + o + P], dft_ctx[:, c, :],
                           start=(c == 0), stop=(c == 1))
                    for t in range(2):
                        for c in range(2):
                            last = mm(bank[:, P:T], U[:, 1 + t, g, c * 256 + o:c * 256 + o + P], dft_lat[:, t, c, :],
                                      start=(t + c == 0), stop=(t + c == 2))
                    last.then_inc(z_done, 1)
                mod_sum(23, 7)

            def route(l):
                m = M[l]
                for t in range(TT):
                    for k in range(KD):
                        last = mm(ps[:, 4, t * 32:t * 32 + NL], hT[:, k, t * P:(t + 1) * P], wroute[:, l, k, :],
                                  start=(k == 0), stop=(k == KD - 1))
                last.then_inc(m["logits"], 1)
                for t in range(TT):
                    for j in range(2):
                        n = 2 * t + j
                        if n >= 4:
                            pe.wait_ge(m["back_act"] if j == 0 else m["back_dve"], t - 1)
                        for k in range(4):
                            last = pe.transpose(ps[:, n % 4, k * P:(k + 1) * P],
                                                hT[:, 4 * j + k, t * P:(t + 1) * P], ident)
                        last.then_inc(m["back_mm"], 1)
                pe.wait_ge(m["chosen"], 1)
                for t in range(TT):
                    mm(ps[:, 5, t * NE:(t + 1) * NE], c_("upper"), both[:, t, :], start=True, stop=(t == 0))
                    for b in range(t):
                        mm(ps[:, 5, t * NE:(t + 1) * NE], c_("ones"), both[:, b, :], start=False, stop=(b == t - 1))
                for t in range(TT):
                    last = mm(ps[:, 5, TT * NE:(TT + 1) * NE], c_("ones"), both[:, t, :],
                              start=(t == 0), stop=(t == TT - 1))
                last.then_inc(m["pos_mm"], 1)
                pe.wait_ge(m["onehots"], 1)
                for c in range(2):
                    for t in range(TT):
                        last = mm(ps[:, 6, 0:2 * NE * WIN], pos_oh[:, c, t, :],
                                  vals[:, c, t].rearrange("p v e w -> p (v e w)"),
                                  start=(c + t == 0), stop=(c == 1 and t == TT - 1))
                last.then_inc(m["idx_mm"], 1)

            def turn_tokens(m):
                for k in range(KD):
                    last = pe.transpose(ps[:, k // 4, (k % 4) * P:(k % 4 + 1) * P], xg[:, k * P:(k + 1) * P], ident)
                last.then_inc(m["turned"], 1)

            def experts(l):
                m = M[l]
                pe.wait_ge(m["idx_ready"], 1)
                n = pe.alloc_register(f"pe_pass{l}")
                pe.reg_mov(n, 0)
                pe.wait_ge(m["gathered"], 16)
                turn_tokens(m)
                with pe.Fori(0, NE // 2) as i:
                    for par in range(2):
                        S = [MOE_SLOTS[l][3 * par + j] for j in range(3)]
                        windows = pe.value_load(npass[0:1, bass.ds(2 * i + par, 1)], min_val=1, max_val=WIN)
                        with pe.Fori(0, windows):
                            pe.reg_add(n, n, 1)
                            k_ = pe.snap(n, min_val=1, max_val=WIN * NE)
                            for s in S:
                                pe.wait_ge(landed[s], 16 * i + 16 * (moe_before[l][s] + 1))
                            pe.wait_ge(m["xt_a"], k_)
                            pe.wait_ge(m["xt_b"], k_)
                            for j, name in ((0, "gate_mm"), (1, "up_mm")):
                                for k in range(KD):
                                    last = mm(ps[:, 2 + j, :], xt[:, k, :], slot3(S[j])[:, k, :],
                                              start=(k == 0), stop=(k == KD - 1))
                                last.then_inc(m[name], 1)
                            pe.wait_ge(m["gathered"], 16 * k_ + 16)
                            turn_tokens(m)
                            pe.wait_ge(m["hid"], k_)
                            for k in range(KF):
                                last = pe.transpose(ps[:, 4, k * P:(k + 1) * P], hid[:, k:F:KF], ident)
                            last.then_inc(m["hid_turned"], 1)
                            pe.wait_ge(m["hidT"], k_)
                            pe.wait_ge(m["y_a"], k_ + 1)
                            pe.wait_ge(m["y_b"], k_ + 1)
                            for j in range(2):
                                for k in range(KF):
                                    last = mm(ps[:, 5 + j, :], hidT[:, k, :],
                                              slot_d(S[2])[:, k, j * C512:(j + 1) * C512],
                                              start=(k == 0), stop=(k == KF - 1))
                                last.then_inc(m["y_mm_a" if j == 0 else "y_mm_b"], 1)

                pe.reg_add(n, n, 1)
                k_ = pe.snap(n, min_val=NE + 1, max_val=WIN * NE + 1)
                for name in ("xt_a", "xt_b"):
                    pe.wait_ge(m[name], k_)
                for name in ("y_a", "y_b"):
                    pe.wait_ge(m[name], k_ + 1)

            modulation()
            turn_norm("a0", True)
            wait_hT("a0")
            for half in range(2):
                project_half(half)
                scan_half(half)
            pe.wait_ge(oT_ready, 6)
            out_project(0, oT, "hgrn", 10)
            turn_norm("m0", True)
            wait_hT("m0")
            route(0)
            experts(0)
            turn_norm("a1", False)
            wait_hT("a1")
            fourier()
            pe.wait_ge(z_evac, KD)
            out_project(1, zT, "four", 0)
            turn_norm("m1", True)
            wait_hT("m1")
            route(1)
            experts(1)

        @block.scalar
        def _(act):
            A = nc.scalar.activation

            def squares(name):
                for t in range(TT):
                    if name == "a0":
                        act.wait_ge(x_ready, 1)
                    elif name in ("m0", "m1"):
                        act.wait_ge(out_mm[int(name[1])], 6)
                        act.wait_ge(out_x[int(name[1])], 4 + t)
                    else:
                        act.wait_ge(M[0 if name == "a1" else 1]["x_done"], t + 1)
                    A(xn[:, t, :], x[:, t, :], ACT.Square, accum_out=stat[:, t:t + 1]).then_inc(n_sq, 1)

            def modulate(name, l, which):
                act.wait_ge(n_col, 1 * NORM[name] + 1)
                for k in range(0, KD, 2):
                    act.wait_ge(n_tp, 8 * NORM[name] + k + 1)
                    A(hT[:, k, 0:P], ps[:, k % 4, 0:P], ACT.Identity, bias=colmod[:, l, 2 * which, 0, k:k + 1],
                      scale=colA[:, k, 0:1])
                    A(hT[:, k, P:T], ps[:, k % 4, P:T], ACT.Identity, bias=colmod[:, l, 2 * which, 1, k:k + 1],
                      scale=colA[:, k, 1:2]).then_inc(n_hA, 1)

            def project_half(half):
                n = 18 * half
                if half == 1:
                    act.wait_ge(s_ready, 4)
                    act.wait_ge(o_mm, 3)
                for kind in range(5):
                    for c in range(4 if kind < 3 else TT):
                        act.wait_ge(proj_mm, n + 1)
                        bank = ps[:, n % 18 % 4, :]
                        sl = slice(c * T, (c + 1) * T)
                        if kind == 0:
                            ins = A(qT[:, sl], bank[:, 0:T], ACT.Copy)
                        elif kind < 3:
                            A(G[kind - 1][1][:, sl], bank[:, 0:T], ACT.Sigmoid)
                            ins = A(kd[kind - 1][:, sl], bank[:, 0:T], ACT.Sigmoid, scale=-1.0)
                        elif kind == 3:
                            ins = A(vrow[:, c, :], bank, ACT.Copy)
                        else:
                            if half == 1 and c == 0:
                                act.wait_ge(o_ready, 3)
                            ins = A(gsil[:, c, :], bank, ACT.Silu)
                        ins.then_inc(proj_evac, 1)
                        n += 1
                    act.sem_inc(hg_unit, 1)

            def scan_half(half):
                act.wait_ge(lvl_mm[0], 8 * half + 8)
                act.wait_ge(lvl_mm[1], 7 * half + 7)
                A(score[:].rearrange("p t h s -> p t (h s)"), ps[:, 0:3, :], ACT.Copy).then_inc(off_copied, 1)
                act.wait_ge(off_copied, half + 1)
                act.wait_ge(sd_copied, 11 * half + 11)
                for g in range(4):
                    r = slice(g * SMALL, (g + 1) * SMALL)
                    A(score[r].rearrange("p t h s -> p (t h) s")[:, :, r], compact[r], ACT.Copy
                      ).then_inc(score_ready, 1)
                for j in range(4):
                    act.wait_ge(kT_mm, 4 * half + j + 1)
                    A(kT[:, j % 2].rearrange("p h s -> p (h s)"), ps[:, [3, 7][j % 2], :], ACT.Copy
                      ).then_inc(kT_ready, 1)
                OB = [6, 7, 3]
                for t in range(TT):
                    act.wait_ge(o_mm, 3 * half + t + 1)
                    for h in range(HH):
                        last = A(on[:, t, h * P:(h + 1) * P], ps[:, OB[t], h * P:(h + 1) * P],
                                 ACT.Square, accum_out=ssq[:, t, h:h + 1])
                    last.then_inc(o_sq, 1)
                for t in range(TT):
                    act.wait_ge(o_tp, 3 * half + t + 1)
                    A(oT[:, HH * half:HH * (half + 1), t * P:(t + 1) * P],
                      ps[:, 4 + t % 2 if t < 2 else 6, :].rearrange("p (h s) -> p h s", h=HH), ACT.Copy
                      ).then_inc(oT_ready, 1)

            def route(l):
                m = M[l]
                act.wait_ge(m["exp_in"], 1)
                A(r4[:], r4[:], ACT.Exp).then_inc(m["exp_out"], 1)
                for t in range(TT):
                    act.wait_ge(m["back_mm"], 2 * t + 1)
                    A(hrow[:, t, 0:C512], ps[:, (2 * t) % 4, :], ACT.Copy).then_inc(m["back_act"], 1)
                    act.wait_ge(m["back_act"], t + 1)
                    act.wait_ge(m["back_dve"], t + 1)
                    act.dma_start(scratch["hrow"][l].rearrange("(t p) n -> p t n", p=P)[:, t, :], hrow[:, t, :]
                                  ).then_inc(m["hrow_out"], 16)
                act.wait_ge(m["exp_in"], 2)
                A(small[:, 6, :], small[:, 5, :], ACT.Exp).then_inc(m["exp_out"], 1)

            def experts(l):
                m = M[l]
                act.wait_ge(m["idx_ready"], 1)
                n = act.alloc_register(f"act_pass{l}")
                act.reg_mov(n, 0)
                act.wait_ge(m["turned"], 1)
                A(xt[:, 0:4, :].rearrange("p k s -> p (k s)"), ps[:, 0, :], ACT.Copy).then_inc(m["xt_a"], 1)
                with act.Fori(0, NE) as e:
                    windows = act.value_load(npass[0:1, bass.ds(e, 1)], min_val=1, max_val=WIN)
                    with act.Fori(0, windows):
                        act.reg_add(n, n, 1)
                        k_ = act.snap(n, min_val=1, max_val=WIN * NE)
                        act.wait_ge(m["gate_mm"], k_)
                        A(sg, ps[:, 2, :], ACT.Silu).then_inc(m["silu"], 1)
                        act.wait_ge(m["turned"], k_ + 1)
                        A(xt[:, 0:4, :].rearrange("p k s -> p (k s)"), ps[:, 0, :], ACT.Copy).then_inc(m["xt_a"], 1)
                        act.wait_ge(m["hid_turned"], k_)
                        A(hidT[:].rearrange("p k s -> p (k s)"), ps[:, 4, :], ACT.Copy).then_inc(m["hidT"], 1)
                        act.wait_ge(m["y_mm_a"], k_)
                        act.wait_ge(m["scattered"], 16 * k_ + 32)
                        A(ysb[:, 0:C512], ps[:, 5, :], ACT.Copy).then_inc(m["y_a"], 1)

            act.wait_ge(s_cond, 32)
            A(scond[:], cond[:], ACT.Silu).then_inc(scond_ready, 1)
            with nc.allow_non_contiguous_dma(reason="per-channel gains, small"):
                for j, (src, l) in enumerate([("norm1_g", 0), ("norm2_g", 0), ("norm1_g", 1), ("norm2_g", 1)]):
                    v = io[src][l]
                    v = v.rearrange("(k p) -> p k", p=P) if j == 2 else v.rearrange("(p k) -> p k", k=KD)
                    act.dma_start(gnorm[:, j, :], v).then_inc(s_small, 16)
                for l in range(2):
                    act.dma_start(wroute[:, l, :, 0:NG], io["router_group_w"][l].rearrange("(p k) n -> p k n", k=KD)
                                  ).then_inc(s_small, 16)
                    act.dma_start(wroute[:, l, :, NG:NL], io["router_expert_w"][l].rearrange("(p k) n -> p k n", k=KD)
                                  ).then_inc(s_small, 16)
                    act.dma_start(broute[:, l, 0:NG], io["router_group_b"][l:l + 1, :].to_broadcast((P, NG))
                                  ).then_inc(s_small, 16)
                    act.dma_start(broute[:, l, NG:NL], io["router_expert_b"][l:l + 1, :].to_broadcast((P, NE))
                                  ).then_inc(s_small, 16)
                act.dma_start(masks[:], io["masks"]).then_inc(s_small, 16)
            squares("a0")
            modulate("a0", 0, 0)
            act.wait_ge(n_tp, 8 * NORM["a0"] + KD)
            for half in range(2):
                if half == 1:
                    act.wait_ge(o_mm, 3)
                    act.wait_ge(gsil_ready, 3)
                for d in range(2):
                    act.dma_start(s0[:, d], io["state_hgrn"][0, 0, d, HH * half:HH * (half + 1)]
                                  .rearrange("h k v -> k h v")).then_inc(hg_in, 16)
                act.dma_start(hnorm, io["hgrn_norm_g"][:, C512 * half:C512 * (half + 1)].to_broadcast((P, C512))
                              ).then_inc(hg_in, 16)
                project_half(half)
                scan_half(half)
            act.wait_ge(out_mm[0], 3)
            act.sem_inc(hg_unit, 1)
            act.wait_ge(out_mm[0], 6)
            act.sem_inc(hg_unit, 1)
            squares("m0")
            modulate("m0", 0, 1)
            route(0)
            experts(0)
            squares("a1")
            act.dma_start(dft_c[:], io["dft_c"]).then_inc(four_in, 16)
            act.dma_start(dft_ctx[:], io["dft_ctx"]).then_inc(four_in, 16)
            act.dma_start(dft_lat[:], io["dft_lat"]).then_inc(four_in, 16)
            modulate("a1", 1, 0)
            for n in range(12):
                act.wait_ge(u_done4, n + 1)
                A(U[:, n // 4, n % 4, :], ps[:, 4 + n % 4, :], ACT.Copy).then_inc(u_evac4, 1)
            for k in range(KD):
                act.wait_ge(z_done, k + 1)
                A(zT[:, k, :], ps[:, k % 4, 0:T], ACT.Copy).then_inc(z_evac, 1)
            squares("m1")
            modulate("m1", 1, 1)
            route(1)
            experts(1)
            squares("fin")

        @block.vector
        def _(dve):
            V = nc.vector
            count = [0]

            def step(ins):
                count[0] += 1
                ins.then_inc(chain, 1)
                dve.wait_ge(chain, count[0])

            def normalise(name, tail_sem=None):
                for t in range(TT):
                    if t == 0:
                        dve.wait_ge(n_rs, 1 * NORM[name] + 1)
                    V.tensor_scalar(xn[:, t, :], x[:, t, :], stat[:, 3 + t:4 + t], None, ALU.mult).then_inc(n_xn, 1)

            def modulate(name, l, which):
                for g in range(2):
                    ins = V.scalar_tensor_tensor(out=colA[:, :, g], in0=colmod[:, l, 2 * which + 1, g, :], scalar=1.0,
                                                 in1=gnorm[:, 2 * l + which, :], op0=ALU.add, op1=ALU.mult)
                    if g == 0:
                        step(ins)
                ins.then_inc(n_col, 1)
                dve.wait_ge(n_col, 1 * NORM[name] + 1)
                for k in range(1, KD, 2):
                    dve.wait_ge(n_tp, 8 * NORM[name] + k + 1)
                    V.tensor_scalar(hT[:, k, 0:P], ps[:, k % 4, 0:P], colA[:, k, 0:1],
                                    colmod[:, l, 2 * which, 0, k:k + 1], ALU.mult, ALU.add)
                    V.tensor_scalar(hT[:, k, P:T], ps[:, k % 4, P:T], colA[:, k, 1:2],
                                    colmod[:, l, 2 * which, 1, k:k + 1], ALU.mult, ALU.add).then_inc(n_hV, 1)

            def mod_evac_row(U, bank):
                dve.wait_ge(mod_mm, U + 1)
                dve.wait_ge(mod_bias, 16 * (U + 1))
                if U:
                    dve.wait_ge(mod_row_out, 16 * U)
                V.tensor_tensor(mod_row[U], ps[0:2, bank, :], mod_b[U], ALU.add).then_inc(mod_evac, 1)

            steps = [0]

            def gemv(U):
                s, val = plan[("mod", U)]
                dve.wait_ge(landed[s], val)
                if U >= 6:
                    dve.wait_ge(mod_mm, U - 1)
                part = (part_hg if U < 20 else part_fo)[:, U % 2]
                for k in range(KD):
                    for g in range(2):
                        if k:
                            dve.wait_ge(gemv_step, steps[0] - 1)
                            ins = V.scalar_tensor_tensor(out=part[:, g, :], in0=slot3(s)[:, k, :],
                                                         scalar=scond[:, g, k:k + 1], in1=part[:, g, :],
                                                         op0=ALU.mult, op1=ALU.add)
                        else:
                            ins = V.tensor_scalar(part[:, g, :], slot3(s)[:, k, :], scond[:, g, k:k + 1], None,
                                                  ALU.mult)
                        ins.then_inc(gemv_step, 1)
                        steps[0] += 1
                dve.wait_ge(gemv_step, steps[0])
                dve.sem_inc(gemv_done, 1)

            def scan_half(half):
                n = 11 * half
                lv = 8 * half

                def take_compact(m, wait):
                    nonlocal n
                    if n:
                        dve.wait_ge(sd_copied, n)
                    V.copy_predicated(compact[:], masks[:, m:m + 1, :].to_broadcast((P, TT * HH, SMALL)),
                                      ps[:, 4 + n % 2, 0:TT * HH * SMALL].rearrange("p (a s) -> p a s", s=SMALL)
                                      ).then_inc(sd_copied, 1)
                    n += 1

                if half == 1:
                    dve.wait_ge(score_ready, 4)
                dve.wait_ge(proj_evac, 18 * half + 12)
                for d in range(2):
                    V.tensor_tensor(qd[d], qT, G[d][1], ALU.mult).then_inc(lvl_upd[d], 1)
                dve.wait_ge(lvl_mm[0], 8 * half + 1)
                take_compact(10, None)
                for i, h in enumerate(SIZES):
                    for d in range(2):
                        dve.wait_ge(lvl_mm[d], (8 * half + 2 + i) if d == 0 else (7 * half + 1 + i))
                        dve.wait_ge(lvl_upd[d], lv + i + 1)
                        halves = [a.rearrange("p (b two h) -> p b two h", two=2, h=h) for a in (qd[d], kd[d])]
                        nb = HH * T // (2 * h)
                        g = G[d][h].rearrange("p (b two) -> p b two", two=2)
                        late, early = (1, 0) if d == 0 else (0, 1)
                        V.tensor_tensor(halves[0][:, :, late, :], halves[0][:, :, late, :],
                                        g[:, :, early:early + 1].to_broadcast((P, nb, h)), ALU.mult)
                        V.tensor_tensor(halves[1][:, :, early, :], halves[1][:, :, early, :],
                                        g[:, :, late:late + 1].to_broadcast((P, nb, h)), ALU.mult)
                        V.tensor_tensor(G[d][2 * h], g[:, :, 0], g[:, :, 1], ALU.mult).then_inc(lvl_upd[d], 1)
                        if h < SMALL:
                            take_compact(2 * i + d, None)
                dve.wait_ge(hg_in, 48 * (half + 1))
                dve.wait_ge(lvl_upd[0], lv + 8)
                dve.wait_ge(lvl_upd[1], lv + 8)
                for j in range(4):
                    dve.wait_ge(u_mm, 4 * half + j + 1)
                    bank = ps[:, 4 + j % 2, :]
                    if j < 2:
                        if half == 1:
                            dve.wait_ge(st_written, 32)
                        V.tensor_copy(s_out[:, j].rearrange("p h v -> p (h v)"), bank).then_inc(s_ready, 1)
                    else:
                        t, d = (1, 0) if j == 2 else (2, 1)
                        for h in range(HH):
                            c = h * TT + t
                            ins = V.scalar_tensor_tensor(out=s1[:, d, h, :], in0=s0[:, d, h, :],
                                                         scalar=G[d][128][:, c:c + 1],
                                                         in1=bank[:, h * P:(h + 1) * P], op0=ALU.mult, op1=ALU.add)
                        ins.then_inc(s_ready, 1)
                dve.wait_ge(proj_evac, 18 * half + 18)
                for t in range(TT):
                    ins = V.tensor_tensor(gsil[:, t, :], gsil[:, t, :], hnorm, ALU.mult)
                    ins.then_inc(gsil_ready, 1)
                dve.wait_ge(gsil_ready, 3 * half + 3)
                OB = [6, 7, 3]
                for t in range(TT):
                    dve.wait_ge(o_rs, 3 * half + t + 1)
                    for h in range(HH):
                        s = slice(h * P, (h + 1) * P)
                        ins = V.scalar_tensor_tensor(out=on[:, t, s], in0=ps[:, OB[t], s], scalar=rsq[:, t, h:h + 1],
                                                     in1=gsil[:, t, s], op0=ALU.mult, op1=ALU.mult)
                    ins.then_inc(o_ready, 1)

            def residual(l):
                for n in range(6):
                    j, t = divmod(n, 3)
                    dve.wait_ge(out_mm[l], n + 1)
                    s = slice(j * C512, (j + 1) * C512)
                    tmp = [sg, hid][n % 2]
                    if n >= 2:
                        dve.wait_ge(out_x[l], n - 1)
                    step(V.tensor_tensor(tmp, ps[:, n % 4, :], gate_bc[:, 0, GROUP_OF[t], s], ALU.mult))
                    V.tensor_tensor(x[:, t, s], x[:, t, s], tmp, ALU.add).then_inc(out_x[l], 1)
                dve.wait_ge(out_x[l], 6)

            def route(l):
                m = M[l]
                b3 = lambda a, w: a.rearrange("p (t o) -> p t o", o=1).to_broadcast((P, TT, w))
                sm = lambda i: small[:, i, :]
                rg = c_("rev_group").rearrange("p (o n) -> p o n", o=1).to_broadcast((P, TT, NG))
                re = c_("rev_expert").rearrange("p (o n) -> p o n", o=1).to_broadcast((P, TT, NE))
                dve.wait_ge(s_small, 16 * 13)
                dve.wait_ge(m["logits"], 1)
                step(V.tensor_tensor(lg[:], ps[:, 4, 0:TT * 32].rearrange("p (t n) -> p t n", n=32)[:, :, 0:NL],
                                     broute[:, l:l + 1, :].to_broadcast((P, TT, NL)), ALU.add))
                step(V.tensor_reduce(sm(0), lg[:, :, 0:NG], AX.X, ALU.max))
                V.tensor_tensor(r4[:], lg[:, :, 0:NG], b3(sm(0), NG), ALU.subtract).then_inc(m["exp_in"], 1)
                step(V.tensor_tensor(ohg[:], lg[:, :, 0:NG], b3(sm(0), NG), ALU.is_equal))
                step(V.tensor_tensor(ohg[:], ohg[:], rg, ALU.mult))
                step(V.tensor_reduce(sm(1), ohg[:], AX.X, ALU.max))
                step(V.tensor_tensor(ohg[:], rg, b3(sm(1), NG), ALU.is_equal))
                go = ohg[:].rearrange("p t (g o) -> p t g o", o=1)
                for t in range(TT):
                    ins = V.tensor_tensor(el[:, t].rearrange("p (g e) -> p g e", g=NG),
                                          lg[:, t, NG:NL].rearrange("p (g e) -> p g e", g=NG),
                                          go[:, t].to_broadcast((P, NG, 4)), ALU.mult)
                    ins2 = V.tensor_scalar(e16[:, t].rearrange("p (g e) -> p g e", g=NG),
                                           go[:, t].to_broadcast((P, NG, 4)), -1.0, NEG, ALU.add, ALU.mult)
                step(ins2)
                step(V.tensor_tensor(el[:], el[:], e16[:], ALU.add))
                for c in range(2):
                    step(V.tensor_reduce(sm(2 + c), el[:], AX.X, ALU.max))
                    step(V.tensor_tensor(oh[:, c], el[:], b3(sm(2 + c), NE), ALU.is_equal))
                    step(V.tensor_tensor(oh[:, c], oh[:, c], re, ALU.mult))
                    step(V.tensor_reduce(sm(4), oh[:, c], AX.X, ALU.max))
                    step(V.tensor_tensor(oh[:, c], re, b3(sm(4), NE), ALU.is_equal))
                    if c == 0:
                        step(V.tensor_scalar(e16[:], oh[:, 0], -4 * NEG, None, ALU.mult))
                        step(V.tensor_tensor(el[:], el[:], e16[:], ALU.add))
                V.tensor_tensor(both[:], oh[:, 0], oh[:, 1], ALU.add).then_inc(m["chosen"], 1)
                V.tensor_tensor(sm(5), sm(3), sm(2), ALU.subtract).then_inc(m["exp_in"], 1)
                for t in range(TT):
                    dve.wait_ge(m["back_mm"], 2 * t + 2)
                    V.tensor_copy(hrow[:, t, C512:D], ps[:, (2 * t + 1) % 4, :]).then_inc(m["back_dve"], 1)
                dve.wait_ge(m["exp_out"], 2)
                step(V.tensor_reduce(sm(7), r4[:], AX.X, ALU.add))
                step(V.tensor_scalar(sm(8), sm(6), 1.0, None, ALU.add))
                step(V.tensor_tensor(sm(7), sm(7), sm(8), ALU.mult))
                step(V.reciprocal(wgt[:, 0, :], sm(7)))
                step(V.tensor_tensor(wgt[:, 1, :], wgt[:, 0, :], sm(6), ALU.mult))
                dve.wait_ge(m["pos_mm"], 1)
                step(V.tensor_copy(pos[:].rearrange("p t n -> p (t n)"), ps[:, 5, 0:TT * NE]))
                step(V.tensor_scalar(npass_f[:], ps[:, 5, TT * NE:(TT + 1) * NE], float(2 * P), 1.0, ALU.is_gt, ALU.add))
                step(V.scalar_tensor_tensor(out=npass_f[:], in0=ps[:, 5, TT * NE:(TT + 1) * NE], scalar=float(P),
                                            in1=npass_f[:], op0=ALU.is_gt, op1=ALU.add))
                step(V.tensor_copy(npass[:], npass_f[:]))
                for c in range(2):
                    step(V.tensor_tensor(e16[:], pos[:], oh[:, c], ALU.mult))
                    step(V.tensor_reduce(sm(9), e16[:], AX.X, ALU.add))
                    step(V.tensor_scalar(sm(10), sm(9), float(P), None, ALU.is_ge))
                    step(V.scalar_tensor_tensor(out=sm(10), in0=sm(9), scalar=float(2 * P), in1=sm(10),
                                                op0=ALU.is_ge, op1=ALU.add))
                    step(V.scalar_tensor_tensor(out=sm(9), in0=sm(10), scalar=-float(P), in1=sm(9),
                                                op0=ALU.mult, op1=ALU.add))
                    step(V.tensor_tensor(wnd[:], c_("window").rearrange("p (o n) -> p o n", o=1)
                                         .to_broadcast((P, TT, WIN)), b3(sm(10), WIN), ALU.is_equal))
                    for t in range(TT):
                        V.tensor_scalar(pos_oh[:, c, t, :], c_("iota"), small[:, 9, t:t + 1], None, ALU.is_equal)
                    for v in range(2):
                        a = CONST_AT["value"][0] + 3 * (2 * c + v)
                        step(V.tensor_tensor(wv[:], wnd[:], b3(const[:, a:a + 3], WIN), ALU.mult))
                        for t in range(TT):
                            ins = V.tensor_tensor(vals[:, c, t, v], oh[:, c, t].rearrange("p (e o) -> p e o", o=1)
                                                  .to_broadcast((P, NE, WIN)),
                                                  wv[:, t:t + 1, :].to_broadcast((P, NE, WIN)), ALU.mult)
                        step(ins)
                V.memset(stat[:, 6:7], 0.0).then_inc(m["onehots"], 1)
                dve.wait_ge(m["idx_mm"], 1)
                V.tensor_scalar(slots_idx[:, :, 0:NE * WIN], ps[:, 6, 0:2 * NE * WIN]
                                .rearrange("p (v n) -> p v n", v=2), -1.0, BIG, ALU.mult, ALU.add).then_inc(m["idx_ready"], 1)

            def experts(l):
                m = M[l]
                dve.wait_ge(m["idx_ready"], 1)
                n = dve.alloc_register(f"dve_pass{l}")
                dve.reg_mov(n, 0)
                dve.wait_ge(m["turned"], 1)
                V.tensor_copy(xt[:, 4:8, :].rearrange("p k s -> p (k s)"), ps[:, 1, :]).then_inc(m["xt_b"], 1)
                with dve.Fori(0, NE) as e:
                    windows = dve.value_load(npass[0:1, bass.ds(e, 1)], min_val=1, max_val=WIN)
                    with dve.Fori(0, windows):
                        dve.reg_add(n, n, 1)
                        k_ = dve.snap(n, min_val=1, max_val=WIN * NE)
                        dve.wait_ge(m["up_mm"], k_)
                        dve.wait_ge(m["silu"], k_)
                        V.tensor_tensor(hid, sg, ps[:, 3, :], ALU.mult).then_inc(m["hid"], 1)
                        dve.wait_ge(m["turned"], k_ + 1)
                        V.tensor_copy(xt[:, 4:8, :].rearrange("p k s -> p (k s)"), ps[:, 1, :]).then_inc(m["xt_b"], 1)
                        dve.wait_ge(m["y_mm_b"], k_)
                        dve.wait_ge(m["scattered"], 16 * k_ + 32)
                        V.tensor_copy(ysb[:, C512:D], ps[:, 6, :]).then_inc(m["y_b"], 1)
                    dve.sem_inc(m["used"], 1)

            def combine(l):
                m = M[l]
                for t in range(TT):
                    dve.wait_ge(m["yback"], 16 * TT)
                    a, b = yall[:, t, 0, :], yall[:, t, 1, :]
                    step(V.tensor_scalar(a, a, wgt[:, 0, t:t + 1], None, ALU.mult))
                    step(V.scalar_tensor_tensor(out=a, in0=b, scalar=wgt[:, 1, t:t + 1], in1=a,
                                                op0=ALU.mult, op1=ALU.add))
                    step(V.tensor_tensor(a, a, gate_bc[:, 1, GROUP_OF[t], :], ALU.mult))
                    V.tensor_tensor(x[:, t, :], x[:, t, :], a, ALU.add).then_inc(m["x_done"], 1)

            dve.wait_ge(s_x, 32)
            dve.wait_ge(s_pos, 16)
            V.tensor_tensor(x[:, 1:3, :], x[:, 1:3, :], yall[:, 0], ALU.add).then_inc(x_ready, 1)
            dve.wait_ge(x_ready, 1)
            for U in range(4):
                mod_evac_row(U, U % 2)
            normalise("a0")
            dve.wait_ge(mod_in[0], 16 * 4)
            dve.wait_ge(s_small, 16 * 13)
            modulate("a0", 0, 0)
            for half in range(2):
                if half == 1:
                    dve.wait_ge(o_tp, 3)
                for U in range(4 + 8 * half, 12 + 8 * half):
                    gemv(U)
                    if U > 4 + 8 * half:
                        mod_evac_row(U - 1, 6 + (U - 1) % 2)
                mod_evac_row(U, 6 + U % 2)
                dve.wait_ge(mod_row_out, 16 * (U + 1))
                scan_half(half)
            dve.wait_ge(mod_in[1], 16 * 8)
            residual(0)
            normalise("m0")
            modulate("m0", 0, 1)
            route(0)
            experts(0)
            combine(0)
            normalise("a1")
            dve.wait_ge(mod_in[2], 16 * 8)
            modulate("a1", 1, 0)
            gemv(20)
            gemv(21)
            mod_evac_row(20, 4)
            gemv(22)
            mod_evac_row(21, 5)
            gemv(23)
            mod_evac_row(22, 6)
            mod_evac_row(23, 7)
            residual(1)
            normalise("m1")
            dve.wait_ge(mod_in[3], 16 * 4)
            modulate("m1", 1, 1)
            route(1)
            experts(1)
            combine(1)
            dve.wait_ge(M[1]["x_done"], TT)
            normalise("fin")
            dve.wait_ge(fin_in, 16)
            dve.wait_ge(n_xn, 3 * NORM["fin"] + TT)
            for t in range(TT):
                V.tensor_tensor(xn[:, t, :], xn[:, t, :], gate_bc[:, 0, 0, :], ALU.mult).then_inc(fin_done, 1)

        @block.gpsimd
        def _(pool):
            G_ = nc.gpsimd

            def experts(l):
                m = M[l]
                pool.wait_ge(out_x[l], 6)
                G_.memset(xg, 0.0).then_inc(m["zeroed"], 1)
                G_.memset(ysb, 0.0).then_inc(m["zeroed"], 1)
                pool.wait_ge(m["zeroed"], 2)
                def send_rows():
                    G_.indirect_dma_start(out=scratch["y"][l],
                                          out_offset=bass.IndirectOffsetOnAxis(ap=si[:, 0:1], axis=0),
                                          in_=ysb, in_offset=None, bounds_check=2 * T - 1, oob_is_err=False
                                          ).then_inc(m["scattered"], 16)

                G_.memset(slots_idx[:, 1, NE * WIN:NE * WIN + 1], int(BIG)).then_inc(m["zeroed"], 1)
                pool.sem_inc(m["y_a"], 2)
                pool.sem_inc(m["y_b"], 2)
                pool.wait_ge(m["zeroed"], 3)
                pool.wait_ge(m["idx_ready"], 1)
                pool.wait_ge(m["hrow_out"], 16 * TT)
                G_.tensor_copy(si[:], slots_idx[:, 1, NE * WIN:NE * WIN + 1]).then_inc(m["zeroed"], 1)
                pool.wait_ge(m["zeroed"], 4)
                send_rows()
                n = pool.alloc_register(f"pool_pass{l}")
                col1 = pool.alloc_register(f"pool_col1_{l}")
                col2 = pool.alloc_register(f"pool_col2_{l}")
                pool.reg_mov(n, 0)
                pool.reg_mov(col1, NE * WIN)
                pool.reg_mov(col2, NE * WIN)

                def gather(k_, col):
                    G_.tensor_copy(gi[:], slots_idx[:, 0, col]).then_inc(m["gi_set"], 1)
                    pool.wait_ge(m["idx_ready"], 1)
                    pool.wait_ge(m["gi_set"], k_)
                    G_.indirect_dma_start(out=xg, out_offset=None, in_=scratch["hrow"][l],
                                          in_offset=bass.IndirectOffsetOnAxis(ap=gi[:, 0:1], axis=0),
                                          bounds_check=T - 1, oob_is_err=False).then_inc(m["gathered"], 16)

                def scatter(k_, col):
                    pool.wait_ge(m["scattered"], 16 * k_)
                    G_.tensor_copy(si[:], slots_idx[:, 1, bass.ds(pool.snap(col, min_val=0, max_val=NE * WIN), 1)]
                                   ).then_inc(m["si_set"], 1)
                    pool.wait_ge(m["idx_ready"], 1)
                    pool.wait_ge(m["y_a"], k_)
                    pool.wait_ge(m["y_b"], k_)
                    pool.wait_ge(m["si_set"], k_)
                    send_rows()

                with pool.Fori(0, NE) as e:
                    windows = pool.value_load(npass[0:1, bass.ds(e, 1)], min_val=1, max_val=WIN)
                    with pool.Fori(0, windows) as w:
                        pool.reg_add(n, n, 1)
                        k_ = pool.snap(n, min_val=1, max_val=WIN * NE)
                        gather(k_, bass.ds(e * WIN + w, 1))
                        scatter(k_, col2)
                        pool.reg_mov(col2, col1)
                        pool.reg_mov(col1, e * WIN + w)
                        pool.wait_ge(m["turned"], k_)
                        pool.wait_ge(m["gathered"], 16 * k_)
                pool.reg_add(n, n, 1)
                k1 = pool.snap(n, min_val=NE + 1, max_val=WIN * NE + 1)
                gather(k1, slice(0, 1))
                scatter(k1, col2)
                pool.reg_add(n, n, 1)
                k2 = pool.snap(n, min_val=NE + 2, max_val=WIN * NE + 2)
                scatter(k2, col1)
                pool.wait_ge(m["used"], NE)
                pool.wait_ge(m["scattered"], 16 * k2 + 16)
                pool.wait_ge(m["xt_a"], k1)
                pool.sem_inc(m["all_out"], 1)
                pool.wait_ge(m["all_out"], 1)
                for t in range(TT):
                    pool.dma_start(yall[:, t].rearrange("p c n -> p (c n)"),
                                   scratch["y"][l].rearrange("(t p c) n -> t p (c n)", p=P, c=2)[t]
                                   ).then_inc(m["yback"], 16)

            def rms(name):
                pool.wait_ge(n_sq, 3 * NORM[name] + TT)
                G_.tensor_scalar(stat[:, 0:3], stat[:, 0:3], 1.0 / D, EPS, ALU.mult, ALU.add).then_inc(n_ms, 1)
                pool.wait_ge(n_ms, 1 * NORM[name] + 1)
                G_.tensor_tensor(stat[:, 3:6], stat[:, 0:3], c_("minus_half")[:, 0:3], ALU.pow
                                 ).then_inc(n_rs, 1)

            def mod_rows(units):
                for U in units:
                    l, u = mod_unit(U)
                    cols = slice(u * C512, (u + 1) * C512)
                    if U == 12:
                        pool.wait_ge(o_tp, 3)
                    if U == 20:
                        pool.wait_ge(M[0]["x_done"], TT)
                    if U:
                        pool.wait_ge(mod_evac, U)
                    pool.dma_start(mod_b[U], io["b_mod"][l:l + 1, cols].to_broadcast((2, C512))
                                   ).then_inc(mod_bias, 16)
                    pool.wait_ge(mod_evac, U + 1)
                    pool.dma_start(scratch["mod"][l][:, cols], mod_row[U]).then_inc(mod_row_out, 16)
                pool.wait_ge(mod_row_out, 16 * (units[-1] + 1))

            def mod_columns(l, c, signal):
                q = [0, 1, 3, 4][c]
                for g in range(2):
                    v = scratch["mod"][l][g, q * D:(q + 1) * D]
                    v = v.rearrange("(k p) -> p k", p=P) if l == 1 and c < 2 else v.rearrange("(p k) -> p k", k=KD)
                    with nc.allow_non_contiguous_dma(reason="a modulation vector, 4 KB"):
                        pool.dma_start(colmod[:, l, c, g, :], v).then_inc(signal, 16)

            def mod_gates(l, w, signal):
                for g in range(2):
                    q = 2 + 3 * w
                    pool.dma_start(gate_bc[:, w, g, :], scratch["mod"][l][g:g + 1, q * D:(q + 1) * D]
                                   .to_broadcast((P, D))).then_inc(signal, 16)

            mod_rows(range(0, 4))
            mod_columns(0, 0, mod_in[0])
            mod_columns(0, 1, mod_in[0])
            pool.wait_ge(s_const, 16)
            rms("a0")
            for half in range(2):
                mod_rows(range(4 + 8 * half, 12 + 8 * half))
                if half == 0:
                    mod_columns(0, 2, mod_in[1])
                    mod_columns(0, 3, mod_in[1])
                    mod_gates(0, 0, mod_in[1])
                    mod_gates(0, 1, mod_in[1])
                for t in range(TT):
                    n = 3 * half + t + 1
                    pool.wait_ge(o_sq, n)
                    G_.tensor_scalar(rsq[:, t, :], ssq[:, t, :], 1.0 / P, EPS, ALU.mult, ALU.add).then_inc(o_ms, 1)
                    pool.wait_ge(o_ms, n)
                    G_.tensor_tensor(rsq[:, t, :], rsq[:, t, :], c_("minus_half"), ALU.pow).then_inc(o_rs, 1)
                for d in range(2):
                    pool.wait_ge(s_ready, 4 * half + d + 1)
                    pool.dma_start(io["o_state"][0, 0, d, HH * half:HH * (half + 1)].rearrange("h k v -> k h v"),
                                   s_out[:, d]).then_inc(st_written, 16)
            rms("m0")
            mod_columns(1, 0, mod_in[2])
            mod_columns(1, 1, mod_in[2])
            mod_columns(1, 2, mod_in[2])
            pool.wait_ge(out_x[0], 6)
            mod_gates(1, 0, mod_in[2])
            experts(0)
            rms("a1")
            mod_rows(range(20, 24))
            mod_columns(1, 3, mod_in[3])
            mod_gates(1, 1, mod_in[3])
            rms("m1")
            experts(1)
            rms("fin")
            pool.dma_start(gate_bc[:, 0, 0, :], io["final_norm_g"].rearrange("(o n) -> o n", o=1)
                           .to_broadcast((P, D))).then_inc(fin_in, 16)
            for t in range(TT):
                pool.wait_ge(fin_done, t + 1)
                dst = (io["o_prompt"].rearrange("b t n -> (b t) n") if t == 0
                       else io["o_sample"].rearrange("b (t p) n -> t (b p) n", p=P)[t - 1])
                pool.dma_start(dst, xn[:, t, :]).then_inc(y_out, 16)


def shape_constants():
    f = np.float32
    const = np.zeros((P, CONST_W), f)

    def put(name, a):
        i, j = CONST_AT[name]
        const[:a.shape[0], i:j] = a

    r = np.arange(P)
    put("ident", np.eye(P))
    put("upper", (r[:, None] < r[None, :]))
    put("ones", np.ones((P, P)))
    put("iota", np.tile(r, (P, 1)))
    put("rev_group", np.tile(4 - np.arange(4), (P, 1)))
    put("rev_expert", np.tile(16 - np.arange(16), (P, 1)))
    put("window", np.tile(np.arange(3), (P, 1)))
    tok = r[:, None] + P * np.arange(TT)[None, :]
    put("value", np.concatenate([BIG - tok, BIG - 2 * tok, BIG - tok, BIG - 2 * tok - 1], 1))
    put("minus_half", np.full((P, 4), -0.5))
    put("pick", np.tile([1, 0, 0, 1], (P, 1)))
    s, t = np.arange(P)[:, None] % SMALL, np.arange(SMALL)[None, :]
    masks = np.zeros((P, NMASK, SMALL), np.int32)
    for i, h in enumerate([1, 2, 4, 8, 16]):
        same = s // (2 * h) == t // (2 * h)
        masks[:, 2 * i] = same & (s // h % 2 == 0) & (t // h % 2 == 1)
        masks[:, 2 * i + 1] = same & (s // h % 2 == 1) & (t // h % 2 == 0)
    masks[:, 10] = s == t
    n, width, quarter = 2 * P, 64, D // 4
    tt = np.arange(n)
    omega = (1.0 / (f(10000.0) ** (np.arange(quarter, dtype=f) / f(quarter)))).astype(f)
    ar = (tt // width).astype(f)[:, None] * omega[None]
    ac = (tt % width).astype(f)[:, None] * omega[None]
    pos = np.concatenate([np.sin(ar), np.cos(ar), np.sin(ac), np.cos(ac)], -1).astype(f)
    pos = np.ascontiguousarray(pos.reshape(2, P, D).transpose(1, 0, 2))

    def dft(m):
        a = 2 * np.pi * (np.outer(np.arange(m), np.arange(m)) % m) / m
        return np.cos(a) / np.sqrt(m), np.sin(a) / np.sqrt(m)

    cc, sc = dft(256)
    dft_c = np.concatenate([cc, sc], 1).reshape(2, P, 512).transpose(1, 0, 2)
    c1, s1 = dft(P)
    dft_ctx = np.stack([c1, -s1], 1)
    dft_lat = np.stack([cc, -sc], 1).reshape(2, P, 2, 256).transpose(1, 0, 2, 3)
    out = dict(const=const, masks=masks, pos=pos, dft_c=dft_c, dft_ctx=dft_ctx, dft_lat=dft_lat)
    return {k: np.ascontiguousarray(v, v.dtype if v.dtype == np.int32 else f) for k, v in out.items()}


_INS = ["x_prompt", "x_sample", "state_hgrn", "c", "c_ctx", "w_mod", "b_mod", "norm1_g", "norm2_g", "hgrn_w_in",
        "hgrn_norm_g", "hgrn_w_out", "fourier_w_out", "router_group_w", "router_group_b", "router_expert_w",
        "router_expert_b", "moe_w_gate", "moe_w_up", "moe_w_down", "final_norm_g"]


def kernel(**inputs):
    import numpy as _np
    import concourse.bacc as _bacc
    from concourse import mybir as _mybir
    from concourse.bass_utils import run_bass_kernel_spmd as _run

    nc = _bacc.Bacc("TRN2", target_bir_lowering=False, num_devices=1)
    arrays = {n: _np.ascontiguousarray(inputs[n]) for n in _INS}
    arrays.update(shape_constants())
    io = {n: nc.dram_tensor(f"in_{n}", a.shape, _mybir.dt.from_np(a.dtype), kind="ExternalInput").ap()
          for n, a in arrays.items()}
    f32 = _mybir.dt.float32
    for n, shape in [("o_prompt", (1, 128, 1024)), ("o_sample", (1, 256, 1024)), ("o_state", (1, 1, 2, 8, 128, 128))]:
        io[n] = nc.dram_tensor(n, shape, f32, kind="ExternalOutput").ap()
    scratch = {"hrow": [nc.dram_tensor(f"hrow{l}", (T, D), f32, kind="Internal").ap() for l in range(2)],
               "mod": [nc.dram_tensor(f"modrow{l}", (2, 6 * D), f32, kind="Internal").ap() for l in range(2)],
               "y": [nc.dram_tensor(f"yrows{l}", (2 * T, D), f32, kind="Internal").ap() for l in range(2)]}
    program(nc, io, scratch)
    r = _run(nc, [{f"in_{n}": a for n, a in arrays.items()}], core_ids=[0]).results[0]
    return r["o_prompt"], r["o_sample"], r["o_state"]
```

```python
from contextlib import ExitStack

import numpy as np
import concourse.bass as bass
from concourse import mybir

F32 = mybir.dt.float32
I32 = mybir.dt.int32
U32 = mybir.dt.uint32
ACT = mybir.ActivationFunctionType
ALU = mybir.AluOpType
AX = mybir.AxisListType

P = 128
D = 1024
KD = D // P
TT = 3
T = TT * P
NH = 8
HH = NH // 2
C512 = 512
NE = 16
NG = 4
NL = 20
F = 512
KF = F // P
WIN = 3
EPS = 1e-6
BIG = 4096.0
NEG = 1e30
RING = 6
UNIT = 4096
SIZES = [1, 2, 4, 8, 16, 32, 64]
SMALL = 32
GROUP_OF = [0, 1, 1]


def const_columns():
    at, n = {}, 0
    for name, w in [("ident", 128), ("upper", 128), ("ones", 128), ("iota", 128), ("rev_group", 4), ("rev_expert", 16), ("window", 3), ("value", 12),
                    ("minus_half", 4), ("pick", 4)]:
        at[name] = (n, n + w)
        n += w
    return at, n


CONST_AT, CONST_W = const_columns()
NMASK = 11


def program(nc, io, scratch):
    with ExitStack() as ctx:
        def sb(name, shape, dt=F32):
            return ctx.enter_context(nc.sbuf_tensor(name, shape, dt))

        def sem(name):
            return ctx.enter_context(nc.semaphore(name))

        ring = sb("ring", [P, RING, UNIT])
        x = sb("x", [P, TT, D])
        hT = sb("hT", [P, KD, T])
        gate_bc = sb("gate_bc", [P, 2, 2, D])
        WORK = 15800
        work = sb("work", [P, WORK])
        const = sb("const", [P, CONST_W])
        masks = sb("masks", [P, NMASK, SMALL], I32)
        cond = sb("cond", [P, 2, KD])
        scond = sb("scond", [P, 2, KD])
        bcol = sb("bcol", [P, 2, KD])
        gnorm = sb("gnorm", [P, 4, KD])
        colmod = sb("colmod", [P, 2, 4, 2, KD])
        colA = sb("colA", [P, KD, 2])
        stat = sb("stat", [P, 8])
        wroute = sb("wroute", [P, 2, KD, NL])
        broute = sb("broute", [P, 2, NL])
        ps = ctx.enter_context(nc.psum_tensor("ps", [P, 8, 512], F32))

        def c_(name):
            a, b = CONST_AT[name]
            return const[:, a:b]

        ident = c_("ident")

        class Area:
            def __init__(self, t, start=0):
                self.t, self.n = t, start

            def take(self, n):
                a = self.t[:, self.n:self.n + n]
                self.n += n
                return a

        flat_ring = ring[:].rearrange("p s n -> p (s n)")
        first_row = work[0:2, WORK - 2 * D:WORK].rearrange("p (u n) -> p u n", u=4)
        mod_row, mod_b = [None] * 4, [None] * 4
        xn_at = [work[:, o:o + TT * D].rearrange("p (t n) -> p t n", t=TT) for o in (0, TT * D)]
        xn = xn_at[0]
        xn_of = lambda name: xn_at[name in ("m0", "m1")]
        hg = Area(work)
        oT = hg.take(KD * T).rearrange("p (k t) -> p k t", k=KD)
        qT = hg.take(HH * T)
        vrow = hg.take(TT * C512).rearrange("p (t n) -> p t n", t=TT)
        gsil = hg.take(TT * C512).rearrange("p (t n) -> p t n", t=TT)
        on = hg.take(TT * C512).rearrange("p (t n) -> p t n", t=TT)
        score = hg.take(TT * HH * P).rearrange("p (t h s) -> p t h s", t=TT, h=HH)
        compact = hg.take(TT * HH * SMALL).rearrange("p (a s) -> p a s", s=SMALL)
        kT = hg.take(2 * HH * P).rearrange("p (b h s) -> p b h s", b=2, h=HH)
        s0 = hg.take(2 * HH * P).rearrange("p (d h v) -> p d h v", d=2, h=HH)
        s1 = hg.take(2 * HH * P).rearrange("p (d h v) -> p d h v", d=2, h=HH)
        s_out = hg.take(2 * HH * P).rearrange("p (d h v) -> p d h v", d=2, h=HH)
        hnorm = hg.take(C512)
        ssq = hg.take(TT * HH).rearrange("p (t h) -> p t h", t=TT)
        rsq = hg.take(TT * HH).rearrange("p (t h) -> p t h", t=TT)
        tail = Area(flat_ring, 3 * UNIT)
        qd = [tail.take(HH * T) for _ in range(2)]
        G = [{h: tail.take(HH * T // h) for h in SIZES[1:] + [128]} for _ in range(2)]
        assert tail.n >= 4 * UNIT
        kd = [tail.take(HH * T) for _ in range(2)]
        for d in range(2):
            G[d][1] = tail.take(HH * T)
        assert hg.n <= WORK and tail.n <= RING * UNIT
        o0 = 3 * D + HH * T + 2 * TT * C512
        part_hg = work[:, o0:o0 + 4 * C512].rearrange("p (b g n) -> p b g n", b=2, g=2)
        mod_row += [work[0:2, o0 + 4 * C512:o0 + 5 * C512]] * 16
        mod_b += [work[0:2, o0 + 5 * C512:o0 + 6 * C512]] * 16
        fo = Area(work, TT * D)
        U = fo.take(TT * 4 * C512).rearrange("p (t g n) -> p t g n", t=TT, g=4)
        dft_c = fo.take(2 * C512).rearrange("p (k n) -> p k n", k=2)
        dft_ctx = fo.take(2 * P).rearrange("p (c n) -> p c n", c=2)
        dft_lat = fo.take(4 * 2 * P).rearrange("p (t c n) -> p t c n", t=2, c=2)
        zT = work[:, 0:TT * D].rearrange("p (k t) -> p k t", k=KD)
        part_fo = fo.take(4 * C512).rearrange("p (b g n) -> p b g n", b=2, g=2)
        assert fo.n <= WORK - 2 * D
        mod_row += [work[0:2, WORK - 2 * D:WORK - 2 * D + C512]] * 4
        mod_b += [work[0:2, WORK - D:WORK - D + C512]] * 4
        me = Area(work)
        hrow = me.take(TT * D).rearrange("p (t n) -> p t n", t=TT)
        yall = work[:, 0:2 * TT * D].rearrange("p (t c n) -> p t c n", t=TT, c=2)
        me.n = 2 * TT * D
        xg = me.take(D)
        xt = me.take(D).rearrange("p (k s) -> p k s", k=KD)
        sg = me.take(F)
        hid = me.take(F)
        hidT = me.take(F).rearrange("p (k s) -> p k s", k=KF)
        ysb = me.take(D)
        pos_oh = me.take(2 * TT * P).rearrange("p (c t s) -> p c t s", c=2, t=TT)
        vals = me.take(2 * TT * 2 * NE * WIN).rearrange("p (c t v e w) -> p c t v e w", c=2, t=TT, v=2, e=NE)
        lgT = me.take(T)
        lg = me.take(TT * NL).rearrange("p (t n) -> p t n", t=TT)
        r4 = me.take(TT * NG).rearrange("p (t n) -> p t n", t=TT)
        ohg = me.take(TT * NG).rearrange("p (t n) -> p t n", t=TT)
        el = me.take(TT * NE).rearrange("p (t n) -> p t n", t=TT)
        e2 = me.take(2 * TT * NE).rearrange("p (c t n) -> p c t n", c=2, t=TT)
        oh = me.take(2 * TT * NE).rearrange("p (c t n) -> p c t n", c=2, t=TT)
        both = me.take(TT * NE).rearrange("p (t n) -> p t n", t=TT)
        small = me.take(16 * TT).rearrange("p (n t) -> p n t", t=TT)
        place_, window_ = me.take(2 * TT), me.take(2 * TT)
        wnd = me.take(2 * TT * WIN).rearrange("p (t w) -> p t w", w=WIN)
        wv = me.take(2 * TT * 2 * WIN).rearrange("p (c t v w) -> p c t v w", c=2, t=TT, v=2)
        assert me.n <= WORK - 2 * D, me.n
        slots_idx = sb("slots_idx", [P, 2, NE * WIN + 1], U32)
        gi = sb("gi", [P, 1], U32)
        si = sb("si", [P, 1], U32)
        npass = sb("npass", [P, NE], I32)
        npass_f = sb("npass_f", [P, NE])
        wgt = sb("wgt", [P, 2, TT])

        landed = [sem(f"landed{s}") for s in range(RING)]
        s_const, s_x, s_cond, s_small = sem("const_in"), sem("x_in"), sem("cond_in"), sem("small_in")
        s_pos = sem("pos_in")
        scond_ready = sem("scond_ready")
        x_ready = sem("x_ready")
        mod_bias, mod_mm, mod_evac, mod_row_out = (sem("mod_bias_in"), sem("mod_mm"), sem("mod_evac"),
                                                   sem("mod_row_out"))
        mod_turned, col_set = sem("mod_turned"), sem("first_columns")
        gemv_step, gemv_done = sem("gemv_step"), sem("gemv_done")
        mod_in = [sem(f"mod_in{i}") for i in range(4)]
        NORM = {"a0": 0, "m0": 1, "a1": 2, "m1": 3, "fin": 4}
        n_sq = sem("square")
        n_rs = sem("rms")
        n_ms = sem("mean_square")
        o_ms, o_rs = sem("o_mean_square"), sem("o_rms")
        n_xn = sem("xn")
        n_tp = sem("xn_turned")
        n_hA = sem("hT_act")
        n_hV = sem("hT_dve")
        n_col = sem("col")
        proj_mm, proj_evac = sem("proj_mm"), sem("proj_evac")
        hg_in = sem("hgrn_in")
        hg_unit = sem("hgrn_unit_used")
        lvl_upd = [sem("level_updated_f"), sem("level_updated_b")]
        lvl_mm = [sem("level_scored_f"), sem("level_scored_b")]
        sd_copied = sem("compact_copied")
        score_ready, kT_mm, kT_ready, u_mm, s_ready = (sem("score_ready"), sem("kT_turned"), sem("kT_ready"),
                                                       sem("u_mm"), sem("state_ready"))
        off_copied = sem("score_off_copied")
        o_mm, o_sq, o_ready, o_tp, oT_ready = (sem("o_mm"), sem("o_square"), sem("o_ready"), sem("o_turned"),
                                               sem("oT_ready"))
        st_written = sem("state_written")
        gsil_ready = sem("gsil_ready")
        out_mm = [sem(f"out_mm{l}") for l in range(2)]
        out_x = [sem(f"out_x{l}") for l in range(2)]
        four_in, u_done4, u_evac4, z_done, z_evac = (sem("dft_in"), sem("dftc_mm"), sem("dftc_evac"),
                                                     sem("dftt_mm"), sem("dftt_evac"))
        M = []
        for l in range(2):
            M.append({n: sem(f"moe{l}_{n}") for n in [
                "logits_t", "logits_sb", "logits", "chosen", "pos_mm", "onehots", "idx_mm", "idx_ready", "back_mm", "back_act",
                "hrow_out", "zeroed", "si_set", "gi_set", "gathered", "turned", "xt_a", "xt_b", "gate_mm", "up_mm",
                "silu", "hid", "hid_turned", "hidT", "y_mm_a", "y_mm_b", "y_a", "y_b", "scattered", "used", "all_out", "second", "weights", "x_done",
                "exp_in", "exp_out"]})
        yback = [sem(f"expert_rows_in{t}") for t in range(TT)]
        chain = sem("dve_chain")
        y_out = sem("y_out")
        fin_in = sem("final_gain_in")
        fin_done = sem("final_done")

        w_mod = io["w_mod"].rearrange("l (p k) n -> l p k n", k=KD)
        w_in = io["hgrn_w_in"].rearrange("l (k p) n -> l p k n", p=P)
        w_o = [io["hgrn_w_out"].rearrange("l (k p) n -> l p k n", p=P),
               io["fourier_w_out"].rearrange("l (k p) n -> l p k n", p=P)]
        w_g = io["moe_w_gate"].rearrange("l e (p k) n -> l e p (k n)", k=KD)
        w_u = io["moe_w_up"].rearrange("l e (p k) n -> l e p (k n)", k=KD)
        w_d = io["moe_w_down"].rearrange("l e (k p) n -> l e p k n", p=P)

        uses = [0] * RING
        plan = {}

        def place(phase, u, s):
            uses[s] += 1
            plan[(phase, u)] = (s, 16 * uses[s])

        def mod_unit(U):
            return (0, U) if U < 12 else (1, U - 12)

        def mod_slot(U):
            return [3, 4, 5, 2][U] if U < 4 else ([2, 3][U % 2] if 12 <= U < 20 else [3, 2][U % 2])

        STREAM = ([("mod", U) for U in range(4)] + [("hgrn", 0), ("hgrn", 1)]
                  + [("mod", 4), ("mod", 5), ("mod", 6), ("mod", 7), ("hgrn", 2), ("mod", 8), ("mod", 9), ("hgrn", 3),
                     ("mod", 10), ("mod", 11), ("hgrn", 4), ("hgrn", 5)]
                  + [("mod", 12), ("hgrn", 6), ("mod", 13), ("mod", 14), ("hgrn", 7), ("mod", 15), ("mod", 16),
                     ("hgrn", 8), ("mod", 17), ("mod", 18), ("hgrn", 9), ("mod", 19), ("hgrn", 10), ("hgrn", 11)])
        for phase, u in STREAM:
            place(phase, u, mod_slot(u) if phase == "mod" else u % 2)
        MOE_SLOTS = [[3, 4, 5, 2, 0, 1], [4, 5, 2, 3, 0, 1]]
        moe_before = [list(uses)]
        for u in range(3 * NE):
            place("moe0", u, MOE_SLOTS[0][u % 6])
        for phase, u, s in [("mod", 20, 3), ("mod", 21, 2), ("four", 0, 0), ("four", 1, 1), ("mod", 22, 3),
                            ("mod", 23, 2)]:
            place(phase, u, s)
        moe_before.append(list(uses))

        def slot3(s):
            return ring[:, s, :].rearrange("p (k n) -> p k n", k=KD)

        def slot_d(s):
            return ring[:, s, :].rearrange("p (k n) -> p k n", k=KF)

        def in_cols(u):
            half, kind = divmod(u, 5)
            return kind * D + half * C512

        TURNED = [[(0, 2), (1, 3), (4, 6), (5, 7)], [(0, 2, 4, 6), (1, 3, 5, 7)]]
        TURN_BANK = [4, 0]
        UP_BANK, HID_BANK = [3, 7], [4, 2]

        def modulated_parts(name, l, which, engine):
            for part in range(2):
                for b in range(engine, len(TURNED[part]), 2):
                    steps = []
                    for i, k in enumerate(TURNED[part][b]):
                        for g in ((0, 1) if part == 0 else (1,)):
                            t = g if part == 0 else 2
                            o = i * 2 * P + t * P if part == 0 else i * P
                            steps.append((hT[:, k, t * P:(t + 1) * P], ps[:, TURN_BANK[part] + b, o:o + P],
                                          colA[:, k, g:g + 1], colmod[:, l, 2 * which, g, k:k + 1],
                                          g == 1))
                    yield part, 6 * NORM[name] + 4 * part + b + 1, steps

        block = ctx.enter_context(nc.Block())

        @block.sync
        def _(sp):
            def mod_load(U):
                l, u = mod_unit(U)
                s, _ = plan[("mod", U)]
                sp.dma_start(slot3(s), w_mod[l, :, :, u * C512:(u + 1) * C512]).then_inc(landed[s], 16)

            def moe_units(l, first_wait):
                slots = MOE_SLOTS[l]
                for u in range(6):
                    first_wait(u)
                    w = [w_g, w_u, w_d][u % 3]
                    s = slots[u]
                    sp.dma_start(slot_d(s) if w is w_d else ring[:, s, :], w[l, u // 3]).then_inc(landed[s], 16)
                with sp.Fori(1, NE // 2) as i:
                    for par in range(2):
                        sp.wait_ge(M[l]["used"], 2 * i + (par - 1))
                        for j, w in enumerate([w_g, w_u, w_d]):
                            s = slots[3 * par + j]
                            sp.dma_start(slot_d(s) if w is w_d else ring[:, s, :], w[l, 2 * i + par]
                                         ).then_inc(landed[s], 16)

            def expert_rows(l):
                sp.wait_ge(M[l]["all_out"], 1)
                for t in range(TT):
                    sp.dma_start(yall[:, t].rearrange("p c n -> p (c n)"),
                                 scratch["y"][l].rearrange("(t p c) n -> t p (c n)", p=P, c=2)[t]
                                 ).then_inc(yback[t], 16)

            sp.dma_start(cond[:, 0, :], io["c_ctx"].rearrange("(p k) -> p k", k=KD)).then_inc(s_cond, 16)
            sp.dma_start(cond[:, 1, :], io["c"].rearrange("b (p k) -> (b p) k", k=KD)).then_inc(s_cond, 16)
            sp.dma_start(const[:], io["const"]).then_inc(s_const, 16)

            for phase, u in STREAM:
                if phase == "hgrn":
                    s, _ = plan[("hgrn", u)]
                    if u >= 2:
                        sp.wait_ge(hg_unit, u - 1)
                    src = (w_in[0, :, :, in_cols(u):in_cols(u) + C512] if u < 10
                           else w_o[0][0, :, :, (u - 10) * C512:(u - 9) * C512])
                    sp.dma_start(slot3(s), src).then_inc(landed[s], 16)
                    continue
                if u == 4:
                    sp.wait_ge(mod_mm, 1)
                elif u == 5:
                    sp.wait_ge(mod_mm, 4)
                elif u > 5:
                    if u == 13:
                        sp.wait_ge(o_mm, 3)
                    sp.wait_ge(gemv_done, u - 4 if u == 12 else u - 5)
                mod_load(u)
                if u == 3:
                    sp.dma_start(x[:, 0, :], io["x_prompt"].rearrange("b t n -> (b t) n")).then_inc(s_x, 16)
                    sp.dma_start(x[:, 1:3, :], io["x_sample"].rearrange("b (t p) n -> (b p) t n", p=P)
                                 ).then_inc(s_x, 16)
                    sp.dma_start(yall[:, 0], io["pos"]).then_inc(s_pos, 16)

            def moe0_wait(u):
                s = MOE_SLOTS[0][u]
                if s >= 3:
                    sp.wait_ge(o_mm, 6)
                if s in (2, 3):
                    sp.wait_ge(gemv_done, 16)
                if s < 2:
                    sp.wait_ge(out_mm[0], 3 * s + 3)
            moe_units(0, moe0_wait)

            sp.wait_ge(M[0]["used"], NE - 1)
            sp.wait_ge(gemv_done, 15)
            mod_load(20)
            sp.wait_ge(M[0]["used"], NE)
            expert_rows(0)
            sp.dma_start(dft_c[:], io["dft_c"]).then_inc(four_in, 16)
            sp.dma_start(dft_ctx[:], io["dft_ctx"]).then_inc(four_in, 16)
            sp.dma_start(dft_lat[:], io["dft_lat"]).then_inc(four_in, 16)
            mod_load(21)
            for u in range(2):
                s, _ = plan[("four", u)]
                sp.dma_start(slot3(s), w_o[1][0, :, :, u * C512:(u + 1) * C512]).then_inc(landed[s], 16)
            for U in (22, 23):
                sp.wait_ge(gemv_done, U - 5)
                mod_load(U)

            def moe1_wait(u):
                s = MOE_SLOTS[1][u]
                if s in (2, 3):
                    sp.wait_ge(gemv_done, 20)
                if s < 2:
                    sp.wait_ge(out_mm[1], 3 * s + 3)
            moe_units(1, moe1_wait)
            expert_rows(1)

            for t in range(TT):
                sp.wait_ge(fin_done, t + 1)
                dst = (io["o_prompt"].rearrange("b t n -> (b t) n") if t == 0
                       else io["o_sample"].rearrange("b (t p) n -> t (b p) n", p=P)[t - 1])
                sp.dma_start(dst, xn[:, t, :]).then_inc(y_out, 16)
            sp.wait_ge(y_out, 16 * TT)
            sp.wait_ge(st_written, 16 * 4)

        @block.tensor
        def _(pe):
            mm = pe.matmul

            def turn_row(U):
                if U == 0:
                    pe.wait_ge(s_const, 16)
                pe.wait_ge(mod_evac, U + 1)
                for c in range(4):
                    j = 4 * U + c
                    last = pe.transpose(ps[:, 4 + U // 2, 2 * j:2 * j + 2], first_row[:, U, c * P:(c + 1) * P],
                                        ident[0:2, 0:2])
                last.then_inc(mod_turned, 1)

            def modulation():
                pe.wait_ge(scond_ready, 1)
                for U in range(4):
                    s, val = plan[("mod", U)]
                    pe.wait_ge(landed[s], val)
                    if U >= 2:
                        pe.wait_ge(mod_evac, U - 1)
                    for k in range(KD):
                        last = mm(ps[0:2, U % 2, :], scond[:, :, k], slot3(s)[:, k, :],
                                  start=(k == 0), stop=(k == KD - 1))
                    last.then_inc(mod_mm, 1)
                    if U:
                        turn_row(U - 1)
                turn_row(3)
            def mod_sum(U, bank):
                pe.wait_ge(gemv_done, U - 3)
                if U >= 6:
                    pe.wait_ge(mod_evac, U - 1)
                part = part_hg if U < 20 else part_fo
                for g in range(2):
                    last = mm(ps[0:2, bank, :], c_("pick")[:, 2 * g:2 * g + 2], part[:, U % 2, g, :],
                              start=(g == 0), stop=(g == 1))
                last.then_inc(mod_mm, 1)

            def turn_norm(name, strided, router=None):
                xn = xn_of(name)
                for part in range(2):
                    pe.wait_ge(n_xn, 3 * NORM[name] + 2 + part)
                    for b, chunks in enumerate(TURNED[part]):
                        for i, k in enumerate(chunks):
                            for t in ((0, 1) if part == 0 else (2,)):
                                o = i * 2 * P + t * P if part == 0 else i * P
                                src = xn[:, t, k:D:KD] if strided else xn[:, t, k * P:(k + 1) * P]
                                last = pe.transpose(ps[:, TURN_BANK[part] + b, o:o + P], src, ident)
                        last.then_inc(n_tp, 1)
                    if router is not None:
                        router_logits(name, router, part)

            def router_logits(name, l, part):
                cols = slice(0, 2 * P) if part == 0 else slice(2 * P, T)
                for k in range(KD):
                    pe.wait_ge(n_hA if k % 2 == 0 else n_hV, 8 * NORM[name] + 4 * part + k // 2 + 1)
                    last = mm(ps[0:NL, 2, cols], wroute[:, l, k, :], hT[:, k, cols], start=(k == 0), stop=(k == KD - 1))
                if part == 1:
                    last.then_inc(M[l]["logits_t"], 1)

            def wait_hT(name):
                pe.wait_ge(n_hA, 8 * NORM[name] + KD)
                pe.wait_ge(n_hV, 8 * NORM[name] + KD)

            def project_half(half):
                n = 18 * half
                for kind in range(5):
                    s, val = plan[("hgrn", 5 * half + kind)]
                    pe.wait_ge(landed[s], val)
                    W = slot3(s)
                    for c in range(4 if kind < 3 else TT):
                        if n % 18 >= 4:
                            pe.wait_ge(proj_evac, n - 3)
                        bank = ps[:, n % 18 % 4, :]
                        for k in range(KD):
                            if kind < 3:
                                last = mm(bank[:, 0:T], W[:, k, c * P:(c + 1) * P], hT[:, k, :],
                                          start=(k == 0), stop=(k == KD - 1))
                            else:
                                last = mm(bank, hT[:, k, c * P:(c + 1) * P], W[:, k, :],
                                          start=(k == 0), stop=(k == KD - 1))
                            if k == 3 and n % 18 >= 16:
                                block_scores(half, 2 * (n % 18 - 16) + 1)
                        last.then_inc(proj_mm, 1)
                        n += 1
                        if n == 19:
                            turn_outputs(0)
                        c18 = n - 18 * half
                        if c18 >= 4 and c18 % 2 == 0:
                            U = 4 + 8 * half + (c18 - 4) // 2
                            if U == 12:
                                pe.wait_ge(oT_ready, 3)
                            mod_sum(U, 6 + U % 2)
                        if c18 in (16, 17):
                            if c18 == 16:
                                pe.wait_ge(proj_evac, 18 * half + 12)
                                compact_scores(half, 0, kd[0], qT, (kd[1], qT)).then_inc(lvl_mm[0], 1)
                            block_scores(half, 2 * (c18 - 16))

            def compact_scores(half, call, lhs, rhs, more=None):
                n = 11 * half + call
                if call >= 2:
                    pe.wait_ge(sd_copied, n - 1)
                bank = ps[:, 4 + n % 2, :]
                for t in range(TT):
                    for h in range(HH):
                        o = (t * HH + h) * SMALL
                        for g in range(4):
                            a = h * T + t * P + g * SMALL
                            pairs = [(lhs, rhs)] + ([more] if more else [])
                            for j, (L, R) in enumerate(pairs):
                                last = mm(bank[g * SMALL:(g + 1) * SMALL, o:o + SMALL], L[:, a:a + SMALL],
                                          R[:, a:a + SMALL], start=(j == 0), stop=(j == len(pairs) - 1))
                return last

            def block_scores(half, i):
                h = SIZES[i]
                for d in range(2):
                    pe.wait_ge(lvl_upd[d], 8 * half + i + 1)
                    if h < SMALL:
                        last = compact_scores(half, 1 + 2 * i + d, kd[d], qd[d])
                    else:
                        if h == SMALL and d == 0:
                            pe.wait_ge(proj_evac, 18 * half + 18)
                        for t in range(TT):
                            for hh in range(HH):
                                for b in range(0, P, 2 * h):
                                    lo, hi = b, b + h
                                    sk, tq = (lo, hi) if d == 0 else (hi, lo)
                                    a = hh * T + t * P
                                    last = mm(ps[sk:sk + h, t, hh * P + tq:hh * P + tq + h],
                                              kd[d][:, a + sk:a + sk + h], qd[d][:, a + tq:a + tq + h],
                                              start=True, stop=True)
                    last.then_inc(lvl_mm[d], 1)

            def scan_half(half):
                for i in range(4, len(SIZES)):
                    block_scores(half, i)
                UNITS = [(0, 0), (0, 1), (1, 0), (2, 1)]

                def turn_keys(j):
                    t, d = UNITS[j]
                    pe.wait_ge(lvl_upd[d], 8 * half + 8)
                    if 4 * half + j >= 2:
                        pe.wait_ge(kT_ready, 4 * half + j - 1)
                        pe.wait_ge(u_mm, 4 * half + j - 1)
                    for h in range(HH):
                        a = h * T + t * P
                        last = pe.transpose(ps[:, [3, 7][j % 2], h * P:(h + 1) * P], kd[d][:, a:a + P], ident)
                    last.then_inc(kT_mm, 1)

                def increment(j):
                    t, d = UNITS[j]
                    pe.wait_ge(kT_ready, 4 * half + j + 1)
                    if j == 0:
                        pe.wait_ge(sd_copied, 11 * half + 11)
                    if j >= 2:
                        pe.wait_ge(s_ready, 4 * half + j - 1)
                    for h in range(HH):
                        last = mm(ps[:, 4 + j % 2, h * P:(h + 1) * P], kT[:, j % 2, h, :],
                                  vrow[:, t, h * P:(h + 1) * P], start=True, stop=True)
                    last.then_inc(u_mm, 1)

                turn_keys(0)
                turn_keys(1)
                for j in range(4):
                    increment(j)
                    if j + 2 < 4:
                        turn_keys(j + 2)

                OB = [6, 7, 3]
                pe.wait_ge(score_ready, 4 * (half + 1))
                pe.wait_ge(kT_ready, 4 * half + 4)
                for t in range(TT):
                    if t == 1:
                        pe.wait_ge(s_ready, 4 * half + 4)
                    for h in range(HH):
                        a = h * T + t * P
                        out = ps[:, OB[t], h * P:(h + 1) * P]
                        last = mm(out, score[:, t, h, :], vrow[:, t, h * P:(h + 1) * P], start=True, stop=(t == 0))
                        if t:
                            st_f = s0[:, 0, h, :] if t == 1 else s1[:, 0, h, :]
                            st_b = s1[:, 1, h, :] if t == 1 else s0[:, 1, h, :]
                            mm(out, qd[0][:, a:a + P], st_f, start=False, stop=False)
                            last = mm(out, qd[1][:, a:a + P], st_b, start=False, stop=True)
                    last.then_inc(o_mm, 1)

            def turn_outputs(half):
                for t in range(TT):
                    pe.wait_ge(o_ready, 3 * half + t + 1)
                    for h in range(HH):
                        last = pe.transpose(ps[:, 4 + t % 2 if t < 2 else 6, h * P:(h + 1) * P],
                                            on[:, t, h * P:(h + 1) * P], ident)
                    last.then_inc(o_tp, 1)

            def out_project(l, src, phase, u0):
                for j in range(2):
                    s, val = plan[(phase, u0 + j)]
                    pe.wait_ge(landed[s], val)
                    for t in range(TT):
                        n = 3 * j + t
                        if l == 1 and n in (1, 3):
                            mod_sum(22 + n // 2, 6 + n // 2)
                        if n >= 4:
                            pe.wait_ge(out_x[l], n - 3)
                        for k in range(KD):
                            last = mm(ps[:, n % 4, :], src[:, k, t * P:(t + 1) * P], slot3(s)[:, k, :],
                                      start=(k == 0), stop=(k == KD - 1))
                        last.then_inc(out_mm[l], 1)

            def fourier():
                pe.wait_ge(four_in, 48)
                for t in range(TT):
                    for g in range(4):
                        n = 4 * t + g
                        if n >= 4:
                            pe.wait_ge(u_evac4, n - 3)
                        for k in range(2):
                            last = mm(ps[:, 4 + n % 4, :], hT[:, 2 * g + k, t * P:(t + 1) * P], dft_c[:, k, :],
                                      start=(k == 0), stop=(k == 1))
                        last.then_inc(u_done4, 1)
                pe.wait_ge(u_evac4, 12)
                mod_sum(20, 4)
                for k in range(KD):
                    if k == 3:
                        mod_sum(21, 5)
                    if k >= 4:
                        pe.wait_ge(z_evac, k - 3)
                    g, o = k // 2, (k % 2) * P
                    bank = ps[:, k % 4, :]
                    for c in range(2):
                        mm(bank[:, 0:P], U[:, 0, g, c * 256 + o:c * 256 + o + P], dft_ctx[:, c, :],
                           start=(c == 0), stop=(c == 1))
                    for t in range(2):
                        for c in range(2):
                            last = mm(bank[:, P:T], U[:, 1 + t, g, c * 256 + o:c * 256 + o + P], dft_lat[:, t, c, :],
                                      start=(t + c == 0), stop=(t + c == 2))
                    last.then_inc(z_done, 1)

            def route(l):
                m = M[l]
                pe.wait_ge(m["logits_sb"], 1)
                for t in range(TT):
                    last = pe.transpose(ps[:, 3, t * 32:t * 32 + NL], lgT[0:NL, t * P:(t + 1) * P], ident[0:NL, 0:NL])
                last.then_inc(m["logits"], 1)
                for t in range(TT):
                    for j in range(2):
                        n = 2 * t + j
                        if n >= 4:
                            pe.wait_ge(m["back_act"], n - 3)
                        for k in range(4):
                            last = pe.transpose(ps[:, 4 + n % 4, k * P:(k + 1) * P],
                                                hT[:, 4 * j + k, t * P:(t + 1) * P], ident)
                        last.then_inc(m["back_mm"], 1)
                pe.wait_ge(m["chosen"], 1)
                for t in range(TT):
                    mm(ps[:, 2, t * NE:(t + 1) * NE], c_("upper"), both[:, t, :], start=True, stop=(t == 0))
                    for b in range(t):
                        mm(ps[:, 2, t * NE:(t + 1) * NE], c_("ones"), both[:, b, :], start=False, stop=(b == t - 1))
                for t in range(TT):
                    last = mm(ps[:, 2, TT * NE:(TT + 1) * NE], c_("ones"), both[:, t, :],
                              start=(t == 0), stop=(t == TT - 1))
                last.then_inc(m["pos_mm"], 1)
                pe.wait_ge(m["back_act"], 2 * TT)
                for c in range(2):
                    pe.wait_ge(m["onehots"], c + 1)
                    for t in range(TT):
                        last = mm(ps[:, 3, 0:2 * NE * WIN], pos_oh[:, c, t, :],
                                  vals[:, c, t].rearrange("p v e w -> p (v e w)"),
                                  start=(c + t == 0), stop=(c == 1 and t == TT - 1))
                last.then_inc(m["idx_mm"], 1)

            def turn_tokens(m):
                for k in range(KD):
                    last = pe.transpose(ps[:, k // 4, (k % 4) * P:(k % 4 + 1) * P], xg[:, k * P:(k + 1) * P], ident)
                last.then_inc(m["turned"], 1)

            def turn_hidden(m, j):
                for k in range(KF // 2):
                    c = j * KF // 2 + k
                    last = pe.transpose(ps[:, HID_BANK[j], k * P:(k + 1) * P], hid[:, c * P:(c + 1) * P], ident)
                last.then_inc(m["hid_turned"], 1)

            def experts(l):
                m = M[l]
                pe.wait_ge(m["idx_ready"], 1)
                n = pe.alloc_register(f"pe_pass{l}")
                pe.reg_mov(n, 0)
                half = pe.alloc_register(f"pe_half{l}")
                pe.reg_mov(half, 0)
                pe.wait_ge(m["gathered"], 16)
                turn_tokens(m)
                with pe.Fori(0, NE // 2) as i:
                    for par in range(2):
                        S = [MOE_SLOTS[l][3 * par + j] for j in range(3)]
                        windows = pe.value_load(npass[0:1, bass.ds(2 * i + par, 1)], min_val=1, max_val=WIN)
                        with pe.Fori(0, windows):
                            pe.reg_add(n, n, 1)
                            pe.reg_add(half, half, 1)
                            first = pe.snap(half, min_val=1, max_val=2 * WIN * NE)
                            pe.reg_add(half, half, 1)
                            second = pe.snap(half, min_val=1, max_val=2 * WIN * NE)
                            k_ = pe.snap(n, min_val=1, max_val=WIN * NE)
                            for s in S:
                                pe.wait_ge(landed[s], 16 * i + 16 * (moe_before[l][s] + 1))
                            pe.wait_ge(m["xt_a"], k_)
                            pe.wait_ge(m["xt_b"], k_)
                            for k in range(KD):
                                last = mm(ps[:, 2, :], xt[:, k, :], slot3(S[0])[:, k, :],
                                          start=(k == 0), stop=(k == KD - 1))
                            last.then_inc(m["gate_mm"], 1)
                            for j in range(2):
                                for k in range(KD):
                                    last = mm(ps[:, UP_BANK[j], 0:F // 2], xt[:, k, :],
                                              slot3(S[1])[:, k, j * F // 2:(j + 1) * F // 2],
                                              start=(k == 0), stop=(k == KD - 1))
                                last.then_inc(m["up_mm"], 1)
                            pe.wait_ge(m["hid"], first)
                            turn_hidden(m, 0)
                            pe.wait_ge(m["gathered"], 16 * k_ + 16)
                            turn_tokens(m)
                            pe.wait_ge(m["hid"], second)
                            turn_hidden(m, 1)
                            pe.wait_ge(m["hidT"], first)
                            pe.wait_ge(m["y_a"], k_ + 1)
                            pe.wait_ge(m["y_b"], k_ + 1)
                            for j in range(2):
                                for k in range(KF):
                                    if j == 0 and k == KF // 2:
                                        pe.wait_ge(m["hidT"], second)
                                    last = mm(ps[:, 5 + j, :], hidT[:, k, :],
                                              slot_d(S[2])[:, k, j * C512:(j + 1) * C512],
                                              start=(k == 0), stop=(k == KF - 1))
                                last.then_inc(m["y_mm_a" if j == 0 else "y_mm_b"], 1)

                pe.reg_add(n, n, 1)
                k_ = pe.snap(n, min_val=NE + 1, max_val=WIN * NE + 1)
                for name in ("xt_a", "xt_b"):
                    pe.wait_ge(m[name], k_)
                for name in ("y_a", "y_b"):
                    pe.wait_ge(m[name], k_ + 1)

            modulation()
            turn_norm("a0", False)
            wait_hT("a0")
            for half in range(2):
                project_half(half)
                scan_half(half)
            turn_outputs(1)
            pe.wait_ge(oT_ready, 6)
            out_project(0, oT, "hgrn", 10)
            turn_norm("m0", True, 0)
            route(0)
            experts(0)
            turn_norm("a1", False)
            wait_hT("a1")
            fourier()
            pe.wait_ge(z_evac, KD)
            out_project(1, zT, "four", 0)
            turn_norm("m1", True, 1)
            route(1)
            experts(1)

        @block.scalar
        def _(act):
            A = nc.scalar.activation

            def squares(name):
                for t in range(TT):
                    if name == "a0":
                        act.wait_ge(x_ready, 1)
                    elif name in ("m0", "m1"):
                        act.wait_ge(out_x[int(name[1])], 4 + t)
                    else:
                        act.wait_ge(M[0 if name == "a1" else 1]["x_done"], t + 1)
                    A(xn_of(name)[:, t, :], x[:, t, :], ACT.Square, accum_out=stat[:, t:t + 1]).then_inc(n_sq, 1)

            def modulate(name, l, which):
                act.wait_ge(n_col, 1 * NORM[name] + 1)
                for part, turned, steps in modulated_parts(name, l, which, 0):
                    act.wait_ge(n_tp, turned)
                    for out, src, scale, shift, last in steps:
                        ins = A(out, src, ACT.Identity, bias=shift, scale=scale)
                        if last:
                            ins.then_inc(n_hA, 1)

            def project_half(half):
                n = 18 * half
                if half == 1:
                    act.wait_ge(s_ready, 4)
                    act.wait_ge(o_mm, 3)
                for kind in range(5):
                    for c in range(4 if kind < 3 else TT):
                        act.wait_ge(proj_mm, n + 1)
                        bank = ps[:, n % 18 % 4, :]
                        sl = slice(c * T, (c + 1) * T)
                        if kind == 0:
                            ins = A(qT[:, sl], bank[:, 0:T], ACT.Copy)
                        elif kind < 3:
                            A(G[kind - 1][1][:, sl], bank[:, 0:T], ACT.Sigmoid)
                            ins = A(kd[kind - 1][:, sl], bank[:, 0:T], ACT.Sigmoid, scale=-1.0)
                        elif kind == 3:
                            ins = A(vrow[:, c, :], bank, ACT.Copy)
                        else:
                            if half == 1 and c == 0:
                                act.wait_ge(o_ready, 3)
                            ins = A(gsil[:, c, :], bank, ACT.Silu)
                        ins.then_inc(proj_evac, 1)
                        n += 1
                    act.sem_inc(hg_unit, 1)

            def scan_half(half):
                act.wait_ge(mod_row_out, 16 * (8 * half + 8))
                act.wait_ge(lvl_mm[0], 8 * half + 8)
                act.wait_ge(lvl_mm[1], 7 * half + 7)
                A(score[:].rearrange("p t h s -> p t (h s)"), ps[:, 0:3, :], ACT.Copy).then_inc(off_copied, 1)
                act.wait_ge(off_copied, half + 1)
                act.wait_ge(sd_copied, 11 * half + 11)
                for g in range(4):
                    r = slice(g * SMALL, (g + 1) * SMALL)
                    A(score[r].rearrange("p t h s -> p (t h) s")[:, :, r], compact[r], ACT.Copy
                      ).then_inc(score_ready, 1)
                for j in range(4):
                    act.wait_ge(kT_mm, 4 * half + j + 1)
                    A(kT[:, j % 2].rearrange("p h s -> p (h s)"), ps[:, [3, 7][j % 2], :], ACT.Copy
                      ).then_inc(kT_ready, 1)
                OB = [6, 7, 3]
                for t in range(TT):
                    act.wait_ge(o_mm, 3 * half + t + 1)
                    for h in range(HH):
                        last = A(on[:, t, h * P:(h + 1) * P], ps[:, OB[t], h * P:(h + 1) * P],
                                 ACT.Square, accum_out=ssq[:, t, h:h + 1])
                    last.then_inc(o_sq, 1)
                for t in range(TT):
                    act.wait_ge(o_tp, 3 * half + t + 1)
                    A(oT[:, HH * half:HH * (half + 1), t * P:(t + 1) * P],
                      ps[:, 4 + t % 2 if t < 2 else 6, :].rearrange("p (h s) -> p h s", h=HH), ACT.Copy
                      ).then_inc(oT_ready, 1)

            def route(l):
                m = M[l]
                act.wait_ge(m["exp_in"], 1)
                A(r4[:], r4[:], ACT.Exp).then_inc(m["exp_out"], 1)
                for t in range(TT):
                    for j in range(2):
                        act.wait_ge(m["back_mm"], 2 * t + j + 1)
                        A(hrow[:, t, j * C512:(j + 1) * C512], ps[:, 4 + (2 * t + j) % 4, :], ACT.Copy
                          ).then_inc(m["back_act"], 1)
                    act.wait_ge(m["back_act"], 2 * t + 2)
                    act.dma_start(scratch["hrow"][l].rearrange("(t p) n -> p t n", p=P)[:, t, :], hrow[:, t, :]
                                  ).then_inc(m["hrow_out"], 16)
                act.wait_ge(m["exp_in"], 2)
                A(small[:, 6, :], small[:, 5, :], ACT.Exp).then_inc(m["exp_out"], 1)

            def experts(l):
                m = M[l]
                act.wait_ge(m["idx_ready"], 1)
                n = act.alloc_register(f"act_pass{l}")
                act.reg_mov(n, 0)
                half = act.alloc_register(f"act_half{l}")
                act.reg_mov(half, 0)
                act.wait_ge(m["turned"], 1)
                A(xt[:, 0:4, :].rearrange("p k s -> p (k s)"), ps[:, 0, :], ACT.Copy).then_inc(m["xt_a"], 1)
                with act.Fori(0, NE) as e:
                    windows = act.value_load(npass[0:1, bass.ds(e, 1)], min_val=1, max_val=WIN)
                    with act.Fori(0, windows):
                        act.reg_add(n, n, 1)
                        act.reg_add(half, half, 1)
                        first = act.snap(half, min_val=1, max_val=2 * WIN * NE)
                        act.reg_add(half, half, 1)
                        second = act.snap(half, min_val=1, max_val=2 * WIN * NE)
                        k_ = act.snap(n, min_val=1, max_val=WIN * NE)
                        act.wait_ge(m["gate_mm"], k_)
                        A(sg, ps[:, 2, :], ACT.Silu).then_inc(m["silu"], 1)
                        act.wait_ge(m["hid_turned"], first)
                        A(hidT[:, 0:KF // 2].rearrange("p k s -> p (k s)"), ps[:, HID_BANK[0], 0:F // 2], ACT.Copy
                          ).then_inc(m["hidT"], 1)
                        act.wait_ge(m["turned"], k_ + 1)
                        A(xt[:, 0:4, :].rearrange("p k s -> p (k s)"), ps[:, 0, :], ACT.Copy).then_inc(m["xt_a"], 1)
                        act.wait_ge(m["hid_turned"], second)
                        A(hidT[:, KF // 2:KF].rearrange("p k s -> p (k s)"), ps[:, HID_BANK[1], 0:F // 2], ACT.Copy
                          ).then_inc(m["hidT"], 1)
                        act.wait_ge(m["y_mm_a"], k_)
                        act.wait_ge(m["scattered"], 16 * k_ + 32)
                        A(ysb[:, 0:C512], ps[:, 5, :], ACT.Copy).then_inc(m["y_a"], 1)

            def combine(l):
                act.wait_ge(M[l]["weights"], 1)
                for t in range(TT):
                    act.wait_ge(yback[t], 16 * (l + 1))
                    A(yall[:, t, 1, :], yall[:, t, 1, :], ACT.Copy, scale=wgt[:, 1, t:t + 1]
                      ).then_inc(M[l]["second"], 1)

            act.wait_ge(s_cond, 32)
            A(scond[:], cond[:], ACT.Silu).then_inc(scond_ready, 1)
            with nc.allow_non_contiguous_dma(reason="per-channel gains, small"):
                act.dma_start(bcol[:].rearrange("p c k -> p (c k)"),
                              io["b_mod"][0, 0:2 * D].rearrange("(n p) -> p n", p=P)).then_inc(mod_in[0], 16)
                for j, (src, l) in enumerate([("norm1_g", 0), ("norm2_g", 0), ("norm1_g", 1), ("norm2_g", 1)]):
                    v = io[src][l]
                    v = v.rearrange("(k p) -> p k", p=P) if j % 2 == 0 else v.rearrange("(p k) -> p k", k=KD)
                    act.dma_start(gnorm[:, j, :], v).then_inc(s_small if j else mod_in[0], 16)
            squares("a0")
            with nc.allow_non_contiguous_dma(reason="the router's weights, small"):
                for l in range(2):
                    act.dma_start(wroute[:, l, :, 0:NG], io["router_group_w"][l].rearrange("(p k) n -> p k n", k=KD)
                                  ).then_inc(s_small, 16)
                    act.dma_start(wroute[:, l, :, NG:NL], io["router_expert_w"][l].rearrange("(p k) n -> p k n", k=KD)
                                  ).then_inc(s_small, 16)
                    act.dma_start(broute[:, l, 0:NG], io["router_group_b"][l:l + 1, :].to_broadcast((P, NG))
                                  ).then_inc(s_small, 16)
                    act.dma_start(broute[:, l, NG:NL], io["router_expert_b"][l:l + 1, :].to_broadcast((P, NE))
                                  ).then_inc(s_small, 16)
                act.dma_start(masks[:], io["masks"]).then_inc(s_small, 16)
            modulate("a0", 0, 0)
            act.wait_ge(n_tp, 6 * NORM["a0"] + 6)
            for half in range(2):
                if half == 1:
                    act.wait_ge(o_mm, 3)
                    act.wait_ge(gsil_ready, 3)
                for d in range(2):
                    act.dma_start(s0[:, d], io["state_hgrn"][0, 0, d, HH * half:HH * (half + 1)]
                                  .rearrange("h k v -> k h v")).then_inc(hg_in, 16)
                act.dma_start(hnorm, io["hgrn_norm_g"][:, C512 * half:C512 * (half + 1)].to_broadcast((P, C512))
                              ).then_inc(hg_in, 16)
                project_half(half)
                scan_half(half)
            squares("m0")
            modulate("m0", 0, 1)
            route(0)
            experts(0)
            combine(0)
            squares("a1")
            modulate("a1", 1, 0)
            for n in range(12):
                act.wait_ge(u_done4, n + 1)
                A(U[:, n // 4, n % 4, :], ps[:, 4 + n % 4, :], ACT.Copy).then_inc(u_evac4, 1)
            for k in range(KD):
                act.wait_ge(z_done, k + 1)
                A(zT[:, k, :], ps[:, k % 4, 0:T], ACT.Copy).then_inc(z_evac, 1)
            squares("m1")
            act.dma_start(gate_bc[:, 0, 0, :], io["final_norm_g"].rearrange("(o n) -> o n", o=1)
                          .to_broadcast((P, D))).then_inc(fin_in, 16)
            modulate("m1", 1, 1)
            route(1)
            experts(1)
            combine(1)
            squares("fin")

        @block.vector
        def _(dve):
            V = nc.vector
            count = [0]

            def step(ins):
                count[0] += 1
                ins.then_inc(chain, 1)
                dve.wait_ge(chain, count[0])

            def normalise(name, tiles=range(TT)):
                for t in tiles:
                    dve.wait_ge(n_rs, 3 * NORM[name] + t + 1)
                    V.tensor_scalar(xn_of(name)[:, t, :], x[:, t, :], stat[:, 3 + t:4 + t], None, ALU.mult
                                    ).then_inc(n_xn, 1)

            def columns(name, l, which):
                for g in range(2):
                    ins = V.scalar_tensor_tensor(out=colA[:, :, g], in0=colmod[:, l, 2 * which + 1, g, :], scalar=1.0,
                                                 in1=gnorm[:, 2 * l + which, :], op0=ALU.add, op1=ALU.mult)
                    if g == 0:
                        step(ins)
                ins.then_inc(n_col, 1)
                dve.wait_ge(n_col, 1 * NORM[name] + 1)

            def modulate(name, l, which, last_tile=False):
                for part, turned, steps in modulated_parts(name, l, which, 1):
                    if part == 1 and last_tile:
                        normalise(name, [2])
                        last_tile = False
                    dve.wait_ge(n_tp, turned)
                    for out, src, scale, shift, last in steps:
                        ins = V.tensor_scalar(out, src, scale, shift, ALU.mult, ALU.add)
                        if last:
                            ins.then_inc(n_hV, 1)

            def mod_evac_row(U, bank):
                dve.wait_ge(mod_mm, U + 1)
                dve.wait_ge(mod_bias, 16 * (U - 3))
                if U > 4:
                    dve.wait_ge(mod_row_out, 16 * (U - 4))
                V.tensor_tensor(mod_row[U], ps[0:2, bank, :], mod_b[U], ALU.add).then_inc(mod_evac, 1)

            steps = [0]

            def gemv(U):
                s, val = plan[("mod", U)]
                dve.wait_ge(landed[s], val)
                if U >= 6:
                    dve.wait_ge(mod_mm, U - 1)
                part = (part_hg if U < 20 else part_fo)[:, U % 2]
                for k in range(KD):
                    for g in range(2):
                        if k:
                            dve.wait_ge(gemv_step, steps[0] - 1)
                            ins = V.scalar_tensor_tensor(out=part[:, g, :], in0=slot3(s)[:, k, :],
                                                         scalar=scond[:, g, k:k + 1], in1=part[:, g, :],
                                                         op0=ALU.mult, op1=ALU.add)
                        else:
                            ins = V.tensor_scalar(part[:, g, :], slot3(s)[:, k, :], scond[:, g, k:k + 1], None,
                                                  ALU.mult)
                        ins.then_inc(gemv_step, 1)
                        steps[0] += 1
                dve.wait_ge(gemv_step, steps[0])
                dve.sem_inc(gemv_done, 1)

            def scan_half(half):
                n = 11 * half
                lv = 8 * half

                def take_compact(m):
                    nonlocal n
                    if n:
                        dve.wait_ge(sd_copied, n)
                    V.copy_predicated(compact[:], masks[:, m:m + 1, :].to_broadcast((P, TT * HH, SMALL)),
                                      ps[:, 4 + n % 2, 0:TT * HH * SMALL].rearrange("p (a s) -> p a s", s=SMALL)
                                      ).then_inc(sd_copied, 1)
                    n += 1

                if half == 1:
                    dve.wait_ge(score_ready, 4)
                dve.wait_ge(s_small, 16 * 12)
                dve.wait_ge(lvl_mm[0], 8 * half + 1)
                take_compact(10)
                for i, h in enumerate(SIZES):
                    if i in (1, 4):
                        U = 10 + 8 * half + i // 4
                        mod_evac_row(U, 6 + U % 2)
                    for d in range(2):
                        dve.wait_ge(lvl_mm[d], (8 * half + 2 + i) if d == 0 else (7 * half + 1 + i))
                        dve.wait_ge(lvl_upd[d], lv + i + 1)
                        halves = [a.rearrange("p (b two h) -> p b two h", two=2, h=h) for a in (qd[d], kd[d])]
                        nb = HH * T // (2 * h)
                        g = G[d][h].rearrange("p (b two) -> p b two", two=2)
                        late, early = (1, 0) if d == 0 else (0, 1)
                        V.tensor_tensor(halves[0][:, :, late, :], halves[0][:, :, late, :],
                                        g[:, :, early:early + 1].to_broadcast((P, nb, h)), ALU.mult)
                        V.tensor_tensor(halves[1][:, :, early, :], halves[1][:, :, early, :],
                                        g[:, :, late:late + 1].to_broadcast((P, nb, h)), ALU.mult)
                        V.tensor_tensor(G[d][2 * h], g[:, :, 0], g[:, :, 1], ALU.mult).then_inc(lvl_upd[d], 1)
                        if h < SMALL:
                            take_compact(2 * i + d)
                dve.wait_ge(hg_in, 48 * (half + 1))
                dve.wait_ge(proj_evac, 18 * half + 18)
                for t in range(TT):
                    ins = V.tensor_tensor(gsil[:, t, :], gsil[:, t, :], hnorm, ALU.mult)
                    ins.then_inc(gsil_ready, 1)
                dve.wait_ge(lvl_upd[0], lv + 8)
                dve.wait_ge(lvl_upd[1], lv + 8)
                for j in range(4):
                    dve.wait_ge(u_mm, 4 * half + j + 1)
                    bank = ps[:, 4 + j % 2, :]
                    if j < 2:
                        if half == 1:
                            dve.wait_ge(st_written, 32)
                        V.tensor_copy(s_out[:, j].rearrange("p h v -> p (h v)"), bank).then_inc(s_ready, 1)
                    else:
                        t, d = (1, 0) if j == 2 else (2, 1)
                        for h in range(HH):
                            c = h * TT + t
                            ins = V.scalar_tensor_tensor(out=s1[:, d, h, :], in0=s0[:, d, h, :],
                                                         scalar=G[d][128][:, c:c + 1],
                                                         in1=bank[:, h * P:(h + 1) * P], op0=ALU.mult, op1=ALU.add)
                        ins.then_inc(s_ready, 1)
                dve.wait_ge(gsil_ready, 3 * half + 3)
                OB = [6, 7, 3]
                for t in range(TT):
                    dve.wait_ge(o_rs, 3 * half + t + 1)
                    for h in range(HH):
                        s = slice(h * P, (h + 1) * P)
                        ins = V.scalar_tensor_tensor(out=on[:, t, s], in0=ps[:, OB[t], s], scalar=rsq[:, t, h:h + 1],
                                                     in1=gsil[:, t, s], op0=ALU.mult, op1=ALU.mult)
                    ins.then_inc(o_ready, 1)

            def residual(l):
                for n in range(6):
                    j, t = divmod(n, 3)
                    if n == 5:
                        normalise(f"m{l}", [0, 1])
                    dve.wait_ge(out_mm[l], n + 1)
                    s = slice(j * C512, (j + 1) * C512)
                    tmp = [sg, hid][n % 2]
                    if n >= 2:
                        dve.wait_ge(out_x[l], n - 1)
                    step(V.tensor_tensor(tmp, ps[:, n % 4, :], gate_bc[:, 0, GROUP_OF[t], s], ALU.mult))
                    V.tensor_tensor(x[:, t, s], x[:, t, s], tmp, ALU.add).then_inc(out_x[l], 1)
                dve.wait_ge(out_x[l], 6)

            def route(l):
                m = M[l]
                b3 = lambda a, w: a.rearrange("p (t o) -> p t o", o=1).to_broadcast((P, TT, w))
                sm = lambda i: small[:, i, :]
                rg = c_("rev_group").rearrange("p (o n) -> p o n", o=1).to_broadcast((P, TT, NG))
                re = c_("rev_expert").rearrange("p (o n) -> p o n", o=1).to_broadcast((P, TT, NE))
                dve.wait_ge(s_small, 16 * 12)
                dve.wait_ge(m["logits_t"], 1)
                V.tensor_copy(lgT[0:NL, :], ps[0:NL, 2, 0:T]).then_inc(m["logits_sb"], 1)
                dve.wait_ge(m["logits"], 1)
                step(V.tensor_tensor(lg[:], ps[:, 3, 0:TT * 32].rearrange("p (t n) -> p t n", n=32)[:, :, 0:NL],
                                     broute[:, l:l + 1, :].to_broadcast((P, TT, NL)), ALU.add))
                step(V.tensor_reduce(sm(0), lg[:, :, 0:NG], AX.X, ALU.max))
                V.tensor_tensor(r4[:], lg[:, :, 0:NG], b3(sm(0), NG), ALU.subtract).then_inc(m["exp_in"], 1)
                step(V.tensor_tensor(ohg[:], lg[:, :, 0:NG], b3(sm(0), NG), ALU.is_equal))
                step(V.tensor_tensor(ohg[:], ohg[:], rg, ALU.mult))
                step(V.tensor_reduce(sm(1), ohg[:], AX.X, ALU.max))
                step(V.tensor_tensor(ohg[:], rg, b3(sm(1), NG), ALU.is_equal))
                step(V.tensor_scalar(ohg[:], ohg[:], -1.0, NEG, ALU.add, ALU.mult))
                for t in range(TT):
                    ins = V.tensor_tensor(el[:, t].rearrange("p (g e) -> p g e", g=NG),
                                          lg[:, t, NG:NL].rearrange("p (g e) -> p g e", g=NG),
                                          ohg[:, t].rearrange("p (g o) -> p g o", o=1).to_broadcast((P, NG, 4)),
                                          ALU.add)
                step(ins)
                for c in range(2):
                    step(V.tensor_reduce(sm(2 + c), el[:], AX.X, ALU.max))
                    step(V.tensor_tensor(oh[:, c], el[:], b3(sm(2 + c), NE), ALU.is_equal))
                    step(V.tensor_tensor(oh[:, c], oh[:, c], re, ALU.mult))
                    step(V.tensor_reduce(sm(4), oh[:, c], AX.X, ALU.max))
                    step(V.tensor_tensor(oh[:, c], re, b3(sm(4), NE), ALU.is_equal))
                    if c == 0:
                        step(V.scalar_tensor_tensor(out=el[:], in0=oh[:, 0], scalar=-4 * NEG, in1=el[:],
                                                    op0=ALU.mult, op1=ALU.add))
                V.tensor_tensor(both[:], oh[:, 0], oh[:, 1], ALU.add).then_inc(m["chosen"], 1)
                V.tensor_tensor(sm(5), sm(3), sm(2), ALU.subtract).then_inc(m["exp_in"], 1)
                dve.wait_ge(m["pos_mm"], 1)
                count_ = ps[:, 2, TT * NE:(TT + 1) * NE]
                for c in range(2):
                    V.tensor_tensor(e2[:, c], ps[:, 2, 0:TT * NE].rearrange("p (t n) -> p t n", n=NE), oh[:, c], ALU.mult)
                step(V.tensor_scalar(npass_f[:], count_, float(2 * P), 1.0, ALU.is_gt, ALU.add))
                V.tensor_reduce(place_, e2[:].rearrange("p c t n -> p (c t) n"), AX.X, ALU.add)
                step(V.scalar_tensor_tensor(out=npass_f[:], in0=count_, scalar=float(P), in1=npass_f[:],
                                            op0=ALU.is_gt, op1=ALU.add))
                V.tensor_scalar(window_, place_, float(P), None, ALU.is_ge)
                step(V.tensor_copy(npass[:], npass_f[:]))
                step(V.scalar_tensor_tensor(out=window_, in0=place_, scalar=float(2 * P), in1=window_,
                                            op0=ALU.is_ge, op1=ALU.add))
                ct = 2 * TT
                V.tensor_tensor(wnd[:], c_("window").rearrange("p (o n) -> p o n", o=1).to_broadcast((P, ct, WIN)),
                                window_.rearrange("p (t o) -> p t o", o=1).to_broadcast((P, ct, WIN)), ALU.is_equal)
                step(V.scalar_tensor_tensor(out=place_, in0=window_, scalar=-float(P), in1=place_,
                                            op0=ALU.mult, op1=ALU.add))
                for c in range(2):
                    for v in range(2):
                        a = CONST_AT["value"][0] + 3 * (2 * c + v)
                        V.tensor_tensor(wv[:, c, :, v, :], wnd[:, TT * c:TT * (c + 1), :],
                                        b3(const[:, a:a + 3], WIN), ALU.mult)
                step(V.tensor_tensor(pos_oh[:].rearrange("p c t s -> p (c t) s"),
                                     c_("iota").rearrange("p (o s) -> p o s", o=1).to_broadcast((P, ct, P)),
                                     place_.rearrange("p (t o) -> p t o", o=1).to_broadcast((P, ct, P)), ALU.is_equal))
                for c in range(2):
                    for t in range(TT):
                        for v in range(2):
                            ins = V.tensor_tensor(vals[:, c, t, v], oh[:, c, t].rearrange("p (e o) -> p e o", o=1)
                                                  .to_broadcast((P, NE, WIN)),
                                                  wv[:, c, t, v:v + 1, :].to_broadcast((P, NE, WIN)), ALU.mult)
                    ins.then_inc(m["onehots"], 1)
                dve.wait_ge(m["idx_mm"], 1)
                V.tensor_scalar(slots_idx[:, :, 0:NE * WIN], ps[:, 3, 0:2 * NE * WIN]
                                .rearrange("p (v n) -> p v n", v=2), -1.0, BIG, ALU.mult, ALU.add).then_inc(m["idx_ready"], 1)
                dve.wait_ge(m["exp_out"], 2)
                step(V.tensor_reduce(sm(7), r4[:], AX.X, ALU.add))
                step(V.tensor_scalar(sm(8), sm(6), 1.0, None, ALU.add))
                step(V.tensor_tensor(sm(7), sm(7), sm(8), ALU.mult))
                step(V.reciprocal(wgt[:, 0, :], sm(7)))
                V.tensor_tensor(wgt[:, 1, :], wgt[:, 0, :], sm(6), ALU.mult).then_inc(m["weights"], 1)
                dve.wait_ge(m["weights"], 1)

            def experts(l):
                m = M[l]
                dve.wait_ge(m["idx_ready"], 1)
                n = dve.alloc_register(f"dve_pass{l}")
                dve.reg_mov(n, 0)
                half = dve.alloc_register(f"dve_half{l}")
                dve.reg_mov(half, 0)
                dve.wait_ge(m["turned"], 1)
                V.tensor_copy(xt[:, 4:8, :].rearrange("p k s -> p (k s)"), ps[:, 1, :]).then_inc(m["xt_b"], 1)
                with dve.Fori(0, NE) as e:
                    windows = dve.value_load(npass[0:1, bass.ds(e, 1)], min_val=1, max_val=WIN)
                    with dve.Fori(0, windows):
                        dve.reg_add(n, n, 1)
                        dve.reg_add(half, half, 1)
                        first = dve.snap(half, min_val=1, max_val=2 * WIN * NE)
                        dve.reg_add(half, half, 1)
                        second = dve.snap(half, min_val=1, max_val=2 * WIN * NE)
                        k_ = dve.snap(n, min_val=1, max_val=WIN * NE)
                        for j in range(2):
                            h = slice(j * F // 2, (j + 1) * F // 2)
                            dve.wait_ge(m["up_mm"], [first, second][j])
                            if j == 0:
                                dve.wait_ge(m["silu"], k_)
                            V.tensor_tensor(hid[:, h], sg[:, h], ps[:, UP_BANK[j], 0:F // 2], ALU.mult
                                            ).then_inc(m["hid"], 1)
                        dve.wait_ge(m["turned"], k_ + 1)
                        V.tensor_copy(xt[:, 4:8, :].rearrange("p k s -> p (k s)"), ps[:, 1, :]).then_inc(m["xt_b"], 1)
                        dve.wait_ge(m["y_mm_b"], k_)
                        dve.wait_ge(m["scattered"], 16 * k_ + 32)
                        V.tensor_copy(ysb[:, C512:D], ps[:, 6, :]).then_inc(m["y_b"], 1)
                    dve.sem_inc(m["used"], 1)

            def combine(l):
                m = M[l]
                for t in range(TT):
                    dve.wait_ge(yback[t], 16 * (l + 1))
                    dve.wait_ge(m["second"], t + 1)
                    a, b = yall[:, t, 0, :], yall[:, t, 1, :]
                    step(V.scalar_tensor_tensor(out=a, in0=a, scalar=wgt[:, 0, t:t + 1], in1=b,
                                                op0=ALU.mult, op1=ALU.add))
                    step(V.tensor_tensor(a, a, gate_bc[:, 1, GROUP_OF[t], :], ALU.mult))
                    V.tensor_tensor(x[:, t, :], x[:, t, :], a, ALU.add).then_inc(m["x_done"], 1)

            def first_row_out(U):
                dve.wait_ge(mod_mm, U + 1)
                V.tensor_copy(first_row[:, U, :], ps[0:2, U % 2, :]).then_inc(mod_evac, 1)

            for U in range(3):
                first_row_out(U)
            dve.wait_ge(s_x, 32)
            dve.wait_ge(s_pos, 16)
            V.tensor_tensor(x[:, 1:3, :], x[:, 1:3, :], yall[:, 0], ALU.add).then_inc(x_ready, 1)
            dve.wait_ge(x_ready, 1)
            first_row_out(3)
            dve.wait_ge(mod_in[0], 16 * 2)
            for c in range(2):
                dve.wait_ge(mod_turned, 2 * c + 2)
                V.tensor_tensor(colmod[:, 0, c], ps[:, 4 + c, 2 * KD * c:2 * KD * (c + 1)].rearrange("p (k g) -> p g k", g=2),
                                bcol[:, c:c + 1, :].to_broadcast((P, 2, KD)), ALU.add).then_inc(col_set, 1)
            dve.wait_ge(col_set, 2)
            normalise("a0")
            columns("a0", 0, 0)
            modulate("a0", 0, 0)
            for half in range(2):
                if half == 1:
                    dve.wait_ge(o_tp, 3)
                for U in range(4 + 8 * half, 12 + 8 * half):
                    gemv(U)
                    if 4 + 8 * half < U < 11 + 8 * half:
                        mod_evac_row(U - 1, 6 + (U - 1) % 2)
                dve.wait_ge(proj_evac, 18 * half + 12)
                for d in range(2):
                    V.tensor_tensor(qd[d], qT, G[d][1], ALU.mult).then_inc(lvl_upd[d], 1)
                scan_half(half)
            dve.wait_ge(mod_in[1], 16 * 8)
            residual(0)
            columns("m0", 0, 1)
            modulate("m0", 0, 1, True)
            route(0)
            experts(0)
            combine(0)
            normalise("a1")
            dve.wait_ge(mod_in[2], 16 * 8)
            columns("a1", 1, 0)
            modulate("a1", 1, 0)
            gemv(20)
            gemv(21)
            mod_evac_row(20, 4)
            gemv(22)
            mod_evac_row(21, 5)
            gemv(23)
            mod_evac_row(22, 6)
            mod_evac_row(23, 7)
            residual(1)
            dve.wait_ge(mod_in[3], 16 * 2)
            columns("m1", 1, 1)
            modulate("m1", 1, 1, True)
            route(1)
            experts(1)
            dve.wait_ge(mod_in[3], 16 * 4)
            combine(1)
            dve.wait_ge(M[1]["x_done"], TT)
            dve.wait_ge(fin_in, 16)
            for t in range(TT):
                dve.wait_ge(n_rs, 3 * NORM["fin"] + t + 1)
                V.scalar_tensor_tensor(out=xn[:, t, :], in0=x[:, t, :], scalar=stat[:, 3 + t:4 + t],
                                       in1=gate_bc[:, 0, 0, :], op0=ALU.mult, op1=ALU.mult).then_inc(fin_done, 1)

        @block.gpsimd
        def _(pool):
            G_ = nc.gpsimd

            def experts(l):
                m = M[l]
                pool.wait_ge(out_x[l], 6)
                G_.memset(xg, 0.0).then_inc(m["zeroed"], 1)
                G_.memset(ysb, 0.0).then_inc(m["zeroed"], 1)
                pool.wait_ge(m["zeroed"], 2)
                def send_rows():
                    G_.indirect_dma_start(out=scratch["y"][l],
                                          out_offset=bass.IndirectOffsetOnAxis(ap=si[:, 0:1], axis=0),
                                          in_=ysb, in_offset=None, bounds_check=2 * T - 1, oob_is_err=False
                                          ).then_inc(m["scattered"], 16)

                G_.memset(slots_idx[:, 1, NE * WIN:NE * WIN + 1], int(BIG)).then_inc(m["zeroed"], 1)
                pool.sem_inc(m["y_a"], 2)
                pool.sem_inc(m["y_b"], 2)
                pool.wait_ge(m["zeroed"], 3)
                G_.tensor_copy(si[:], slots_idx[:, 1, NE * WIN:NE * WIN + 1]).then_inc(m["zeroed"], 1)
                pool.wait_ge(m["zeroed"], 4)
                send_rows()
                pool.wait_ge(m["idx_ready"], 1)
                pool.wait_ge(m["hrow_out"], 16 * TT)
                n = pool.alloc_register(f"pool_pass{l}")
                col1 = pool.alloc_register(f"pool_col1_{l}")
                col2 = pool.alloc_register(f"pool_col2_{l}")
                pool.reg_mov(n, 0)
                pool.reg_mov(col1, NE * WIN)
                pool.reg_mov(col2, NE * WIN)

                def gather(k_, col):
                    G_.tensor_copy(gi[:], slots_idx[:, 0, col]).then_inc(m["gi_set"], 1)
                    pool.wait_ge(m["idx_ready"], 1)
                    pool.wait_ge(m["gi_set"], k_)
                    G_.indirect_dma_start(out=xg, out_offset=None, in_=scratch["hrow"][l],
                                          in_offset=bass.IndirectOffsetOnAxis(ap=gi[:, 0:1], axis=0),
                                          bounds_check=T - 1, oob_is_err=False).then_inc(m["gathered"], 16)

                def scatter(k_, col):
                    pool.wait_ge(m["scattered"], 16 * k_)
                    G_.tensor_copy(si[:], slots_idx[:, 1, bass.ds(pool.snap(col, min_val=0, max_val=NE * WIN), 1)]
                                   ).then_inc(m["si_set"], 1)
                    pool.wait_ge(m["idx_ready"], 1)
                    pool.wait_ge(m["y_a"], k_)
                    pool.wait_ge(m["y_b"], k_)
                    pool.wait_ge(m["si_set"], k_)
                    send_rows()

                with pool.Fori(0, NE) as e:
                    windows = pool.value_load(npass[0:1, bass.ds(e, 1)], min_val=1, max_val=WIN)
                    with pool.Fori(0, windows) as w:
                        pool.reg_add(n, n, 1)
                        k_ = pool.snap(n, min_val=1, max_val=WIN * NE)
                        gather(k_, bass.ds(e * WIN + w, 1))
                        scatter(k_, col2)
                        pool.reg_mov(col2, col1)
                        pool.reg_mov(col1, e * WIN + w)
                        pool.wait_ge(m["turned"], k_)
                        pool.wait_ge(m["gathered"], 16 * k_)
                pool.reg_add(n, n, 1)
                k1 = pool.snap(n, min_val=NE + 1, max_val=WIN * NE + 1)
                gather(k1, slice(0, 1))
                scatter(k1, col2)
                pool.reg_add(n, n, 1)
                k2 = pool.snap(n, min_val=NE + 2, max_val=WIN * NE + 2)
                scatter(k2, col1)
                pool.wait_ge(m["used"], NE)
                pool.wait_ge(m["scattered"], 16 * k2 + 16)
                pool.wait_ge(m["xt_a"], k1)
                pool.sem_inc(m["all_out"], 1)

            def rms(name):
                for t in range(TT):
                    n = 3 * NORM[name] + t + 1
                    pool.wait_ge(n_sq, n)
                    G_.tensor_scalar(stat[:, t:t + 1], stat[:, t:t + 1], 1.0 / D, EPS, ALU.mult, ALU.add
                                     ).then_inc(n_ms, 1)
                    pool.wait_ge(n_ms, n)
                    G_.tensor_tensor(stat[:, 3 + t:4 + t], stat[:, t:t + 1], c_("minus_half")[:, 0:1], ALU.pow
                                     ).then_inc(n_rs, 1)

            def mod_rows(units):
                for U in units:
                    l, u = mod_unit(U)
                    cols = slice(u * C512, (u + 1) * C512)
                    if U == 12:
                        pool.wait_ge(o_tp, 3)
                    if U == 20:
                        pool.wait_ge(M[0]["x_done"], TT)
                    if U > 4:
                        pool.wait_ge(mod_evac, U)
                    pool.dma_start(mod_b[U], io["b_mod"][l:l + 1, cols].to_broadcast((2, C512))
                                   ).then_inc(mod_bias, 16)
                    pool.wait_ge(mod_evac, U + 1)
                    pool.dma_start(scratch["mod"][l][:, cols], mod_row[U]).then_inc(mod_row_out, 16)
                pool.wait_ge(mod_row_out, 16 * (units[-1] - 3))

            def mod_columns(l, c, signal):
                q = [0, 1, 3, 4][c]
                for g in range(2):
                    v = scratch["mod"][l][g, q * D:(q + 1) * D]
                    v = v.rearrange("(k p) -> p k", p=P) if l == 1 and c < 2 else v.rearrange("(p k) -> p k", k=KD)
                    with nc.allow_non_contiguous_dma(reason="a modulation vector, 4 KB"):
                        pool.dma_start(colmod[:, l, c, g, :], v).then_inc(signal, 16)

            def mod_gates(l, w, signal):
                for g in range(2):
                    q = 2 + 3 * w
                    pool.dma_start(gate_bc[:, w, g, :], scratch["mod"][l][g:g + 1, q * D:(q + 1) * D]
                                   .to_broadcast((P, D))).then_inc(signal, 16)

            pool.wait_ge(s_const, 16)
            rms("a0")
            for half in range(2):
                mod_rows(range(4 + 8 * half, 12 + 8 * half))
                if half == 0:
                    mod_columns(0, 2, mod_in[1])
                    mod_columns(0, 3, mod_in[1])
                    mod_gates(0, 0, mod_in[1])
                    mod_gates(0, 1, mod_in[1])
                for t in range(TT):
                    n = 3 * half + t + 1
                    pool.wait_ge(o_sq, n)
                    G_.tensor_scalar(rsq[:, t, :], ssq[:, t, :], 1.0 / P, EPS, ALU.mult, ALU.add).then_inc(o_ms, 1)
                    pool.wait_ge(o_ms, n)
                    G_.tensor_tensor(rsq[:, t, :], rsq[:, t, :], c_("minus_half"), ALU.pow).then_inc(o_rs, 1)
                for d in range(2):
                    pool.wait_ge(s_ready, 4 * half + d + 1)
                    pool.dma_start(io["o_state"][0, 0, d, HH * half:HH * (half + 1)].rearrange("h k v -> k h v"),
                                   s_out[:, d]).then_inc(st_written, 16)
            rms("m0")
            mod_columns(1, 0, mod_in[2])
            mod_columns(1, 1, mod_in[2])
            mod_columns(1, 2, mod_in[2])
            pool.wait_ge(out_x[0], 6)
            mod_gates(1, 0, mod_in[2])
            experts(0)
            rms("a1")
            mod_rows(range(20, 22))
            mod_columns(1, 3, mod_in[3])
            mod_rows(range(22, 24))
            pool.wait_ge(mod_in[3], 16 * 2)
            rms("m1")
            mod_gates(1, 1, mod_in[3])
            experts(1)
            rms("fin")


def shape_constants():
    f = np.float32
    const = np.zeros((P, CONST_W), f)

    def put(name, a):
        i, j = CONST_AT[name]
        const[:a.shape[0], i:j] = a

    r = np.arange(P)
    put("ident", np.eye(P))
    put("upper", (r[:, None] < r[None, :]))
    put("ones", np.ones((P, P)))
    put("iota", np.tile(r, (P, 1)))
    put("rev_group", np.tile(4 - np.arange(4), (P, 1)))
    put("rev_expert", np.tile(16 - np.arange(16), (P, 1)))
    put("window", np.tile(np.arange(3), (P, 1)))
    tok = r[:, None] + P * np.arange(TT)[None, :]
    put("value", np.concatenate([BIG - tok, BIG - 2 * tok, BIG - tok, BIG - 2 * tok - 1], 1))
    put("minus_half", np.full((P, 4), -0.5))
    put("pick", np.tile([1, 0, 0, 1], (P, 1)))
    s, t = np.arange(P)[:, None] % SMALL, np.arange(SMALL)[None, :]
    masks = np.zeros((P, NMASK, SMALL), np.int32)
    for i, h in enumerate([1, 2, 4, 8, 16]):
        same = s // (2 * h) == t // (2 * h)
        masks[:, 2 * i] = same & (s // h % 2 == 0) & (t // h % 2 == 1)
        masks[:, 2 * i + 1] = same & (s // h % 2 == 1) & (t // h % 2 == 0)
    masks[:, 10] = s == t
    n, width, quarter = 2 * P, 64, D // 4
    tt = np.arange(n)
    omega = (1.0 / (f(10000.0) ** (np.arange(quarter, dtype=f) / f(quarter)))).astype(f)
    ar = (tt // width).astype(f)[:, None] * omega[None]
    ac = (tt % width).astype(f)[:, None] * omega[None]
    pos = np.concatenate([np.sin(ar), np.cos(ar), np.sin(ac), np.cos(ac)], -1).astype(f)
    pos = np.ascontiguousarray(pos.reshape(2, P, D).transpose(1, 0, 2))

    def dft(m):
        a = 2 * np.pi * (np.outer(np.arange(m), np.arange(m)) % m) / m
        return np.cos(a) / np.sqrt(m), np.sin(a) / np.sqrt(m)

    cc, sc = dft(256)
    dft_c = np.concatenate([cc, sc], 1).reshape(2, P, 512).transpose(1, 0, 2)
    c1, s1 = dft(P)
    dft_ctx = np.stack([c1, -s1], 1)
    dft_lat = np.stack([cc, -sc], 1).reshape(2, P, 2, 256).transpose(1, 0, 2, 3)
    out = dict(const=const, masks=masks, pos=pos, dft_c=dft_c, dft_ctx=dft_ctx, dft_lat=dft_lat)
    return {k: np.ascontiguousarray(v, v.dtype if v.dtype == np.int32 else f) for k, v in out.items()}


_INS = ["x_prompt", "x_sample", "state_hgrn", "c", "c_ctx", "w_mod", "b_mod", "norm1_g", "norm2_g", "hgrn_w_in",
        "hgrn_norm_g", "hgrn_w_out", "fourier_w_out", "router_group_w", "router_group_b", "router_expert_w",
        "router_expert_b", "moe_w_gate", "moe_w_up", "moe_w_down", "final_norm_g"]


def kernel(**inputs):
    import numpy as _np
    import concourse.bacc as _bacc
    from concourse import mybir as _mybir
    from concourse.bass_utils import run_bass_kernel_spmd as _run

    nc = _bacc.Bacc("TRN2", target_bir_lowering=False, num_devices=1)
    arrays = {n: _np.ascontiguousarray(inputs[n]) for n in _INS}
    arrays.update(shape_constants())
    io = {n: nc.dram_tensor(f"in_{n}", a.shape, _mybir.dt.from_np(a.dtype), kind="ExternalInput").ap()
          for n, a in arrays.items()}
    f32 = _mybir.dt.float32
    for n, shape in [("o_prompt", (1, 128, 1024)), ("o_sample", (1, 256, 1024)), ("o_state", (1, 1, 2, 8, 128, 128))]:
        io[n] = nc.dram_tensor(n, shape, f32, kind="ExternalOutput").ap()
    scratch = {"hrow": [nc.dram_tensor(f"hrow{l}", (T, D), f32, kind="Internal").ap() for l in range(2)],
               "mod": [nc.dram_tensor(f"modrow{l}", (2, 6 * D), f32, kind="Internal").ap() for l in range(2)],
               "y": [nc.dram_tensor(f"yrows{l}", (2 * T, D), f32, kind="Internal").ap() for l in range(2)]}
    program(nc, io, scratch)
    r = _run(nc, [{f"in_{n}": a for n, a in arrays.items()}], core_ids=[0]).results[0]
    return r["o_prompt"], r["o_sample"], r["o_state"]
```
